# Optimizing a Trainium2 kernel written in Bass

```python
import math
import jax
import jax.numpy as jnp
from jax import lax
import numpy as np
import jax, jax.numpy as jnp

D_MODEL = 1024
BATCH = 1
SEQ = 256
DEPTH = 1

CTX_LEN = 256
GRID_W = 64
H_M = 8
D_HM = 64
W_M = H_M * D_HM
H_R = 8
D_HR = 64
W_R = H_R * D_HR
MIX_W = W_M + W_R
W_LORA = 64
A_LORA = 64
G_LORA = 128
CONV_K = 3
CONV_CH = 2 * W_M + 3 * W_R
SECTION_WIDTHS = (W_M, W_M, W_R, W_R, W_R, W_M, W_M, 4 * H_M, W_LORA, W_LORA, A_LORA, G_LORA)
IN_COLS = sum(SECTION_WIDTHS)
SPLIT_POINTS = tuple(int(v) for v in np.cumsum(SECTION_WIDTHS)[:-1])
CHUNK = 64
N_GROUPS = 4
E_PER_GROUP = 8
N_EXPERTS = N_GROUPS * E_PER_GROUP
TOP_K_IN_GROUP = 2
D_EXPERT = 512
MOE_BLOCK = 256
ALPHA = (2.0 * DEPTH) ** 0.25
BETA = (8.0 * DEPTH) ** -0.25
DECAY_SCALE = math.exp(-0.5)
LN_EPS = 1e-6
GN_EPS = 64e-5


def _layernorm(z, gain=None, bias=None):
    zf = z.astype(jnp.float32)
    mu = jnp.mean(zf, -1, keepdims=True)
    var = jnp.mean(jnp.square(zf - mu), -1, keepdims=True)
    y = (zf - mu) * lax.rsqrt(var + LN_EPS)
    if gain is not None:
        y = y * gain + bias
    return y.astype(z.dtype)

def _headnorm(z, eps):
    zf = z.astype(jnp.float32)
    mu = jnp.mean(zf, -1, keepdims=True)
    var = jnp.mean(jnp.square(zf - mu), -1, keepdims=True)
    return (zf - mu) * lax.rsqrt(var + eps)

def _modulate(z, shift, scale):
    return _layernorm(z) * (1 + scale) + shift

def _rev_segments(u):
    return jnp.concatenate([jnp.flip(u[:, :CTX_LEN], 1), jnp.flip(u[:, CTX_LEN:], 1)], axis=1)

def _dir_stack(u_fwd, u_bwd):
    return jnp.concatenate([u_fwd, _rev_segments(u_bwd)], axis=0)

def _dir_merge(y):
    b = y.shape[0] // 2
    return y[:b] + _rev_segments(y[b:])

def _conv_grid(u, w, rows):
    b, l, ch = u.shape
    img = u.reshape(b, rows, l // rows, ch)
    out = lax.conv_general_dilated(img, w[:, :, None, :].astype(u.dtype), (1, 1), 'SAME',
                                   dimension_numbers=('NHWC', 'HWIO', 'NHWC'), feature_group_count=ch)
    return out.reshape(b, l, ch)

def _conv_seq(u, w_row):
    ch = u.shape[-1]
    return lax.conv_general_dilated(u, w_row[:, None, :].astype(u.dtype), (1,), 'SAME',
                                    dimension_numbers=('NWC', 'WIO', 'NWC'), feature_group_count=ch)

def _mlstm_chunkwise(q, k, v, log_i, log_f):
    z, t, h, dh = q.shape
    nc = t // CHUNK
    def chunks(a):
        a = a.astype(jnp.float32).reshape((z, nc, CHUNK, h) + a.shape[3:])
        return jnp.swapaxes(jnp.swapaxes(a, 0, 1), 2, 3)
    qc, kc, vc, lic, lfc = chunks(q), chunks(k), chunks(v), chunks(log_i), chunks(log_f)
    tri = jnp.tril(jnp.ones((CHUNK, CHUNK), bool))

    def step(carry, inp):
        c_mat, n_vec, m = carry
        qb, kb, vb, li, lf = inp
        b = jnp.cumsum(lf, -1)
        dmat = jnp.where(tri, b[..., :, None] - b[..., None, :] + li[..., None, :], -jnp.inf)
        m_inter = b + m[..., None]
        m_t = jnp.maximum(m_inter, jnp.max(dmat, -1))
        s = jnp.einsum('zhtd,zhsd->zhts', qb, kb) * jnp.exp(dmat - m_t[..., None])
        inter = jnp.exp(m_inter - m_t)
        num = inter[..., None] * jnp.einsum('zhtd,zhde->zhte', qb, c_mat) + jnp.einsum('zhts,zhse->zhte', s, vb)
        den = inter * jnp.einsum('zhtd,zhd->zht', qb, n_vec) + jnp.sum(s, -1)
        h_out = num / jnp.maximum(jnp.abs(den), jnp.exp(-m_t))[..., None]
        b_last = b[..., -1]
        g = b_last[..., None] - b + li
        m_new = jnp.maximum(b_last + m, jnp.max(g, -1))
        wts = jnp.exp(g - m_new[..., None])
        decay = jnp.exp(b_last + m - m_new)
        c_mat = decay[..., None, None] * c_mat + jnp.einsum('zhs,zhsd,zhse->zhde', wts, kb, vb)
        n_vec = decay[..., None] * n_vec + jnp.einsum('zhs,zhsd->zhd', wts, kb)
        return (c_mat, n_vec, m_new), h_out

    init = (jnp.zeros((z, h, dh, dh), jnp.float32), jnp.zeros((z, h, dh), jnp.float32), jnp.zeros((z, h), jnp.float32))
    _, hs = lax.scan(step, init, (qc, kc, vc, lic, lfc))
    return jnp.swapaxes(jnp.swapaxes(hs, 2, 3), 0, 1).reshape(z, t, h, dh)

def _mlstm_group(mq, mk, mv, mo, gates, b_i, b_f, norm_w):
    b, t, _ = mq.shape
    q = jax.nn.silu(mq).reshape(b, t, H_M, D_HM)
    k = jax.nn.silu(mk).reshape(b, t, H_M, D_HM) * (D_HM ** -0.5)
    v = mv.reshape(b, t, H_M, D_HM)
    gt = gates.astype(jnp.float32).reshape(b, t, 4, H_M)
    li_f = gt[:, :, 0] + b_i[0]
    lf_f = jax.nn.log_sigmoid(gt[:, :, 1] + b_f[0])
    li_b = gt[:, :, 2] + b_i[1]
    lf_b = jax.nn.log_sigmoid(gt[:, :, 3] + b_f[1])
    h = _mlstm_chunkwise(_dir_stack(q, q), _dir_stack(k, k), _dir_stack(v, v),
                         _dir_stack(li_f, li_b), _dir_stack(lf_f, lf_b))
    h = _headnorm(_dir_merge(h), LN_EPS) * norm_w.reshape(H_M, D_HM)
    return jax.nn.sigmoid(mo) * h.reshape(b, t, W_M)

def _rwkv7_scan(r, w, k, v, kh, a):
    z, t, h, n = r.shape
    seq = tuple(jnp.moveaxis(s.astype(jnp.float32), 1, 0) for s in (r, w, k, v, kh, a))

    def step(state, inp):
        r_t, w_t, k_t, v_t, kh_t, a_t = inp
        removed = jnp.einsum('zhvk,zhk->zhv', state, kh_t)
        state = (state * w_t[:, :, None, :] - removed[..., None] * (kh_t * a_t)[:, :, None, :]
                 + v_t[..., None] * k_t[:, :, None, :])
        return state, jnp.einsum('zhvk,zhk->zhv', state, r_t)

    _, y = lax.scan(step, jnp.zeros((z, h, n, n), jnp.float32), seq)
    return jnp.moveaxis(y, 0, 1)

def _rwkv7_group(rr, rk, rv, lw_f, lw_b, la, lg, w0, w_b_mat, a0, a_b_mat, g_b_mat, kk, ka, bonus_w, gn_w, gn_b):
    b, t, _ = rr.shape
    shp = (b, t, H_R, D_HR)
    w_fwd = jnp.exp(-DECAY_SCALE * jax.nn.sigmoid((w0[0] + jnp.tanh(lw_f) @ w_b_mat[0]).astype(jnp.float32)))
    w_bwd = jnp.exp(-DECAY_SCALE * jax.nn.sigmoid((w0[1] + jnp.tanh(lw_b) @ w_b_mat[1]).astype(jnp.float32)))
    a = jax.nn.sigmoid(a0 + la @ a_b_mat)
    g = jax.nn.sigmoid(lg) @ g_b_mat
    kap = (rk * kk).reshape(shp).astype(jnp.float32)
    kh = kap / jnp.maximum(jnp.sqrt(jnp.sum(jnp.square(kap), -1, keepdims=True)), 1e-12)
    kmod = (rk * (1 + (a - 1) * ka)).reshape(shp)
    r = rr.reshape(shp)
    v = rv.reshape(shp)
    a_h = a.reshape(shp)
    y = _rwkv7_scan(_dir_stack(r, r), _dir_stack(w_fwd.reshape(shp), w_bwd.reshape(shp)), _dir_stack(kmod, kmod),
                    _dir_stack(v, v), _dir_stack(kh, kh), _dir_stack(a_h, a_h))
    y = _headnorm(_dir_merge(y), GN_EPS) * gn_w.reshape(H_R, D_HR) + gn_b.reshape(H_R, D_HR)
    bonus = jnp.sum(r * kmod * bonus_w, -1, keepdims=True) * v
    return (y + bonus).reshape(b, t, W_R) * g

def _mixer(h_ctx, h_lat, rows, w_in, conv_w, m_bias_i, m_bias_f, m_norm_w, r_w0, r_wB, r_a0, r_aB, r_gB,
           r_kk, r_ka, r_bonus, r_norm_w, r_norm_b):
    p_ctx = h_ctx @ w_in
    p_lat = h_lat @ w_in
    p_ctx = jnp.concatenate([_conv_seq(p_ctx[..., :CONV_CH], conv_w[CONV_K // 2]), p_ctx[..., CONV_CH:]], -1)
    p_lat = jnp.concatenate([_conv_grid(p_lat[..., :CONV_CH], conv_w, rows), p_lat[..., CONV_CH:]], -1)
    u = jnp.concatenate([p_ctx, p_lat], axis=1)
    mq, mk, rr, rk, rv, mv, mo, gates, lw_f, lw_b, la, lg = jnp.split(u, SPLIT_POINTS, axis=-1)
    out_m = _mlstm_group(mq, mk, mv, mo, gates, m_bias_i, m_bias_f, m_norm_w)
    out_r = _rwkv7_group(rr, rk, rv, lw_f, lw_b, la, lg, r_w0, r_wB, r_a0, r_aB, r_gB, r_kk, r_ka, r_bonus,
                         r_norm_w, r_norm_b)
    return jnp.concatenate([out_m.astype(out_r.dtype), out_r], -1)

def _hier_moe(h, rt_g, rt_g_b, rt_e, rt_e_b, ex_gate, ex_up, ex_down):
    b, t, d = h.shape
    tok = h.reshape(b * t, d)
    n = tok.shape[0]
    lg = (tok @ rt_g + rt_g_b).astype(jnp.float32)
    p_grp = jax.nn.softmax(lg, axis=-1)
    grp = jnp.argmax(lg, axis=-1).astype(jnp.int32)
    p_top = jnp.take_along_axis(p_grp, grp[:, None], axis=-1)
    le = (tok @ rt_e + rt_e_b).astype(jnp.float32).reshape(n, N_GROUPS, E_PER_GROUP)
    le_grp = jnp.take_along_axis(le, jnp.broadcast_to(grp[:, None, None], (n, 1, E_PER_GROUP)), axis=1)[:, 0]
    top_val, top_idx = lax.top_k(le_grp, TOP_K_IN_GROUP)
    wts = jax.nn.softmax(top_val, axis=-1) * p_top
    e_flat = (grp[:, None] * E_PER_GROUP + top_idx.astype(jnp.int32)).reshape(-1)
    w_flat = wts.reshape(-1)
    t_flat = jnp.repeat(jnp.arange(n, dtype=jnp.int32), TOP_K_IN_GROUP)
    order = jnp.argsort(e_flat)
    e_s, t_s, w_s = e_flat[order], t_flat[order], w_flat[order]
    counts = jnp.zeros((N_EXPERTS,), jnp.int32).at[e_flat].add(1)
    starts = jnp.cumsum(counts) - counts
    padded = (counts + MOE_BLOCK - 1) // MOE_BLOCK * MOE_BLOCK
    pad_ends = jnp.cumsum(padded)
    pad_starts = pad_ends - padded
    dest = pad_starts[e_s] + jnp.arange(e_s.shape[0], dtype=jnp.int32) - starts[e_s]
    n_pairs = n * TOP_K_IN_GROUP
    buf = (-(-n_pairs // MOE_BLOCK) + N_EXPERTS) * MOE_BLOCK
    tok_buf = jnp.full((buf,), n, jnp.int32).at[dest].set(t_s)
    w_buf = jnp.zeros((buf,), w_s.dtype).at[dest].set(w_s)
    n_blk = buf // MOE_BLOCK
    blk_exp = jnp.minimum(jnp.searchsorted(pad_ends, jnp.arange(n_blk, dtype=jnp.int32) * MOE_BLOCK, side='right'),
                          N_EXPERTS - 1)
    tok_pad = jnp.concatenate([tok, jnp.zeros((1, d), tok.dtype)], 0)

    def expert_block(args):
        idx, w, e = args
        xb = tok_pad[idx]
        hb = jax.nn.silu(xb @ ex_gate[e]) * (xb @ ex_up[e])
        return (hb @ ex_down[e]) * w[:, None]

    y = lax.map(expert_block, (tok_buf.reshape(n_blk, MOE_BLOCK), w_buf.reshape(n_blk, MOE_BLOCK), blk_exp))
    out = jnp.zeros((n + 1, d), y.dtype).at[tok_buf].add(y.reshape(buf, d))
    return out[:n].reshape(b, t, d).astype(h.dtype)

def first_inputs(seed: int = 0) -> dict:
    key = jax.random.key(seed)
    ks = jax.random.split(key, 40)
    def nrm(k, shape, s):
        return jax.random.normal(k, shape, jnp.float32) * s
    L = DEPTH
    return {
        'x': nrm(ks[0], (BATCH, SEQ, D_MODEL), 1.0),
        'c': nrm(ks[1], (BATCH, D_MODEL), 1.0),
        'ctx': nrm(ks[2], (BATCH, CTX_LEN, D_MODEL), 1.0),
        'c_ctx': nrm(ks[3], (D_MODEL,), 1.0),
        'w_ada': nrm(ks[4], (L, D_MODEL, 6 * D_MODEL), D_MODEL ** -0.5),
        'b_ada': nrm(ks[5], (L, 6 * D_MODEL), 0.02),
        'w_in': nrm(ks[6], (L, D_MODEL, IN_COLS), D_MODEL ** -0.5),
        'conv_w': nrm(ks[7], (L, CONV_K, CONV_K, CONV_CH), 0.3),
        'm_bias_i': nrm(ks[8], (L, 2, H_M), 0.5),
        'm_bias_f': 3.0 + nrm(ks[9], (L, 2, H_M), 0.5),
        'm_norm_w': 1.0 + nrm(ks[10], (L, W_M), 0.05),
        'r_w0': nrm(ks[11], (L, 2, W_R), 0.5),
        'r_wB': nrm(ks[12], (L, 2, W_LORA, W_R), W_LORA ** -0.5),
        'r_a0': nrm(ks[13], (L, W_R), 0.5),
        'r_aB': nrm(ks[14], (L, A_LORA, W_R), A_LORA ** -0.5),
        'r_gB': nrm(ks[15], (L, G_LORA, W_R), G_LORA ** -0.5),
        'r_kk': 0.85 + nrm(ks[16], (L, W_R), 0.05),
        'r_ka': 1.0 + nrm(ks[17], (L, W_R), 0.05),
        'r_bonus': nrm(ks[18], (L, H_R, D_HR), 0.1),
        'r_norm_w': 1.0 + nrm(ks[19], (L, W_R), 0.05),
        'r_norm_b': nrm(ks[20], (L, W_R), 0.02),
        'w_out': nrm(ks[21], (L, MIX_W, D_MODEL), BETA * MIX_W ** -0.5),
        'ln1_g': 1.0 + nrm(ks[22], (L, D_MODEL), 0.05),
        'ln1_b': nrm(ks[23], (L, D_MODEL), 0.02),
        'ln2_g': 1.0 + nrm(ks[24], (L, D_MODEL), 0.05),
        'ln2_b': nrm(ks[25], (L, D_MODEL), 0.02),
        'rt_g': nrm(ks[26], (L, D_MODEL, N_GROUPS), D_MODEL ** -0.5),
        'rt_g_b': nrm(ks[27], (L, N_GROUPS), 0.01),
        'rt_e': nrm(ks[28], (L, D_MODEL, N_EXPERTS), D_MODEL ** -0.5),
        'rt_e_b': nrm(ks[29], (L, N_EXPERTS), 0.01),
        'ex_gate': nrm(ks[30], (L, N_EXPERTS, D_MODEL, D_EXPERT), D_MODEL ** -0.5),
        'ex_up': nrm(ks[31], (L, N_EXPERTS, D_MODEL, D_EXPERT), D_MODEL ** -0.5),
        'ex_down': nrm(ks[32], (L, N_EXPERTS, D_EXPERT, D_MODEL), BETA * D_EXPERT ** -0.5),
    }

def first_block(x, c, ctx, c_ctx, w_ada, b_ada, w_in, conv_w, m_bias_i, m_bias_f, m_norm_w, r_w0, r_wB, r_a0, r_aB,
              r_gB, r_kk, r_ka, r_bonus, r_norm_w, r_norm_b, w_out, ln1_g, ln1_b, ln2_g, ln2_b, rt_g, rt_g_b, rt_e,
              rt_e_b, ex_gate, ex_up, ex_down):
    rows = x.shape[1] // GRID_W
    for l in range(DEPTH):
        mod = jax.nn.silu(c) @ w_ada[l] + b_ada[l]
        mod_c = jax.nn.silu(c_ctx) @ w_ada[l] + b_ada[l]
        sh1, sc1, g1, sh2, sc2, g2 = jnp.split(mod[:, None, :], 6, axis=-1)
        sh1c, sc1c, g1c, sh2c, sc2c, g2c = jnp.split(mod_c, 6)
        mixed = _mixer(_modulate(ctx, sh1c, sc1c), _modulate(x, sh1, sc1), rows, w_in[l], conv_w[l], m_bias_i[l],
                       m_bias_f[l], m_norm_w[l], r_w0[l], r_wB[l], r_a0[l], r_aB[l], r_gB[l], r_kk[l], r_ka[l],
                       r_bonus[l], r_norm_w[l], r_norm_b[l])
        x = _layernorm(ALPHA * x + g1 * (mixed[:, CTX_LEN:] @ w_out[l]), ln1_g[l], ln1_b[l])
        ffn = _hier_moe(_modulate(x, sh2, sc2), rt_g[l], rt_g_b[l], rt_e[l], rt_e_b[l], ex_gate[l], ex_up[l], ex_down[l])
        x = _layernorm(ALPHA * x + g2 * ffn, ln2_g[l], ln2_b[l])
        if l + 1 < DEPTH:
            ctx = _layernorm(ALPHA * ctx + g1c * (mixed[:, :CTX_LEN] @ w_out[l]), ln1_g[l], ln1_b[l])
            ffn_c = _hier_moe(_modulate(ctx, sh2c, sc2c), rt_g[l], rt_g_b[l], rt_e[l], rt_e_b[l], ex_gate[l],
                              ex_up[l], ex_down[l])
            ctx = _layernorm(ALPHA * ctx + g2c * ffn_c, ln2_g[l], ln2_b[l])
    return x


DEPTH_2 = 2

N_MIXERS = 2
N_LAYERS_A = (DEPTH_2 + 1) // 2
N_LAYERS_B = DEPTH_2 // 2
EPS = 1e-6
N_MOD = 6

MLA_HEADS = 16
Q_LORA = 512
KV_LORA = 256
QK_NOPE = 64
QK_ROPE = 32
V_HEAD = 64
ROPE_THETA = 10000.0
Q_BLOCK = 128
MASK_VALUE = -1e30

GDN_HEADS = 8
GDN_DK = 128
GDN_DV = 128
CONV_K_2 = 4

D_FF = 2816
N_EXPERTS_2 = 8
TOP_K = 2
D_FF_EXPERT = 1408

MLA_IN = Q_LORA + KV_LORA + QK_ROPE
GDN_QKV = 2 * GDN_HEADS * GDN_DK + GDN_HEADS * GDN_DV
GDN_IN = GDN_QKV + GDN_HEADS * GDN_DV + 2 * GDN_HEADS


def rms_norm(x, g):
    xf = x.astype(jnp.float32)
    y = xf * lax.rsqrt(jnp.mean(xf * xf, axis=-1, keepdims=True) + EPS)
    return (y * g.astype(jnp.float32)).astype(x.dtype)

def l2_norm(x):
    xf = x.astype(jnp.float32)
    return xf * lax.rsqrt(jnp.sum(xf * xf, axis=-1, keepdims=True) + EPS)

def apply_rope(x, pos):
    half = QK_ROPE // 2
    inv_freq = ROPE_THETA ** (-jnp.arange(half, dtype=jnp.float32) / half)
    ang = pos.astype(jnp.float32)[:, :, None, None] * inv_freq
    cos, sin = jnp.cos(ang), jnp.sin(ang)
    xf = x.astype(jnp.float32)
    x1, x2 = xf[..., :half], xf[..., half:]
    out = jnp.concatenate([x1 * cos - x2 * sin, x2 * cos + x1 * sin], axis=-1)
    return out.astype(x.dtype)

def mla_mixer(h, pos, w_in, q_norm, w_qb, kv_norm, w_kvb, w_out):
    B, S, _ = h.shape
    H = MLA_HEADS
    proj = h @ w_in
    q_lat, kv_lat, k_rope = jnp.split(proj, [Q_LORA, Q_LORA + KV_LORA], axis=-1)
    q = (rms_norm(q_lat, q_norm) @ w_qb).reshape(B, S, H, QK_NOPE + QK_ROPE)
    q_nope = q[..., :QK_NOPE]
    q_rope = apply_rope(q[..., QK_NOPE:], pos)
    kv = (rms_norm(kv_lat, kv_norm) @ w_kvb).reshape(B, S, H, QK_NOPE + V_HEAD)
    k_nope, v = kv[..., :QK_NOPE], kv[..., QK_NOPE:]
    k_rope = apply_rope(k_rope[:, :, None, :], pos)[:, :, 0, :]
    scale = (QK_NOPE + QK_ROPE) ** -0.5
    n_blk = S // Q_BLOCK
    qn_b = q_nope.reshape(B, n_blk, Q_BLOCK, H, QK_NOPE).transpose(1, 0, 2, 3, 4)
    qr_b = q_rope.reshape(B, n_blk, Q_BLOCK, H, QK_ROPE).transpose(1, 0, 2, 3, 4)
    key_idx = jnp.arange(S)

    def attend(args):
        blk, qn, qr = args
        s = (jnp.einsum('bqhd,bkhd->bhqk', qn, k_nope)
             + jnp.einsum('bqhr,bkr->bhqk', qr, k_rope)).astype(jnp.float32) * scale
        q_idx = blk * Q_BLOCK + jnp.arange(Q_BLOCK)
        causal = key_idx[None, :] <= q_idx[:, None]
        s = jnp.where(causal, s, MASK_VALUE)
        p = jax.nn.softmax(s, axis=-1).astype(v.dtype)
        return jnp.einsum('bhqk,bkhd->bqhd', p, v)

    o = lax.map(attend, (jnp.arange(n_blk), qn_b, qr_b))
    o = o.transpose(1, 0, 2, 3, 4).reshape(B, S, H * V_HEAD)
    return o @ w_out

def causal_conv(x, w):
    C = x.shape[-1]
    return lax.conv_general_dilated(
        x, w[:, None, :].astype(x.dtype), window_strides=(1,),
        padding=[(CONV_K_2 - 1, 0)], dimension_numbers=('NWC', 'WIO', 'NWC'),
        feature_group_count=C)

def chunk_gated_delta(q, k, v, g, beta):
    B, S, H, DK = q.shape
    DV = v.shape[-1]
    N = S // CHUNK

    def to_chunks(t):
        return t.astype(jnp.float32).reshape(B, N, CHUNK, H, -1).transpose(0, 3, 1, 2, 4)

    q, k, v = to_chunks(q), to_chunks(k), to_chunks(v)
    beta = beta.astype(jnp.float32).reshape(B, N, CHUNK, H).transpose(0, 3, 1, 2)
    g = g.astype(jnp.float32).reshape(B, N, CHUNK, H).transpose(0, 3, 1, 2)
    gc = jnp.cumsum(g, axis=-1)
    causal = jnp.tril(jnp.ones((CHUNK, CHUNK), dtype=bool))
    strict = jnp.tril(jnp.ones((CHUNK, CHUNK), dtype=bool), -1)
    diff = gc[..., :, None] - gc[..., None, :]
    decay = jnp.where(causal, jnp.exp(jnp.where(causal, diff, 0.0)), 0.0)
    k_beta = k * beta[..., None]
    a_mat = jnp.where(strict, jnp.einsum('bhnid,bhnjd->bhnij', k_beta, k) * decay, 0.0)
    t_mat = a_mat + jnp.eye(CHUNK, dtype=jnp.float32)
    rhs = jnp.concatenate([v * beta[..., None], k_beta * jnp.exp(gc)[..., None]], axis=-1)
    sol = lax.linalg.triangular_solve(t_mat, rhs, left_side=True, lower=True,
                                      unit_diagonal=True)
    u, w = sol[..., :DV], sol[..., DV:]
    attn_intra = jnp.where(causal, jnp.einsum('bhnid,bhnjd->bhnij', q, k) * decay, 0.0)
    q_dec = q * jnp.exp(gc)[..., None]
    g_last = gc[..., -1]
    k_state = k * jnp.exp(g_last[..., None] - gc)[..., None]
    chunk_decay = jnp.exp(g_last)

    def step(state, xs):
        u_c, w_c, qd_c, at_c, ks_c, dec_c = xs
        v_new = u_c - w_c @ state
        o_c = qd_c @ state + at_c @ v_new
        state = state * dec_c[..., None, None] + jnp.einsum('bhcd,bhce->bhde', ks_c, v_new)
        return state, o_c

    xs = (jnp.moveaxis(u, 2, 0), jnp.moveaxis(w, 2, 0), jnp.moveaxis(q_dec, 2, 0),
          jnp.moveaxis(attn_intra, 2, 0), jnp.moveaxis(k_state, 2, 0),
          jnp.moveaxis(chunk_decay, 2, 0))
    s0 = jnp.zeros((B, H, DK, DV), jnp.float32)
    _, o = lax.scan(step, s0, xs)
    return o.transpose(1, 0, 3, 2, 4).reshape(B, S, H, DV)

def gdn_mixer(h, w_in, conv_w, a_log, dt_bias, out_norm, w_out):
    B, S, _ = h.shape
    H = GDN_HEADS
    proj = h @ w_in
    qkv, z, b, a = jnp.split(proj, [GDN_QKV, GDN_QKV + H * GDN_DV, GDN_QKV + H * GDN_DV + H],
                             axis=-1)
    qkv = jax.nn.silu(causal_conv(qkv, conv_w))
    q, k, v = jnp.split(qkv, [H * GDN_DK, 2 * H * GDN_DK], axis=-1)
    q = l2_norm(q.reshape(B, S, H, GDN_DK)) * (GDN_DK ** -0.5)
    k = l2_norm(k.reshape(B, S, H, GDN_DK))
    v = v.reshape(B, S, H, GDN_DV)
    beta = jax.nn.sigmoid(b.astype(jnp.float32))
    g = -jnp.exp(a_log.astype(jnp.float32)) * jax.nn.softplus(
        a.astype(jnp.float32) + dt_bias.astype(jnp.float32))
    o = chunk_gated_delta(q, k, v, g, beta).astype(h.dtype)
    o = rms_norm(o, out_norm) * jax.nn.silu(z.reshape(B, S, H, GDN_DV))
    return o.reshape(B, S, H * GDN_DV) @ w_out

def swiglu_ffn(h, w_gate_up, w_down):
    gt, up = jnp.split(h @ w_gate_up, 2, axis=-1)
    return (jax.nn.silu(gt) * up) @ w_down

def moe_ffn(h, w_router, w_gate_up, w_down):
    B, S, D = h.shape
    t = h.reshape(B * S, D)
    logits = (t @ w_router).astype(jnp.float32)
    top_val, top_idx = lax.top_k(logits, TOP_K)
    top_w = jax.nn.softmax(top_val, axis=-1)
    combine = jnp.sum(jax.nn.one_hot(top_idx, N_EXPERTS_2, dtype=jnp.float32)
                      * top_w[..., None], axis=1)
    out = jnp.zeros((B * S, D), jnp.float32)
    for e in range(N_EXPERTS_2):
        y_e = swiglu_ffn(t, w_gate_up[e], w_down[e])
        out = out + combine[:, e:e + 1] * y_e
    return out.reshape(B, S, D).astype(h.dtype)

def second_inputs(seed: int = 0) -> dict:
    key = jax.random.key(seed)
    ks = iter(jax.random.split(key, 40))
    f32 = jnp.float32

    def nrm(shape, fan_in, scale=1.0):
        return jax.random.normal(next(ks), shape, f32) * (scale * fan_in ** -0.5)

    def gain(shape):
        return 1.0 + 0.05 * jax.random.normal(next(ks), shape, f32)

    D = D_MODEL
    A, Bn = N_LAYERS_A, N_LAYERS_B
    x = jax.random.normal(next(ks), (BATCH, SEQ, D), f32)
    c = jax.random.normal(next(ks), (BATCH, D), f32)
    positions = jnp.broadcast_to(jnp.arange(SEQ, dtype=jnp.int32)[None, :], (BATCH, SEQ))
    dt = jnp.exp(jax.random.uniform(next(ks), (Bn, GDN_HEADS), f32,
                                    minval=jnp.log(0.001), maxval=jnp.log(0.1)))
    return {
        'x': x,
        'c': c,
        'positions': positions,
        'ada_w': nrm((DEPTH_2, D, N_MOD * D), D, 0.5),
        'ada_b': 0.02 * jax.random.normal(next(ks), (DEPTH_2, N_MOD * D), f32),
        'norm_mix': gain((DEPTH_2, D)),
        'norm_ffn': gain((DEPTH_2, D)),
        'mla_w_in': nrm((A, D, MLA_IN), D),
        'mla_q_norm': gain((A, Q_LORA)),
        'mla_w_qb': nrm((A, Q_LORA, MLA_HEADS * (QK_NOPE + QK_ROPE)), Q_LORA),
        'mla_kv_norm': gain((A, KV_LORA)),
        'mla_w_kvb': nrm((A, KV_LORA, MLA_HEADS * (QK_NOPE + V_HEAD)), KV_LORA),
        'mla_w_out': nrm((A, MLA_HEADS * V_HEAD, D), MLA_HEADS * V_HEAD),
        'ffn_w_gate_up': nrm((A, D, 2 * D_FF), D),
        'ffn_w_down': nrm((A, D_FF, D), D_FF),
        'gdn_w_in': nrm((Bn, D, GDN_IN), D),
        'gdn_conv_w': nrm((Bn, CONV_K_2, GDN_QKV), CONV_K_2),
        'gdn_a_log': jnp.log(jax.random.uniform(next(ks), (Bn, GDN_HEADS), f32,
                                                minval=1.0, maxval=16.0)),
        'gdn_dt_bias': dt + jnp.log(-jnp.expm1(-dt)),
        'gdn_out_norm': gain((Bn, GDN_DV)),
        'gdn_w_out': nrm((Bn, GDN_HEADS * GDN_DV, D), GDN_HEADS * GDN_DV),
        'moe_w_router': nrm((Bn, D, N_EXPERTS_2), D),
        'moe_w_gate_up': nrm((Bn, N_EXPERTS_2, D, 2 * D_FF_EXPERT), D),
        'moe_w_down': nrm((Bn, N_EXPERTS_2, D_FF_EXPERT, D), D_FF_EXPERT),
        'final_norm': gain((D,)),
    }

def second_block(x, c, positions, ada_w, ada_b, norm_mix, norm_ffn,
              mla_w_in, mla_q_norm, mla_w_qb, mla_kv_norm, mla_w_kvb, mla_w_out,
              ffn_w_gate_up, ffn_w_down,
              gdn_w_in, gdn_conv_w, gdn_a_log, gdn_dt_bias, gdn_out_norm, gdn_w_out,
              moe_w_router, moe_w_gate_up, moe_w_down, final_norm):
    cond = jax.nn.silu(c)
    for i in range(DEPTH_2):
        j = i // N_MIXERS
        mod = cond @ ada_w[i] + ada_b[i]
        sh1, sc1, g1, sh2, sc2, g2 = [m[:, None, :] for m in jnp.split(mod, N_MOD, axis=-1)]
        h = rms_norm(x, norm_mix[i]) * (1.0 + sc1) + sh1
        if i % N_MIXERS == 0:
            y = mla_mixer(h, positions, mla_w_in[j], mla_q_norm[j], mla_w_qb[j],
                          mla_kv_norm[j], mla_w_kvb[j], mla_w_out[j])
        else:
            y = gdn_mixer(h, gdn_w_in[j], gdn_conv_w[j], gdn_a_log[j], gdn_dt_bias[j],
                          gdn_out_norm[j], gdn_w_out[j])
        x = x + g1 * y
        h = rms_norm(x, norm_ffn[i]) * (1.0 + sc2) + sh2
        if i % 2 == 0:
            y = swiglu_ffn(h, ffn_w_gate_up[j], ffn_w_down[j])
        else:
            y = moe_ffn(h, moe_w_router[j], moe_w_gate_up[j], moe_w_down[j])
        x = x + g2 * y
    return rms_norm(x, final_norm)


def setup_inputs(seed=0):
    out = dict(first_inputs(seed))
    for name, value in second_inputs(seed + 1).items():
        if name != "x":
            out[name + "_2"] = value
    return out


def reference(
    x, c, ctx, c_ctx, w_ada, b_ada, w_in, conv_w, m_bias_i, m_bias_f, m_norm_w, r_w0, r_wB,
    r_a0, r_aB, r_gB, r_kk, r_ka, r_bonus, r_norm_w, r_norm_b, w_out, ln1_g, ln1_b, ln2_g,
    ln2_b, rt_g, rt_g_b, rt_e, rt_e_b, ex_gate, ex_up, ex_down, c_2, positions_2, ada_w_2,
    ada_b_2, norm_mix_2, norm_ffn_2, mla_w_in_2, mla_q_norm_2, mla_w_qb_2, mla_kv_norm_2,
    mla_w_kvb_2, mla_w_out_2, ffn_w_gate_up_2, ffn_w_down_2, gdn_w_in_2, gdn_conv_w_2,
    gdn_a_log_2, gdn_dt_bias_2, gdn_out_norm_2, gdn_w_out_2, moe_w_router_2, moe_w_gate_up_2,
    moe_w_down_2, final_norm_2,
):
    x = first_block(
        x, c, ctx, c_ctx, w_ada, b_ada, w_in, conv_w, m_bias_i, m_bias_f, m_norm_w, r_w0, r_wB,
        r_a0, r_aB, r_gB, r_kk, r_ka, r_bonus, r_norm_w, r_norm_b, w_out, ln1_g, ln1_b, ln2_g,
        ln2_b, rt_g, rt_g_b, rt_e, rt_e_b, ex_gate, ex_up, ex_down,
    )
    return second_block(
        x, c_2, positions_2, ada_w_2, ada_b_2, norm_mix_2, norm_ffn_2, mla_w_in_2, mla_q_norm_2,
        mla_w_qb_2, mla_kv_norm_2, mla_w_kvb_2, mla_w_out_2, ffn_w_gate_up_2, ffn_w_down_2,
        gdn_w_in_2, gdn_conv_w_2, gdn_a_log_2, gdn_dt_bias_2, gdn_out_norm_2, gdn_w_out_2,
        moe_w_router_2, moe_w_gate_up_2, moe_w_down_2, final_norm_2,
    )


_drawn_inputs = setup_inputs


def setup_inputs(seed=0):
    import zlib

    import numpy as np

    out = dict(_drawn_inputs(seed))
    spreads = {}
    factors = {'m_bias_i': 2.817,
     'm_norm_w': 4.439,
     'r_kk': 6.375,
     'r_norm_w': 3.911,
     'r_norm_b': 6.434,
     'rt_g_b': 8.0,
     'rt_e_b': 8.0,
     'mla_q_norm_2': 8.0,
     'mla_kv_norm_2': 4.544,
     'gdn_out_norm_2': 4.637,
     'norm_ffn_2': 3.25}
    for name, (base, spread) in spreads.items():
        noise = np.random.default_rng([zlib.crc32(name.encode()), seed]).standard_normal(out[name].shape)
        drawn = base * np.exp(spread * noise) if base else spread * noise
        out[name] = jnp.asarray(drawn.astype(out[name].dtype))
    for name, factor in factors.items():
        out[name] = (out[name] * factor).astype(out[name].dtype)
    return out
```

```python
from contextlib import ExitStack
import math

import numpy as np

import concourse.bass as bass
from concourse import mybir

ALU = mybir.AluOpType
ACT = mybir.ActivationFunctionType
AX = mybir.AxisListType
F32 = mybir.dt.float32
I32 = mybir.dt.int32
U32 = mybir.dt.uint32

P = 128
D = 1024
KT = D // P
N = 256
C = 64
NCH = 2 * N // C
H = 8
SLOT = 4096
SLOTS = 6
SEG = {"mq": 0, "mk": 4, "rr": 8, "rk": 12, "rv": 16, "mv": 20, "mo": 24}
GATES = 3584
N_EXP1, F_EXP1 = 32, 512
N_EXP2, F_EXP2 = 8, 1408
D_FF = 2816
HM, QK, ROPE, VH = 16, 96, 32, 64
Q_LORA, KV_LORA = 512, 256
ALPHA = 2.0 ** 0.25
DECAY_SCALE = math.exp(-0.5)
LN_EPS, GN_EPS, EPS = 1e-6, 64e-5, 1e-6
NEG = -1e30

ORDER = [list(range(8)), [3, 2, 1, 0, 7, 6, 5, 4]]


def constants():
    parts, at = [], {}
    p = np.arange(P)

    def put(name, a):
        a = np.asarray(a, np.float32).reshape(a.shape[0], -1)
        full = np.zeros((P, a.shape[1]), np.float32)
        full[: a.shape[0]] = a
        at[name] = (sum(x.shape[1] for x in parts), a.shape[1])
        parts.append(full)

    put("ident", np.eye(P))
    put("ones", np.ones((P, P)))
    put("zeros", np.zeros((P, P)))
    put("blk1", (p[:, None] // C) == (p[None, :] // C))
    s, t = np.arange(C)[:, None], np.arange(C)[None, :]
    past = [s < t, s > t]
    seen = [s <= t, s >= t]
    rw = np.stack([np.concatenate([past[d], seen[d]], 1) for d in range(2)], 1)
    put("rwmask", np.concatenate([rw, rw], 0))
    put("bmask65", (p[:, None] // C) == (np.arange(130)[None, :] // 65))
    lv = np.zeros((C, 6, 2, C))
    for lev in range(6):
        b = 1 << lev
        same = (s // (2 * b) == t // (2 * b)) & (s // b != t // b)
        for d in range(2):
            lv[:, lev, d] = same & past[d]
    put("level", lv)
    put("madd", np.stack([np.where(seen[d], 0.0, NEG) for d in range(2)], 1))
    pick = np.zeros((40, 2 * H, C))
    for d in range(2):
        for h in range(H):
            pick[32 * d + h, d * H + h] = 1
    put("pick", pick)
    tok = np.arange(2 * N)
    put("resetf", np.broadcast_to(tok % C != 0, (P, 2 * N)))
    put("resetb", np.broadcast_to(tok % C != C - 1, (P, 2 * N)))
    q, k = p[:, None], p[None, :]
    caus = np.where(k <= q, 0.0, NEG)
    put("causal", np.concatenate([caus, np.zeros((P, P)), caus], 1))
    put("iota8", np.broadcast_to(np.arange(8), (P, 8)))
    rot = np.zeros((QK, QK))
    half = ROPE // 2
    for i in range(half):
        rot[64 + half + i, 64 + i] = -1
        rot[64 + i, 64 + half + i] = 1
    put("rot", rot)
    inv = np.zeros((P, 1))
    inv[64:96, 0] = np.tile((10000.0 ** (-np.arange(half, dtype=np.float32) / half)).astype(np.float32), 2)
    put("invfreq", inv)
    return np.ascontiguousarray(np.concatenate(parts, 1)), at


def row_params():
    return [("c", 8), ("c_ctx", 8), ("c_2", 8), ("b_ada", 48), ("ada_b_2", 96), ("conv_w", 180), ("m_norm_w", 4),
            ("r_w0", 8), ("r_a0", 4), ("r_kk", 4), ("r_ka", 4), ("r_bonus", 4), ("r_norm_w", 4), ("r_norm_b", 4),
            ("ln1_g", 8), ("ln1_b", 8), ("ln2_g", 8), ("ln2_b", 8), ("norm_mix_2", 16), ("norm_ffn_2", 16),
            ("final_norm_2", 8), ("mla_q_norm_2", 4), ("mla_kv_norm_2", 2), ("gdn_conv_w_2", 96),
            ("gdn_out_norm_2", 1)]


ROW_TILES = 5


class Sems(dict):

    def __init__(self, nc, ctx):
        super().__init__()
        self.nc, self.ctx = nc, ctx

    def __missing__(self, name):
        self[name] = self.ctx.enter_context(self.nc.semaphore(name))
        return self[name]


class Chain:

    def __init__(self, eng, sem):
        self.eng, self.sem, self.n = eng, sem, 0

    def link(self, ins):
        self.n += 1
        ins.then_inc(self.sem, 1)
        self.eng.wait_ge(self.sem, self.n)


class Space:

    def __init__(self, tensor, start, end):
        self.t, self.pos, self.end, self.high = tensor, start, end, start

    def take(self, *shape):
        n = int(np.prod(shape))
        a = self.t[:, self.pos:self.pos + n]
        self.pos += n
        self.high = max(self.high, self.pos)
        assert self.pos <= self.end, (self.pos, self.end)
        if len(shape) == 1:
            return a
        names = "abcd"[:len(shape)]
        return a.rearrange(f"p ({' '.join(names)}) -> p {' '.join(names)}",
                           **{x: s for x, s in zip(names[1:], shape[1:])})


def along(ap, n):
    return ap.unsqueeze(len(ap.shape)).broadcast_to(list(ap.shape) + [n])


def over(ap, n, axis=1):
    shape = list(ap.shape)
    return ap.unsqueeze(axis).broadcast_to(shape[:axis] + [n] + shape[axis:])


def build(nc, A, out, const_at):
    ctx = ExitStack()
    S = Sems(nc, ctx)

    def sb(name, shape, dt=F32):
        return ctx.enter_context(nc.sbuf_tensor(name, shape, dt))[tuple(slice(None) for _ in shape)]

    n_const = sum(w for _, w in const_at.values())
    consts = sb("consts", [P, n_const])
    cols = sb("param_cols", [P, ROW_TILES * P])
    w_lora = sb("w_lora", [P, H * C])
    w_a = sb("w_a", [C, H * C])
    w_g = sb("w_g", [P, H * C])
    w_gate = sb("w_gate", [P, KT, 2, 40])
    w_rt1 = sb("w_rt1", [P, KT, 36])
    w_rt2 = sb("w_rt2", [P, KT, N_EXP2])
    w_ba = sb("w_ba", [P, KT, 16])
    rt_bias = sb("rt_bias", [P, 36])
    gate_bias = sb("gate_bias", [40, 2])
    gdn_bias = sb("gdn_bias", [H, 2])
    cond = sb("cond", [P, 3, KT, 2])
    mod1 = sb("mod1", [P, 48, 2])
    mod2 = sb("mod2", [P, 2, 48, 2])
    gain2 = sb("gain2", [P, 4, KT])
    xT = sb("xT", [P, KT, N])
    hT = sb("hT", [P, KT, N])
    xc = sb("xc", [P, KT, N])
    sq = sb("sq", [P, KT, N])
    mean = sb("mean", [P, N])
    rstd = sb("rstd", [P, N])
    tmp = sb("tmp", [P, 2, N])
    work_len = SLOTS * SLOT + 15100
    work = sb("work", [P, work_len])
    PS = ctx.enter_context(nc.psum_tensor("PS", [P, 8, 512], F32))

    ring = [work[:, i * SLOT:(i + 1) * SLOT] for i in range(SLOTS)]
    ABOVE = SLOTS * SLOT

    def const(name, parts=P):
        at, w = const_at[name]
        return consts[0:parts, at:at + w]

    ident, ones, zeros = const("ident"), const("ones"), const("zeros")

    row_at, n_rows = {}, 0
    for name, n in row_params():
        row_at[name] = n_rows
        n_rows += n
    assert n_rows <= ROW_TILES * P

    def col(name, t=0, n=1):
        return cols[:, row_at[name] + t:row_at[name] + t + n]

    pe, dve, act, pool, sp = nc.tensor, nc.vector, nc.scalar, nc.gpsimd, nc.sync
    dv = Chain(dve, S["dve_step"])
    ac = Chain(act, S["act_step"])

    landed = [S[f"landed{i}"] for i in range(SLOTS)]
    U = {}
    n_units = 0
    for name, n in (("ada", 36), ("w_in", 8), ("w_out", 2), ("moe1", 96), ("mla", 5), ("mla_out", 2), ("ffn", 18),
                    ("gdn_in", 8), ("gdn_out", 2), ("moe2", 72)):
        U[name] = n_units
        n_units += n

    def unit(u, k, n):
        return ring[u % SLOTS][:, 0:k * n].rearrange("p (k n) -> p k n", k=k)

    LOOPED = {"ada": 0, "moe1": 36, "ffn": 36 + 32, "moe2": 36 + 32 + 6}
    downs_before = LOOPED
    unit_tile = {}

    def released(u):
        name = max((x for x in U if U[x] <= u), key=lambda x: U[x])
        j = u - U[name]
        if name in LOOPED:
            n = {"ada": j + 1, "moe1": 32, "ffn": 6, "moe2": 24}[name]
            sp.wait_ge(S["weights_used"], LOOPED[name] + n)
        else:
            tile, i = unit_tile[name][j]
            sp.wait_ge(S["tile_full"], first_tile[tile] + i + 1)

    def load(u, src):
        if u >= SLOTS:
            released(u - SLOTS)
        sp.dma_start(unit(u, src.shape[1], src.shape[2]), src).then_inc(landed[u % SLOTS], 16)

    def arrived(u, i=0):
        pe.wait_ge(landed[u % SLOTS], i * 16 + 16 * (u // SLOTS + 1))

    def ktiles(w, n0, n):
        return w.rearrange("(k p) n -> p k n", p=P)[:, :, n0:n0 + n]

    tile_owner = []
    tile_count = {"act": 0, "dve": 0}
    first_tile = {}
    for name, spec in (("w_in", ["dve"] * 20 + ["act"] * 13), ("lora", ["act"] * 16), ("kap", ["act"] * 4),
                       ("bonus", ["dve"] * 4), ("w_out", ["dve"] * 8), ("mla", ["act"] * 7 + ["dve"]),
                       ("q", ["act"] * 16), ("rot", ["dve"] * 16), ("kv", ["act"] * 20), ("mla_out", ["dve"] * 8),
                       ("gdn_in", ["dve"] * 24 + ["act"] * 9), ("l2", ["act"] * 8), ("gdn_out", ["dve"] * 8)):
        first_tile[name] = len(tile_owner)
        for e in spec:
            tile_count[e] += 1
            tile_owner.append((e, tile_count[e]))

    unit_tile["w_in"] = [("w_in", 4 * j + 3) for j in range(7)] + [("w_in", 32)]
    unit_tile["w_out"] = [("w_out", 3), ("w_out", 7)]
    unit_tile["mla"] = [("mla", 3), ("mla", 6), ("q", 7), ("q", 15), ("kv", 19)]
    unit_tile["mla_out"] = [("mla_out", 3), ("mla_out", 7)]
    unit_tile["gdn_in"] = [("gdn_in", 4 * j + 3) for j in range(8)]
    unit_tile["gdn_out"] = [("gdn_out", 3), ("gdn_out", 7)]

    def tile_begin(name, i):
        g = first_tile[name] + i
        if g >= 4:
            e, n = tile_owner[g - 4]
            pe.wait_ge(S[f"emptied_{e}"], n)
        return PS[:, 4 + g % 4, :]

    def tile_full(eng, name, i):
        g = first_tile[name] + i
        eng.wait_ge(S["tile_full"], g + 1)
        return PS[:, 4 + g % 4, :]

    def all_emptied(eng, name):
        names = list(first_tile)
        at = names.index(name) + 1
        end = first_tile[names[at]] if at < len(names) else len(tile_owner)
        for e in ("act", "dve"):
            n = max([k for o, k in tile_owner[:end] if o == e], default=0)
            if n:
                eng.wait_ge(S[f"emptied_{e}"], n)

    def product(outp, pairs, **kw):
        for n, (lhs, rhs) in enumerate(pairs):
            ins = pe.matmul(outp, lhs, rhs, start=n == 0, stop=n == len(pairs) - 1, **kw)
        return ins

    tok = work[:, ABOVE:ABOVE + 4096].rearrange("p (t n) -> p t n", t=4)
    rows = work[:, ABOVE + 6144:ABOVE + 6144 + ROW_TILES * P].rearrange("p (t n) -> p t n", n=P)
    small_loads = [0]

    def stage0_act():
        def ld(dst, src):
            small_loads[0] += 1
            act.dma_start(dst, src).then_inc(S["small"], 16)

        ld(consts[:, :], A["consts"])
        ld(tok[:, 0:2, :], A["ctx"][0].rearrange("(t p) d -> p t d", p=P))
        ld(tok[:, 2:4, :], A["x"][0].rearrange("(t p) d -> p t d", p=P))
        r = 0
        act.wait_ge(S["zeroed"], 4)
        for name, n in row_params():
            a = A[name]
            flat = a
            while len(flat.shape) > 1:
                k = len(flat.shape)
                flat = flat.rearrange("a b -> (a b)" if k == 2 else "a b c -> (a b) c" if k == 3 else "a b c d -> (a b) c d")
            v = flat.rearrange("(t p) -> t p", p=P)
            t = 0
            while t < n:
                m = min(n - t, P - (r + t) % P)
                ld(rows[(r + t) % P:(r + t) % P + m, (r + t) // P, :], v[t:t + m, :])
                t += m
            r += n
        for d in range(2):
            for j in range(2):
                c0 = GATES + 16 * d + 8 * j
                ld(w_gate[:, :, j, 32 * d:32 * d + 8], ktiles(A["w_in"][0], c0, 8))
            ld(gate_bias[32 * d:32 * d + 8, 0:1], A["m_bias_i"][0, d:d + 1, :].rearrange("a h -> h a"))
            ld(gate_bias[32 * d:32 * d + 8, 1:2], A["m_bias_f"][0, d:d + 1, :].rearrange("a h -> h a"))
        ld(w_lora[:, :], A["r_wB"][0].rearrange("d k n -> (d k) n"))
        ld(w_a[:, :], A["r_aB"][0])
        ld(w_g[:, :], A["r_gB"][0])
        ld(w_rt1[:, :, 0:4], ktiles(A["rt_g"][0], 0, 4))
        ld(w_rt1[:, :, 4:36], ktiles(A["rt_e"][0], 0, 32))
        ld(w_rt2[:, :, :], ktiles(A["moe_w_router_2"][0], 0, N_EXP2))
        ld(w_ba[:, :, :], ktiles(A["gdn_w_in_2"][0], 4096, 16))
        ld(rt_bias[:, 0:4], A["rt_g_b"][0:1, :].broadcast_to([P, 4]))
        ld(rt_bias[:, 4:36], A["rt_e_b"][0:1, :].broadcast_to([P, 32]))
        ld(gdn_bias[:, 0:1], A["gdn_a_log_2"].rearrange("a h -> h a"))
        ld(gdn_bias[:, 1:2], A["gdn_dt_bias_2"].rearrange("a h -> h a"))

    def stage0_pool():
        pool.memset(w_gate[:, :, :, :], 0.0).then_inc(S["zeroed"], 1)
        pool.memset(gate_bias[:, :], 0.0).then_inc(S["zeroed"], 1)
        pool.memset(rows[:, :, :], 0.0).then_inc(S["zeroed"], 1)
        pool.memset(mean[:, :], 0.0).then_inc(S["zeroed"], 1)

    def stage0_pe():
        pe.wait_ge(S["small"], 16 * small_loads[0])
        for t in range(ROW_TILES):
            ins = pe.transpose(PS[:, t // 4, (t % 4) * P:(t % 4 + 1) * P], rows[:, t, :], ident)
        ins.then_inc(S["params_turned"], 1)
        pe.wait_ge(S["params"], 1)
        for tt in range(4):
            if tt >= 2:
                pe.wait_ge(S["x_evac"], tt - 1)
            for k in range(KT):
                ins = pe.transpose(PS[:, 2 * (tt % 2) + k // 4, (k % 4) * P:(k % 4 + 1) * P],
                                   tok[:, tt, k * P:(k + 1) * P], ident)
            ins.then_inc(S["x_turned"], 1)

    ctxT = work[:, ABOVE + 4096:ABOVE + 4096 + 2048].rearrange("p (k n) -> p k n", k=KT)

    def stage0_dve():
        dve.wait_ge(S["params_turned"], 1)
        dv.link(dve.tensor_copy(cols[:, 0:512], PS[:, 0, :]))
        dve.tensor_copy(cols[:, 512:640], PS[:, 1, 0:128]).then_inc(S["params"], 1)
        dve.wait_ge(S["params"], 1)

    def stage0_act2():
        act.wait_ge(S["params"], 1)
        for a, (l, c) in enumerate((("c", "c_ctx"), ("c_2", "c_2"), ("c_2", "c_2"))):
            act.activation(cond[:, a, :, 0], col(l, 0, KT), ACT.Silu)
            ins = act.activation(cond[:, a, :, 1], col(c, 0, KT), ACT.Silu)
        ins.then_inc(S["cond"], 1)
        for tt in range(4):
            act.wait_ge(S["x_turned"], tt + 1)
            dst = (ctxT if tt < 2 else xT)[:, :, (tt % 2) * P:(tt % 2 + 1) * P]
            b = 2 * (tt % 2)
            act.activation(dst, PS[:, b:b + 2, :].rearrange("p b (k n) -> p (b k) n", n=P), ACT.Copy)\
               .then_inc(S["x_evac"], 1)

    ADA_BANK = 7
    ada_src = [(A["w_ada"][0]), (A["ada_w_2"][0]), (A["ada_w_2"][1])]

    def ada_sp():
        for a in range(3):
            for i in range(2):
                for j in range(SLOTS):
                    load(12 * a + 6 * i + j, ktiles(ada_src[a], (6 * i + j) * 512, 512))

    def ada_pe():
        pe.wait_ge(S["cond"], 1)
        for a in range(3):
            with pe.Fori(0, 2) as i:
                for j in range(SLOTS):
                    u = 12 * a + j
                    arrived(u, i)
                    w = unit(u, KT, 512)
                    for m in range(4):
                        o = PS[:, ADA_BANK, bass.ds(i * 48 + (a * 96 + (j * 4 + m) * 2), 2)]
                        ins = product(o, [(w[:, k, m * P:(m + 1) * P], cond[:, a, k, :]) for k in range(KT)])
                    ins.then_inc(S["weights_used"], 1)

    def ada_dve():
        dve.wait_ge(S["weights_used"], U["w_in"])
        dv.link(dve.tensor_tensor(mod1[:, :, :], PS[:, ADA_BANK, 0:96].rearrange("p (m s) -> p m s", s=2),
                                  along(col("b_ada", 0, 48), 2), ALU.add))
        dv.link(dve.tensor_tensor(mod2[:, :, :, :].rearrange("p l m s -> p (l m) s"),
                                  PS[:, ADA_BANK, 96:288].rearrange("p (m s) -> p m s", s=2),
                                  along(col("ada_b_2", 0, 96), 2), ALU.add))
        for m in (8, 32):
            dv.link(dve.tensor_scalar(mod1[:, m:m + 8, :], mod1[:, m:m + 8, :], 1.0, None, ALU.add))
            dv.link(dve.tensor_scalar(mod2[:, :, m:m + 8, :], mod2[:, :, m:m + 8, :], 1.0, None, ALU.add))
        for l in range(2):
            dv.link(dve.tensor_tensor(gain2[:, 2 * l, :], mod2[:, l, 8:16, 0], col("norm_mix_2", 8 * l, 8), ALU.mult))
            dv.link(dve.tensor_tensor(gain2[:, 2 * l + 1, :], mod2[:, l, 32:40, 0], col("norm_ffn_2", 8 * l, 8), ALU.mult))

    def norm_pe(n, src, kt, centred, ready):
        if centred:
            ready(pe)
            product(PS[:, 0, 0:N], [(ones, src[:, k, :]) for k in range(kt)]).then_inc(S["norm_mean"], 1)
        pe.wait_ge(S["norm_sq"], n + 1)
        product(PS[:, 1, 0:N], [(ones, sq[:, k, :]) for k in range(kt)]).then_inc(S["norm_var"], 1)

    centred_norms = [0]

    def norm_dve(n, src, kt, centred, dst, gains, biases, eps):
        width = kt * P
        if centred:
            centred_norms[0] += 1
            dve.wait_ge(S["norm_mean"], centred_norms[0])
            dv.link(dve.tensor_scalar(mean[:, :], PS[:, 0, 0:N], 1.0 / width, None, ALU.mult))
            dv.link(dve.tensor_tensor(xc[:, 0:kt, :], src, over(mean[:, :], kt), ALU.subtract))
            src = xc[:, 0:kt, :]
        dve.tensor_tensor(sq[:, 0:kt, :], src, src, ALU.mult).then_inc(S["norm_sq"], 1)
        dve.wait_ge(S["norm_var"], n + 1)
        dve.tensor_scalar(tmp[:, 0, :], PS[:, 1, 0:N], 1.0 / width, eps, ALU.mult, ALU.add).then_inc(S["norm_ms"], 1)
        dve.wait_ge(S["norm_std"], n + 1)
        dv.link(dve.reciprocal(rstd[:, :], tmp[:, 1, :]))
        dv.link(dve.tensor_tensor(xc[:, 0:kt, :], src, over(rstd[:, :], kt), ALU.mult))
        for k in range(kt):
            if biases is None:
                ins = dve.tensor_scalar(dst[:, k, :], xc[:, k, :], gains(k), None, ALU.mult)
            else:
                ins = dve.tensor_scalar(dst[:, k, :], xc[:, k, :], gains(k), biases(k), ALU.mult, ALU.add)
        ins.then_inc(S["norm_done"], 1)
        dve.wait_ge(S["norm_done"], n + 1)

    def norm_act(n):
        act.wait_ge(S["norm_ms"], n + 1)
        act.activation(tmp[:, 1, :], tmp[:, 0, :], ACT.Sqrt).then_inc(S["norm_std"], 1)

    above = Space(work, ABOVE, work_len)
    hall = above.take(KT, 2 * N)
    q1 = above.take(4, N)
    rr = above.take(4, N)
    rv = above.take(4, C + 2 * N)
    mo = above.take(4, N)
    li, lf = above.take(2 * N), above.take(2 * N)
    lw, la, lg = above.take(2 * N), above.take(2 * N), above.take(N)
    mixT = above.take(KT, N)
    gT = above.take(4, N)
    k1 = hT[:, :, :].rearrange("p (k a) n -> p k (a n)", a=2)
    rk = xc[:, :, :].rearrange("p (k a) n -> p k (a n)", a=2)
    mv = sq[:, :, :].rearrange("p (k a) n -> p k (a n)", a=2)
    section = [("mq", q1, True), ("mk", k1, False), ("rr", rr, True), ("rk", rk, False), ("rv", rv[:, :, C:], False),
               ("mv", mv, False), ("mo", mo, True)]

    def w_in_sp():
        for j in range(7):
            load(U["w_in"] + j, ktiles(A["w_in"][0], 512 * j, 512))
        load(U["w_in"] + 7, ktiles(A["w_in"][0], GATES, 352))

    def norm1_pe():
        for n, src in enumerate((ctxT, xT)):
            norm_pe(n, src, KT, True, lambda e: e.wait_ge(S["x_evac"], 4))

    def norm1_act():
        for n in range(2):
            norm_act(n)

    def norm1_dve():
        for n, (src, which) in enumerate(((ctxT, 1), (xT, 0))):
            norm_dve(n, src, KT, True, hall[:, :, n * N:(n + 1) * N], lambda k: mod1[:, 8 + k, which:which + 1],
                     lambda k: mod1[:, k, which:which + 1], LN_EPS)

    def w_in_pe():
        pe.wait_ge(S["norm_done"], 2)
        for i in range(28):
            if i % 4 == 0:
                arrived(U["w_in"] + i // 4)
            w = unit(U["w_in"] + i // 4, KT, 512)
            o = tile_begin("w_in", i)
            lat = section[i // 4][2]
            t0, n = (N, N) if lat else (0, 2 * N)
            product(o[:, 0:n], [(w[:, k, (i % 4) * P:(i % 4 + 1) * P], hall[:, k, t0:t0 + n]) for k in range(KT)])\
                .then_inc(S["tile_full"], 1)
        for j in range(2):
            o = tile_begin("w_in", 28 + j)
            product(o[0:40, :], [(w_gate[:, k, j, :], hall[:, k, :]) for k in range(KT)]).then_inc(S["tile_full"], 1)
        arrived(U["w_in"] + 7)
        w = unit(U["w_in"] + 7, KT, 352)
        for j, (c0, m, t0, n) in enumerate(((32, P, 0, 2 * N), (160, C, 0, 2 * N), (224, P, N, N))):
            o = tile_begin("w_in", 30 + j)
            product(o[0:m, 0:n], [(w[:, k, c0:c0 + m], hall[:, k, t0:t0 + n]) for k in range(KT)])\
                .then_inc(S["tile_full"], 1)

    def conv_dve():
        for i in range(20):
            o = tile_full(dve, "w_in", i)
            _, dst, lat = section[i // 4]
            y = dst[:, i % 4, :]

            def w(a, b):
                return col("conv_w", (3 * a + b) * 20 + i)

            n = N if lat else 2 * N
            dv.link(dve.tensor_scalar(y, o[:, 0:n], w(1, 1), None, ALU.mult))
            if not lat:
                for b, (y0, y1, x0, x1) in ((0, (1, N, 0, N - 1)), (2, (0, N - 1, 1, N))):
                    dv.link(dve.scalar_tensor_tensor(out=y[:, y0:y1], in0=o[:, x0:x1], scalar=w(1, b), in1=y[:, y0:y1],
                                                     op0=ALU.mult, op1=ALU.add))
            yg = y[:, n - N:n].rearrange("p (r c) -> p r c", c=64)
            xg = o[:, n - N:n].rearrange("p (r c) -> p r c", c=64)
            taps = [(a, b) for a in range(3) for b in range(3) if (a, b) != (1, 1)]
            for a, b in taps:
                r0, r1 = max(0, 1 - a), min(4, 5 - a)
                c0, c1 = max(0, 1 - b), min(64, 65 - b)
                ins = dve.scalar_tensor_tensor(
                    out=yg[:, r0:r1, c0:c1], in0=xg[:, r0 + a - 1:r1 + a - 1, c0 + b - 1:c1 + b - 1], scalar=w(a, b),
                    in1=yg[:, r0:r1, c0:c1], op0=ALU.mult, op1=ALU.add)
                if (a, b) == taps[-1]:
                    ins.then_inc(S["emptied_dve"], 1)
                else:
                    dv.link(ins)

    def w_in_act():
        def evac(i, dst, src, func, **kw):
            act.activation(dst, src, func, **kw).then_inc(S["emptied_act"], 1)

        for i in range(20, 24):
            evac(i, mv[:, i - 20, :], tile_full(act, "w_in", i), ACT.Copy)
        for i in range(24, 28):
            evac(i, mo[:, i - 24, :], tile_full(act, "w_in", i)[:, 0:N], ACT.Sigmoid)
        for j, dst in enumerate((li, lf)):
            evac(28 + j, dst[0:40, :], tile_full(act, "w_in", 28 + j)[0:40, :], ACT.Identity, bias=gate_bias[:, j:j + 1])
        evac(30, lw, tile_full(act, "w_in", 30), ACT.Tanh)
        evac(31, la[0:C, :], tile_full(act, "w_in", 31)[0:C, :], ACT.Copy)
        evac(32, lg, tile_full(act, "w_in", 32)[:, 0:N], ACT.Sigmoid)
        act.wait_ge(S["emptied_dve"], 8)
        ac.link(act.activation(q1, q1, ACT.Silu))
        ac.link(act.activation(k1, k1, ACT.Silu))
        act.activation(k1, k1, ACT.Copy, scale=C ** -0.5).then_inc(S["qk_ready"], 1)

    R40 = 40
    ml = Space(work, 0, SLOTS * SLOT)
    z_ = ml.take(2 * N)
    e_ = ml.take(2 * N)
    b_, m_, a_, Dm, nD = (ml.take(2 * N) for _ in range(5))
    inter, einvm, wts = (ml.take(2 * N) for _ in range(3))
    mprev, DC, decay = (ml.take(NCH) for _ in range(3))
    diag = ml.take(NCH, R40)
    wtok = ml.take(NCH, R40)
    gtok = ml.take(3, 4, R40)
    decb = ml.take(NCH, R40)
    vt = ml.take(NCH, H, C + 1)
    Cst = ml.take(4, 2, 2 * (C + 1))
    kw = ml.take(2, H, C)
    Em = ml.take(2, H, C)
    Pm = ml.take(2, H, C)
    hn = ml.take(2, 2, 4, C + 1)
    den, rden = ml.take(2, H), ml.take(2, H)
    hs = ml.take(4, H * C)
    hsq = ml.take(4, H * C)
    ct = ml.take(4, 2, 2 * (C + 1))
    kw2 = ml.take(2, H, C)
    hstat = [ml.take(4 * H) for _ in range(2)]
    g40 = lambda t: t[0:R40, :]
    T64 = lambda t: t[0:C]

    def ml_pool():
        pool.wait_ge(S["tile_full"], first_tile["w_in"] + 33)
        for t in (b_, m_, mprev, DC):
            pool.memset(g40(t), 0.0)
        pool.memset(vt[0:C], 1.0)
        pool.memset(Cst, 0.0)
        pool.memset(hs[0:C], 0.0)
        pool.memset(rv[:, :, 0:C], 0.0).then_inc(S["ml_zero"], 1)

    def ml_gates_dve():
        dve.wait_ge(S["emptied_act"], 10)
        dve.wait_ge(S["tile_full"], first_tile["w_in"] + 33)
        dve.wait_ge(S["ml_zero"], 1)
        dve.scalar_tensor_tensor(out=g40(z_), in0=g40(lf), scalar=-1.0, in1=g40(lf), op0=ALU.mult, op1=ALU.max).then_inc(S["ml_z"], 1)
        dve.wait_ge(S["ml_l"], 1)
        dv.link(dve.scalar_tensor_tensor(out=g40(lf), in0=g40(lf), scalar=0.0, in1=g40(e_), op0=ALU.min,
                                         op1=ALU.subtract))
        f, w = slice(0, 8), slice(32, 40)
        rf, rb = const("resetf"), const("resetb")
        dv.link(dve.tensor_tensor_scan(b_[f, :], rf[f, :], lf[f, :], 0.0, ALU.mult, ALU.add))
        dv.link(dve.tensor_tensor_scan(b_[w, ::-1], rb[w, ::-1], lf[w, ::-1], 0.0, ALU.mult, ALU.add))
        dv.link(dve.tensor_tensor_scan(m_[f, :], lf[f, :], li[f, :], 0.0, ALU.add, ALU.max))
        for s0 in (0, N):
            part = lambda t: t[w, s0:s0 + N][:, ::-1]
            dv.link(dve.tensor_tensor_scan(part(m_), part(lf), part(li), m_[w, 0:1] if s0 else 0.0, ALU.add, ALU.max))
        dv.link(dve.tensor_copy(mprev[f, 1:8], m_[f, 63:511:C]))
        dv.link(dve.tensor_copy(mprev[w, 0:3], m_[w, 64:256:C]))
        dv.link(dve.tensor_copy(mprev[w, 4:7], m_[w, 320:512:C]))
        dv.link(dve.tensor_copy(mprev[w, 7:8], m_[w, 0:1]))
        dv.link(dve.tensor_tensor(g40(a_), g40(li), g40(b_), ALU.subtract))
        dv.link(dve.tensor_tensor(g40(Dm), g40(m_), g40(b_), ALU.subtract))
        dv.link(dve.tensor_tensor(g40(nD), g40(b_), g40(m_), ALU.subtract))
        dv.link(dve.tensor_copy(DC[f, :], Dm[f, 63::C]))
        dv.link(dve.tensor_copy(DC[w, :], Dm[w, 0::C]))
        chunked = lambda t: g40(t).rearrange("p (c t) -> p c t", t=C)
        dv.link(dve.tensor_tensor(chunked(inter), along(g40(mprev), C), chunked(Dm), ALU.subtract))
        dv.link(dve.tensor_tensor(chunked(wts), chunked(a_), along(g40(DC), C), ALU.subtract))
        dve.tensor_tensor(g40(decay), g40(mprev), g40(DC), ALU.subtract).then_inc(S["ml_args"], 1)
        dve.wait_ge(S["ml_gexp"], 1)
        dve.tensor_tensor(diag[0:R40], over(ident[0:R40, 0:R40], NCH), along(g40(decay), R40), ALU.mult)\
           .then_inc(S["ml_diag"], 1)
        dve.wait_ge(S["ml_tok"], 1)
        dv.link(dve.tensor_copy(T64(wtok), PS[0:C, 0, 0:NCH * R40].rearrange("p (c r) -> p c r", r=R40)))
        dv.link(dve.tensor_copy(T64(gtok), PS[0:C, 1, 0:12 * R40].rearrange("p (g c r) -> p g c r", g=3, r=R40)))
        dve.tensor_copy(decb, PS[:, 2, 0:NCH * R40].rearrange("p (c r) -> p c r", r=R40)).then_inc(S["ml_gtok"], 1)
        dve.wait_ge(S["ml_gtok"], 1)

    def ml_gates_act():
        act.wait_ge(S["ml_z"], 1)
        ac.link(act.activation(g40(e_), g40(z_), ACT.Exp, scale=-1.0))
        act.activation(g40(e_), g40(e_), ACT.Ln, bias=1.0).then_inc(S["ml_l"], 1)
        act.wait_ge(S["ml_args"], 1)
        act.activation(g40(inter), g40(inter), ACT.Exp)
        act.activation(g40(wts), g40(wts), ACT.Exp)
        act.activation(g40(decay), g40(decay), ACT.Exp)
        act.activation(g40(einvm), g40(m_), ACT.Exp, scale=-1.0).then_inc(S["ml_gexp"], 1)
        act.wait_ge(S["ml_zero"], 1)
        for c in range(NCH):
            act.wait_ge(S["ml_vt"], c + 1)
            act.activation(vt[0:C, c, :, 0:C], PS[0:C, 4 + c % 4, :].rearrange("p (h e) -> p h e", h=H), ACT.Copy)\
               .then_inc(S["ml_ve"], 1)

    def ml_gates_pe():
        all_emptied(pe, "w_in")
        for c in range(NCH):
            if c >= 4:
                pe.wait_ge(S["ml_ve"], c - 3)
            for p in range(4):
                ins = pe.transpose(PS[0:C, 4 + c % 4, p * P:(p + 1) * P], mv[:, p, c * C:(c + 1) * C], ident)
            ins.then_inc(S["ml_vt"], 1)
        pe.wait_ge(S["ml_diag"], 1)
        i40 = ident[0:R40, 0:R40]
        for c in range(NCH):
            pe.transpose(PS[0:C, 0, c * R40:(c + 1) * R40], wts[0:R40, c * C:(c + 1) * C], i40)
        for g, t in enumerate((a_, inter, einvm)):
            for c in range(4):
                o = (g * 4 + c) * R40
                pe.transpose(PS[0:C, 1, o:o + R40], t[0:R40, (4 + c) * C:(5 + c) * C], i40)
        pe.matmul(PS[:, 2, 0:NCH * R40], ones[0:R40, :], diag[0:R40].rearrange("p c r -> p (c r)"), start=True,
                  stop=True).then_inc(S["ml_tok"], 1)
        pe.wait_ge(S["ml_ve"], NCH)
        pe.wait_ge(S["ml_gtok"], 1)
        pe.wait_ge(S["qk_ready"], 1)

    def half(h):
        return slice(C * (h % 2), C * (h % 2) + C)

    def ml_step_pe(i):
        if i:
            pe.wait_ge(S["ml_step"], i)
        cs = [ORDER[d][i] for d in range(2)]
        lat = i >= 4
        for d in range(2):
            for p in range(4):
                ins = pe.transpose(PS[0:C, d, p * P:(p + 1) * P], k1[:, p, cs[d] * C:(cs[d] + 1) * C], ident)
        ins.then_inc(S["ml_ktok"], 1)
        if lat:
            for d in range(2):
                ck, cq = cs[d] * C, (cs[d] - 4) * C
                for h in range(H):
                    at = (d * 4 + h // 2) * C
                    pe.matmul(PS[0:C, 2 + h % 2, at:at + C], k1[half(h), h // 2, ck:ck + C],
                              q1[half(h), h // 2, cq:cq + C], start=True, stop=True)
                o = PS[0:C, 4 + d, :]
                pe.matmul(o, ident[0:C, 0:C], over(const("madd", C)[:, d * C:(d + 1) * C], H), start=True, stop=False,
                          skip_group_check=True)
                for h in range(H):
                    at = (d * H + h) * C
                    ins = pe.matmul(o[:, h * C:(h + 1) * C], const("pick", R40)[:, at:at + C],
                                    nD[0:R40, ck:ck + C], start=False, stop=h == H - 1, skip_group_check=True)
            ins.then_inc(S["ml_sc"], 1)
            pe.wait_ge(S["ml_p"], i - 3)
        pe.wait_ge(S["ml_kw"], i + 1)
        if lat:
            for d in range(2):
                cq = (cs[d] - 4) * C
                for p in range(4):
                    pe.matmul(PS[0:C, 4 + 2 * d + p // 2, (p % 2) * 130:(p % 2) * 130 + 130], q1[:, p, cq:cq + C],
                              Cst[:, 2 * d + p // 2, p % 2, :], start=True, stop=True)
                for h in range(H):
                    ins = pe.matmul(PS[0:C, 2 * d + h // 4, (h % 4) * 65:(h % 4) * 65 + 65], Pm[0:C, d, h, :],
                                    vt[0:C, cs[d], h, :], start=True, stop=True)
            ins.then_inc(S["ml_num"], 1)
            pe.wait_ge(S["ml_hn"], i - 3)
        if i < NCH - 1:
            for d in range(2):
                for p in range(4):
                    ins = pe.matmul(PS[:, 4 + 2 * d + p // 2, (p % 2) * 130:(p % 2) * 130 + 130],
                                    kw[0:C, d, 2 * p:2 * p + 2, :].rearrange("s h e -> s (h e)"),
                                    vt[0:C, cs[d], 2 * p:2 * p + 2, :].rearrange("s h e -> s (h e)"), start=True, stop=True)
            ins.then_inc(S["ml_st"], 1)

    def ml_step_dve(i):
        cs = [ORDER[d][i] for d in range(2)]
        lat = i >= 4
        rows_of = lambda d: slice(32 * d, 32 * d + 8)
        dve.wait_ge(S["ml_ktok"], i + 1)
        for d in range(2):
            ins = dve.tensor_tensor(kw[0:C, d], PS[0:C, d, :].rearrange("p (h e) -> p h e", h=H),
                                    along(wtok[0:C, cs[d], rows_of(d)], C), ALU.mult)
        ins.then_inc(S["ml_kw"], 1)
        if lat:
            j = i - 4
            dve.wait_ge(S["ml_sc"], j + 1)
            for d in range(2):
                ins = dve.tensor_tensor(Em[0:C, d], PS[0:C, 4 + d, :].rearrange("p (h t) -> p h t", h=H),
                                        along(gtok[0:C, 0, cs[d] - 4, rows_of(d)], C), ALU.add)
            ins.then_inc(S["ml_e"], 1)
            dve.wait_ge(S["ml_exp"], j + 1)
            for b in range(2):
                ins = dve.tensor_tensor(Pm[0:C, :, b::2, :], PS[0:C, 2 + b, :].rearrange("p (d h t) -> p d h t", d=2, t=C),
                                        Em[0:C, :, b::2, :], ALU.mult)
            ins.then_inc(S["ml_p"], 1)
            dve.wait_ge(S["ml_num"], j + 1)
            for d in range(2):
                g = gtok[0:C, 1, cs[d] - 4, rows_of(d)].rearrange("p (b h) -> p b h", b=2)
                ins = dve.tensor_tensor(hn[0:C, d], PS[0:C, 4 + 2 * d:6 + 2 * d, 0:260].rearrange("p b (h e) -> p b h e", h=4),
                                        along(g, C + 1), ALU.mult)
            dv.link(ins)
            h4 = hn[0:C].rearrange("p d b h e -> p (d b) (h e)")
            dve.tensor_tensor(h4, h4, PS[0:C, 0:4, 0:260], ALU.add).then_inc(S["ml_hn"], 1)
            dve.wait_ge(S["ml_hn"], j + 1)
            hz = hn[0:C].rearrange("p d b h e -> p d (b h) e")
            dv.link(dve.scalar_tensor_tensor(out=den[0:C], in0=hz[:, :, :, C], scalar=-1.0, in1=hz[:, :, :, C], op0=ALU.mult,
                                             op1=ALU.max))
            for d in range(2):
                ins = dve.tensor_tensor(den[0:C, d], den[0:C, d], gtok[0:C, 2, cs[d] - 4, rows_of(d)], ALU.max)
            dv.link(ins)
            dv.link(dve.reciprocal(rden[0:C], den[0:C]))
            dv.link(dve.tensor_tensor(kw2[0:C], hz[:, :, :, 0:C], along(rden[0:C], C), ALU.mult))
            for d in range(2):
                dst = hs[0:C, cs[d] - 4, :].rearrange("p (h e) -> p h e", h=H)
                dv.link(dve.tensor_tensor(dst, dst, kw2[0:C, d], ALU.add))
        if i < NCH - 1:
            dve.wait_ge(S["ml_st"], i + 1)
            dv.link(dve.tensor_tensor(ct, PS[:, 4:8, 0:260].rearrange("p b (q e) -> p b q e", q=2),
                                      over(over(const("bmask65"), 2), 4), ALU.mult))
            for d in range(2):
                cv = Cst[:, 2 * d:2 * d + 2].rearrange("p b q (h e) -> p (b q h) e", h=2)
                ins = dve.tensor_tensor(cv, cv, along(decb[:, cs[d], rows_of(d)], C + 1), ALU.mult)
            dv.link(ins)
            dve.tensor_tensor(Cst, Cst, ct, ALU.add).then_inc(S["ml_step"], 1)
            dve.wait_ge(S["ml_step"], i + 1)

    def ml_step_act(i):
        if i >= 4:
            act.wait_ge(S["ml_e"], i - 3)
            act.activation(Em[0:C], Em[0:C], ACT.Exp).then_inc(S["ml_exp"], 1)

    def headnorm_dve(n, buf, scratch, stat, eps):
        v = buf[0:C].rearrange("p c (h e) -> p (c h) e", e=C)
        w = scratch[0:C].rearrange("p c (h e) -> p (c h) e", e=C)
        s0, s1 = stat[0][0:C, :], stat[1][0:C, :]
        dv.link(dve.tensor_reduce(s0, v, AX.X, ALU.add))
        dv.link(dve.tensor_scalar(s0, s0, 1.0 / C, None, ALU.mult))
        dv.link(dve.tensor_tensor(v, v, along(s0, C), ALU.subtract))
        dv.link(dve.tensor_tensor(w, v, v, ALU.mult))
        dv.link(dve.tensor_reduce(s0, w, AX.X, ALU.add))
        dve.tensor_scalar(s1, s0, 1.0 / C, eps, ALU.mult, ALU.add).then_inc(S["hn_var"], 1)
        dve.wait_ge(S["hn_std"], n + 1)
        dv.link(dve.reciprocal(s0, s1))
        dve.tensor_tensor(v, v, along(s0, C), ALU.mult).then_inc(S["hn_done"], 1)
        dve.wait_ge(S["hn_done"], n + 1)

    def headnorm_act(n, stat):
        act.wait_ge(S["hn_var"], n + 1)
        act.activation(stat[1][0:C, :], stat[1][0:C, :], ACT.Sqrt).then_inc(S["hn_std"], 1)

    def headnorm_pe(n, buf):
        pe.wait_ge(S["hn_done"], n + 1)
        for p in range(4):
            for c in range(4):
                ins = pe.transpose(PS[:, p, c * C:(c + 1) * C], buf[0:C, c, p * P:(p + 1) * P], ident[0:C, 0:C])
        ins.then_inc(S["hn_turned"], 1)

    def ml_out_dve():
        dve.wait_ge(S["hn_turned"], 1)
        dve.wait_ge(S["emptied_act"], 8)
        for p in range(4):
            ins = dve.scalar_tensor_tensor(out=mixT[:, p, :], in0=PS[:, p, 0:N], scalar=col("m_norm_w", p),
                                           in1=mo[:, p, :], op0=ALU.mult, op1=ALU.mult)
        ins.then_inc(S["ml_out"], 1)
        dve.wait_ge(S["ml_out"], 1)

    rw = Space(work, 0, SLOTS * SLOT)
    BK = rw.take(2, 4, NCH * 2 * C)
    KR = rw.take(2, 4, NCH * 2 * C)
    BKc = [BK[:, d].rearrange("p q (c j t) -> p q c j t", c=NCH, j=2) for d in range(2)]
    KRc = [KR[:, d].rearrange("p q (c j t) -> p q c j t", c=NCH, j=2) for d in range(2)]
    lw2 = [rw.take(4, 2 * N), hall[:, 0:4, :]]
    kh, nb = rw.take(4, 2 * N), rw.take(4, 2 * N)
    kmod = hall[:, 4:8, :]
    csum = k1
    eb = [rk, mv]
    kss = mv
    at = rw.pos - 3 * 4 * 2 * N
    later = Space(work, at, rw.pos)
    Msc = later.take(2 * H, 2 * C)
    BKt, UV = later.take(2, H * C), later.take(2, H * C)
    CTm, Xm = later.take(2 * H, C), later.take(2 * H, C)
    later = Space(work, ABOVE, ABOVE + KT * 2 * N)
    XTm, Ym = later.take(2 * H, C), later.take(2 * H, C)
    Gs = later.take(2, H * C)
    S0 = later.take(2, 4, P)
    yr = hT[:, :, :].rearrange("p (c a) n -> p c (a n)", a=2)
    st = xc[:, 0:4, :].rearrange("p (d q) n -> p d (q n)", d=2).rearrange("p d (q n) -> p d q n", n=P)
    ysq = sq[:, :, :].rearrange("p (c a) n -> p c (a n)", a=2)
    ystat = [tmp[:, 0, 128 + 32 * j:160 + 32 * j] for j in range(2)]
    eC = tmp[:, 0, 0:64].rearrange("p (d q c) -> p d q c", d=2, q=4)
    omka = tmp[:, 0, 64:68]
    prod = q1
    rv_all = rv[:, :, C:]

    def rw_prep_pe():
        pe.wait_ge(S["hn_turned"], 1)
        for j in range(12):
            o = tile_begin("lora", j)
            p = j % 4
            if j < 8:
                s = slice(C * (j // 4), C * (j // 4) + C)
                pairs = [(w_lora[s, p * P:(p + 1) * P], lw[s, :])]
            else:
                pairs = [(w_a[:, p * P:(p + 1) * P], la[0:C, :])]
            product(o, pairs).then_inc(S["tile_full"], 1)
        for p in range(4):
            product(tile_begin("lora", 12 + p)[:, 0:N], [(w_g[:, p * P:(p + 1) * P], lg)]).then_inc(S["tile_full"], 1)
        pe.wait_ge(S["rw_kap"], 1)
        for p in range(4):
            product(tile_begin("kap", p), [(const("blk1"), eb[1][:, p, :])]).then_inc(S["tile_full"], 1)
        pe.wait_ge(S["rw_bonus"], 1)
        for p in range(4):
            product(tile_begin("bonus", p)[:, 0:N], [(const("blk1"), prod[:, p, :])]).then_inc(S["tile_full"], 1)

    def rw_prep_act():
        def evac(name, i, dst, src, func, **kw):
            act.activation(dst, src, func, **kw).then_inc(S["emptied_act"], 1)

        act.wait_ge(S["ml_out"], 1)
        for j in range(12):
            p = j % 4
            dst, bias = (lw2[j // 4][:, p, :], col("r_w0", j)) if j < 8 else (nb[:, p, :], col("r_a0", p))
            evac("lora", j, dst, tile_full(act, "lora", j), ACT.Sigmoid, bias=bias)
        for p in range(4):
            evac("lora", 12 + p, gT[:, p, :], tile_full(act, "lora", 12 + p)[:, 0:N], ACT.Copy)
        for p in range(4):
            evac("kap", p, csum[:, p, :], tile_full(act, "kap", p), ACT.Copy)
        act.wait_ge(S["rw_kss"], 1)
        ac.link(act.activation(csum, csum, ACT.Ln, scale=2.0 ** 20))
        act.activation(csum, csum, ACT.Exp, scale=-0.5, bias=10 * math.log(2.0)).then_inc(S["rw_rs"], 1)
        for n in range(6):
            act.wait_ge(S["rw_arg"], n + 1)
            src, scale = ((eb[n % 2], 1.0), (csum, 1.0), (csum, -1.0))[n % 3]
            act.activation(eb[n % 2], src, ACT.Exp, scale=scale).then_inc(S["rw_exp"], 1)

    def rw_prep_dve():
        for p in range(4):
            ins = dve.tensor_scalar(kh[:, p, :], rk[:, p, :], col("r_kk", p), None, ALU.mult)
        dv.link(ins)
        dve.tensor_tensor(eb[1], kh, kh, ALU.mult).then_inc(S["rw_kap"], 1)
        dv.link(dve.tensor_scalar(omka, col("r_ka", 0, 4), -1.0, 1.0, ALU.mult, ALU.add))
        dve.wait_ge(S["emptied_act"], tile_owner[first_tile["lora"] + 11][1])
        for p in range(4):
            ins = dve.tensor_scalar(kmod[:, p, :], nb[:, p, :], col("r_ka", p), omka[:, p:p + 1], ALU.mult, ALU.add)
        dv.link(ins)
        dv.link(dve.tensor_tensor(kmod, kmod, rk, ALU.mult))
        for p in range(4):
            ins = dve.scalar_tensor_tensor(out=prod[:, p, :], in0=rr[:, p, :], scalar=col("r_bonus", p),
                                           in1=kmod[:, p, N:2 * N], op0=ALU.mult, op1=ALU.mult)
        ins.then_inc(S["rw_bonus"], 1)
        dve.wait_ge(S["emptied_act"], tile_owner[first_tile["kap"] + 3][1])
        dve.tensor_scalar(csum, csum, 1e-24, None, ALU.max).then_inc(S["rw_kss"], 1)
        for p in range(4):
            o = tile_full(dve, "bonus", p)[:, 0:N]
            ins = dve.tensor_tensor(prod[:, p, :], o, rv_all[:, p, N:2 * N], ALU.mult)
            ins.then_inc(S["emptied_dve"], 1)
        dve.wait_ge(S["rw_rs"], 1)
        dv.link(dve.tensor_tensor(kh, kh, csum, ALU.mult))
        dv.link(dve.scalar_tensor_tensor(out=nb, in0=kh, scalar=-1.0, in1=nb, op0=ALU.mult, op1=ALU.mult))
        n = 0
        for d in range(2):
            dv.link(dve.tensor_scalar(lw2[d], lw2[d], -DECAY_SCALE, None, ALU.mult))
            mask = const("resetb" if d else "resetf")
            step = -1 if d else 1
            for p in range(4):
                ins = dve.tensor_tensor_scan(csum[:, p, ::step], mask[:, ::step], lw2[d][:, p, ::step], 0.0, ALU.mult,
                                             ALU.add)
            dv.link(ins)
            chunks = lambda t: t.rearrange("p q (c t) -> p q c t", t=C)
            dve.tensor_tensor(eb[n % 2], csum, lw2[d], ALU.subtract).then_inc(S["rw_arg"], 1)
            dve.wait_ge(S["rw_exp"], n + 1)
            dve.tensor_tensor(KRc[d][:, :, :, 0, :], chunks(kh), chunks(eb[n % 2]), ALU.mult).then_inc(S["rw_arg"], 1)
            n += 1
            dve.wait_ge(S["rw_exp"], n + 1)
            e = chunks(eb[n % 2])
            dv.link(dve.tensor_copy(eC[:, d], e[:, :, :, 0 if d else C - 1]))
            dve.tensor_tensor(KRc[d][:, :, 4:8, 1, :], chunks(rr), e[:, :, 4:8, :], ALU.mult).then_inc(S["rw_arg"], 1)
            n += 1
            dve.wait_ge(S["rw_exp"], n + 1)
            e = chunks(eb[n % 2])
            dv.link(dve.tensor_tensor(BKc[d][:, :, :, 0, :], chunks(nb), e, ALU.mult))
            dv.link(dve.tensor_tensor(BKc[d][:, :, :, 1, :], chunks(kmod), e, ALU.mult))
            n += 1
        dve.wait_ge(S["ml_zero"], 1)
        dv.link(dve.memset(S0, 0.0))
        dve.memset(yr[0:C], 0.0).then_inc(S["rw_ready"], 1)
        dve.wait_ge(S["rw_ready"], 1)

    i64 = ident[0:C, 0:C]

    def inverse_pe(n, CT, X, XT, Y):
        def each(bank, lhs, rhs):
            for z in range(2 * H):
                ins = pe.matmul(PS[0:C, bank + z // 8, (z % 8) * C:(z % 8 + 1) * C], lhs[0:C, z, :],
                                rhs[0:C, z, :] if rhs is not None else i64, start=True, stop=True)
            return ins

        for lev in range(6):
            pe.wait_ge(S["inv_ct"], 6 * n + lev + 1)
            each(0, CT, X if lev else None).then_inc(S["inv_y"], 1)
            if lev:
                pe.wait_ge(S["inv_ye"], 5 * n + lev)
                if lev < 5:
                    each(2, XT, Y)
                each(4, Y, XT).then_inc(S["inv_z"], 1)
        pe.wait_ge(S["inv_done"], n + 1)

    def inverse_dve(n, NT, mask, CT, X, XT):
        flat = lambda b: PS[0:C, b:b + 2, :].rearrange("p b (z t) -> p (b z) t", t=C)
        for lev in range(6):
            if lev:
                dve.wait_ge(S["inv_z"], 5 * n + lev - 1) if lev > 1 else None
            shape = NT.shape
            c = CT[0:C] if len(shape) == 3 else CT[0:C].rearrange("p (d h) t -> p d h t", d=shape[1])
            dve.tensor_tensor(c, NT, mask(lev), ALU.mult).then_inc(S["inv_ct"], 1)
            if lev == 0:
                dve.wait_ge(S["inv_ct"], 6 * n + 1)
                dv.link(dve.tensor_tensor(XT[0:C], CT[0:C], over(i64, 2 * H), ALU.add))
                dve.wait_ge(S["inv_y"], 6 * n + 1)
                dv.link(dve.tensor_tensor(X[0:C], flat(0), over(i64, 2 * H), ALU.add))
            else:
                dve.wait_ge(S["inv_z"], 5 * n + lev)
                if lev < 5:
                    dve.tensor_tensor(X[0:C], X[0:C], flat(2), ALU.add)
                ins = dve.tensor_tensor(XT[0:C], XT[0:C], flat(4), ALU.add)
                if lev < 5:
                    dv.link(ins)
                else:
                    ins.then_inc(S["inv_done"], 1)
                    dve.wait_ge(S["inv_done"], n + 1)

    def inverse_act(n, Y):
        for lev in range(1, 6):
            act.wait_ge(S["inv_y"], 6 * n + lev + 1)
            act.activation(Y[0:C].rearrange("p (b z) t -> p b (z t)", b=2), PS[0:C, 0:2, :], ACT.Copy)\
               .then_inc(S["inv_ye"], 1)

    def rw_step_pe(i):
        pe.wait_ge(S["rw_step"], i) if i else pe.wait_ge(S["rw_ready"], 1)
        cs = [ORDER[d][i] for d in range(2)]
        lat = i >= 4
        for d in range(2):
            for h in range(H):
                c = cs[d]
                lhs = BK[half(h), d, h // 2, c * P:(c + 1) * P]
                n = P if lat else C
                ins = pe.matmul(PS[:, 2 * d + h % 2, (h // 2) * P:(h // 2) * P + n], lhs,
                                KR[half(h), d, h // 2, c * P:c * P + n], start=True, stop=True)
        ins.then_inc(S["rw_sc"], 1)
        for d in range(2):
            for p in range(4):
                pe.transpose(PS[:, 4 + d, p * P:(p + 1) * P], BK[:, d, p, cs[d] * P:(cs[d] + 1) * P], ident)
                ins = pe.transpose(PS[:, 6 + d, p * P:(p + 1) * P], rv[:, p, cs[d] * C:cs[d] * C + P], ident)
        ins.then_inc(S["rw_tr"], 1)
        pe.wait_ge(S["rw_m"], i + 1)
        pe.wait_ge(S["rw_bk"], i + 1)
        for d in range(2):
            for p in range(4):
                o = PS[0:C, 6 + d, p * P:(p + 1) * P]
                pe.matmul(o, KR[:, d, p, cs[d] * P:cs[d] * P + C], S0[:, d, p, :], start=True, stop=False,
                          skip_group_check=True)
                for h in (2 * p, 2 * p + 1):
                    ins = pe.matmul(PS[0:C, 6 + d, h * C:(h + 1) * C], Msc[C:P, d * H + h, 0:C],
                                    UV[C:P, d, h * C:(h + 1) * C], start=False, stop=h % 2 == 1, skip_group_check=True)
        ins.then_inc(S["rw_g"], 1)
        inverse_pe(i, CTm, Xm, XTm, Ym)
        pe.wait_ge(S["rw_ge"], i + 1)
        for d in range(2):
            for h in range(H):
                ins = pe.matmul(PS[0:C, d, h * C:(h + 1) * C], XTm[0:C, d * H + h, :], Gs[0:C, d, h * C:(h + 1) * C],
                                start=True, stop=True)
        ins.then_inc(S["rw_u"], 1)
        pe.wait_ge(S["rw_ue"], i + 1)
        for d in range(2):
            if lat:
                for p in range(4):
                    pe.matmul(PS[0:C, 2 + d, p * P:(p + 1) * P], KR[:, d, p, cs[d] * P + C:(cs[d] + 1) * P],
                              S0[:, d, p, :], start=True, stop=False, skip_group_check=True)
                    for h in (2 * p, 2 * p + 1):
                        ins = pe.matmul(PS[0:C, 2 + d, h * C:(h + 1) * C], Msc[:, d * H + h, C:P],
                                        UV[:, d, h * C:(h + 1) * C], start=False, stop=h % 2 == 1,
                                        skip_group_check=True)
            if i < NCH - 1:
                for p in range(4):
                    ins = pe.matmul(PS[:, 4 + d, p * P:(p + 1) * P], BKt[:, d, p * P:(p + 1) * P],
                                    UV[:, d, p * P:(p + 1) * P], start=True, stop=True)
        ins.then_inc(S["rw_y"], 1)

    def rw_step_dve(i):
        cs = [ORDER[d][i] for d in range(2)]
        lat = i >= 4
        n = P if lat else C
        dve.wait_ge(S["rw_sc"], i + 1)
        for d in range(2):
            mask = const("rwmask")[:, d * P:d * P + n]
            for b in range(2):
                ins = dve.tensor_tensor(Msc[:, d * H + b:(d + 1) * H:2, 0:n],
                                        PS[:, 2 * d + b, :].rearrange("p (h j) -> p h j", j=P)[:, :, 0:n],
                                        over(mask, 4), ALU.mult)
        ins.then_inc(S["rw_m"], 1)
        dve.wait_ge(S["rw_m"], i + 1)
        NT = Msc[0:C, :, 0:C].rearrange("p (d h) t -> p d h t", d=2)

        def mask(lev):
            a = const("level", C)[:, lev * P:(lev + 1) * P].rearrange("p (d t) -> p d t", d=2)
            return over(a, H, 2)

        inverse_dve(i, NT, mask, CTm, Xm, XTm)
        dve.wait_ge(S["rw_y"], i + 1)
        if lat:
            for d in range(2):
                dst = yr[0:C, cs[d] - 4, :]
                dv.link(dve.tensor_tensor(dst, dst, PS[0:C, 2 + d, :], ALU.add))
        if i < NCH - 1:
            b8 = over(const("blk1"), 8)
            dv.link(dve.tensor_tensor(st.rearrange("p d q n -> p (d q) n"),
                                      PS[:, 4:6, :].rearrange("p b (q n) -> p (b q) n", n=P), b8, ALU.mult))
            dv.link(dve.tensor_tensor(S0, S0, st, ALU.add))
            for d in range(2):
                ins = dve.tensor_tensor(S0[:, d], S0[:, d], along(eC[:, d, :, cs[d]], P), ALU.mult)
            ins.then_inc(S["rw_step"], 1)
            dve.wait_ge(S["rw_step"], i + 1)

    def rw_step_act(i):
        act.wait_ge(S["rw_tr"], i + 1)
        act.activation(BKt, PS[:, 4:6, :], ACT.Copy)
        act.activation(UV[C:P], PS[C:P, 6:8, :], ACT.Copy).then_inc(S["rw_bk"], 1)
        act.wait_ge(S["rw_g"], i + 1)
        act.activation(Gs[0:C], PS[0:C, 6:8, :], ACT.Copy).then_inc(S["rw_ge"], 1)
        inverse_act(i, Ym)
        act.wait_ge(S["rw_u"], i + 1)
        act.activation(UV[0:C], PS[0:C, 0:2, :], ACT.Copy).then_inc(S["rw_ue"], 1)

    def rw_out_dve():
        dve.wait_ge(S["hn_turned"], 2)
        for p in range(4):
            dv.link(dve.tensor_scalar(mixT[:, 4 + p, :], PS[:, p, 0:N], col("r_norm_w", p), col("r_norm_b", p), ALU.mult,
                                      ALU.add))
            dv.link(dve.tensor_tensor(mixT[:, 4 + p, :], mixT[:, 4 + p, :], prod[:, p, :], ALU.add))
            ins = dve.tensor_tensor(mixT[:, 4 + p, :], mixT[:, 4 + p, :], gT[:, p, :], ALU.mult)
        ins.then_inc(S["mixed"], 1)
        dve.wait_ge(S["mixed"], 1)

    def out_sp(name, w):
        for j in range(2):
            load(U[name] + j, ktiles(w, 512 * j, 512))

    def out_pe(name, src):
        for m in range(KT):
            if m % 4 == 0:
                arrived(U[name] + m // 4)
            w = unit(U[name] + m // 4, KT, 512)
            product(tile_begin(name, m)[:, 0:N], [(w[:, k, (m % 4) * P:(m % 4 + 1) * P], src[:, k, :]) for k in range(KT)])\
                .then_inc(S["tile_full"], 1)

    residuals = [0]

    def residual(m, o, gate, alpha):
        t = tmp[:, m % 2, :]
        dv.link(dve.tensor_scalar(t, o, gate, None, ALU.mult))
        return dve.scalar_tensor_tensor(out=xT[:, m, :], in0=xT[:, m, :], scalar=alpha, in1=t, op0=ALU.mult, op1=ALU.add)

    def out_dve(name, gate, alpha):
        for m in range(KT):
            residual(m, tile_full(dve, name, m)[:, 0:N], gate(m), alpha).then_inc(S["emptied_dve"], 1)
        all_emptied(dve, name)

    SPLIT = {"moe1": [4], "ffn": [4, 4, 3], "moe2": [4, 4, 3]}
    COUNT = {"moe1": N_EXP1, "ffn": 2, "moe2": N_EXP2}
    FFN_F = D_FF // 2
    ex_tiles, n = {}, 0
    for name in SPLIT:
        ex_tiles[name] = n
        n += COUNT[name] * sum(SPLIT[name])

    moe = Space(work, ABOVE, work_len)
    wbc = moe.take(N_EXP1, N)
    hid = moe.take(11, N)
    sil = moe.take(4, N)
    diagw = moe.take(2, 4, P)
    rt_pos = moe.pos

    def ex_units(name):
        out, t0 = [], 0
        for n in SPLIT[name]:
            out += [("gate", t0, n), ("up", t0, n)]
            t0 += n
        t0 = 0
        for n in SPLIT[name]:
            out.append(("down", t0, n))
            t0 += n
        return out

    def ex_src(name, what, t0, n, e):
        if name == "moe1":
            w = {"gate": A["ex_gate"], "up": A["ex_up"], "down": A["ex_down"]}[what][0]
            w = w[bass.ds(e, 1)].rearrange("a k n -> (a k) n")
            c0 = 0
        elif name == "ffn":
            w = (A["ffn_w_down_2"] if what == "down" else A["ffn_w_gate_up_2"])[0]
            if what == "down":
                w = w[e * FFN_F:(e + 1) * FFN_F, :]
            c0 = e * FFN_F + (D_FF if what == "up" else 0)
        else:
            w = (A["moe_w_down_2"] if what == "down" else A["moe_w_gate_up_2"])[0]
            w = w[bass.ds(e, 1)].rearrange("a k n -> (a k) n")
            c0 = F_EXP2 if what == "up" else 0
        if what == "down":
            return w[t0 * P:(t0 + n) * P, :].rearrange("(k p) n -> p k n", p=P)
        return ktiles(w, c0 + t0 * P, n * P)

    def ex_sp(name):
        per = ex_units(name)
        body = [(e, j) for e in range(2) for j in range(len(per))]
        FT = sum(SPLIT[name])
        n_down = len(SPLIT[name])

        def released_in(b, i):
            e, j = body[b]
            what, t0, n = per[j]
            if what == "down":
                at = downs_before[name] + e * n_down + (j - 2 * n_down) + 1
                sp.wait_ge(S["weights_used"], i * (2 * n_down) + at)
            else:
                sp.wait_ge(S["gate_up"], i * (2 * FT) + (ex_tiles[name] + e * FT + t0 + n))

        def put(b, i, e0):
            e, j = body[b]
            what, t0, n = per[j]
            src = ex_src(name, what, t0, n, e0 + e)
            sp.dma_start(unit(U[name] + b, src.shape[1], src.shape[2]), src)\
                .then_inc(landed[(U[name] + b) % SLOTS], 16)

        for b in range(len(body)):
            if b < SLOTS:
                released(U[name] + b - SLOTS)
            else:
                released_in(b - SLOTS, 0)
            put(b, 0, 0)
        if COUNT[name] > 2:
            with sp.Fori(0, COUNT[name] // 2 - 1) as i:
                for b in range(len(body)):
                    back = b - SLOTS
                    if back < 0:
                        released_in(back + len(body), i)
                    else:
                        released_in(back, i + 1)
                    put(b, i, i * 2 + 2)

    def ex_pe(name):
        FT = sum(SPLIT[name])
        per = ex_units(name)
        rounds = 2 * len(per) // SLOTS
        for b in range(4):
            pe.matmul(PS[:, b, :], zeros, consts[:, 0:512], start=True, stop=False, skip_group_check=True)
        with pe.Fori(0, COUNT[name] // 2) as i:
            for e in range(2):
                base = ex_tiles[name] + e * FT
                u = U[name] + e * len(per)
                for n in SPLIT[name]:
                    t0 = per[u - U[name] - e * len(per)][1]
                    arrived(u, i * rounds)
                    arrived(u + 1, i * rounds)
                    wg, wu = unit(u, KT, n * P), unit(u + 1, KT, n * P)
                    for t in range(n):
                        f = t0 + t
                        if f >= 4:
                            pe.wait_ge(S["hidden"], i * (2 * FT) + (base + f - 3))
                        for j, w in enumerate((wg, wu)):
                            ins = product(PS[:, 4 + f % 4, j * N:(j + 1) * N],
                                          [(w[:, k, t * P:(t + 1) * P], hT[:, k, :]) for k in range(KT)])
                        ins.then_inc(S["gate_up"], 1)
                    u += 2
                f = 0
                for n in SPLIT[name]:
                    arrived(u, i * rounds)
                    wd = unit(u, n, D)
                    for t in range(n):
                        pe.wait_ge(S["hidden"], i * (2 * FT) + (base + f + 1))
                        for m in range(KT):
                            ins = pe.matmul(PS[:, m // 2, (m % 2) * N:(m % 2 + 1) * N], wd[:, t, m * P:(m + 1) * P],
                                            hid[:, f, :], start=False, stop=False, skip_group_check=True)
                        f += 1
                    ins.then_inc(S["weights_used"], 1)
                    u += 1
        for b in range(4):
            ins = pe.matmul(PS[:, b, :], zeros, consts[:, 0:512], start=False, stop=True, skip_group_check=True)
        ins.then_inc(S["experts"], 1)

    def ex_act(name):
        FT = sum(SPLIT[name])
        with act.Fori(0, COUNT[name] // 2) as i:
            for e in range(2):
                for f in range(FT):
                    act.wait_ge(S["gate_up"], i * (2 * FT) + (ex_tiles[name] + e * FT + f + 1))
                    act.activation(sil[:, f % 4, :], PS[:, 4 + f % 4, 0:N], ACT.Silu).then_inc(S["silu"], 1)

    def ex_dve(name, weighted):
        FT = sum(SPLIT[name])
        with dve.Fori(0, COUNT[name] // 2) as i:
            for e in range(2):
                for f in range(FT):
                    at = ex_tiles[name] + e * FT + f + 1
                    dve.wait_ge(S["silu"], i * (2 * FT) + at)
                    up = PS[:, 4 + f % 4, N:2 * N]
                    if weighted:
                        dve.tensor_tensor(sil[:, f % 4, :], sil[:, f % 4, :], up, ALU.mult).then_inc(S["silu_up"], 1)
                        unweighted = ex_tiles["moe2"] - ex_tiles["ffn"] if name == "moe2" else 0
                        dve.wait_ge(S["silu_up"], i * (2 * FT) + (at - unweighted))
                        w = wbc[:, bass.ds(i * 2 + e, 1), :].rearrange("p a n -> p (a n)")
                        ins = dve.tensor_tensor(hid[:, f, :], sil[:, f % 4, :], w, ALU.mult)
                    else:
                        ins = dve.tensor_tensor(hid[:, f, :], sil[:, f % 4, :], up, ALU.mult)
                    ins.then_inc(S["hidden"], 1)

    ex_names = list(SPLIT)

    def ex_resid_dve(name, gate, alpha):
        dve.wait_ge(S["experts"], ex_names.index(name) + 1)
        for m in range(KT):
            ins = residual(m, PS[:, m // 2, (m % 2) * N:(m % 2 + 1) * N], gate(m), alpha)
            if m < KT - 1:
                dv.link(ins)
        ins.then_inc(S["resid"], 1)

    def resid_wait(eng, n):
        eng.wait_ge(S["resid"], n)

    wb_rounds = [0, 0, 0]

    def route_pe(w, cols_n, n_norm, n_exp):
        pe.wait_ge(S["norm_done"], n_norm + 1)
        for tt in range(2):
            ins = product(PS[:, 4, tt * 64:tt * 64 + cols_n], [(hT[:, k, tt * P:(tt + 1) * P], w[:, k, :]) for k in range(KT)])
        ins.then_inc(S["logits"], 1)
        for r in range(2 * n_exp // 4):
            g = wb_rounds[1]
            pe.wait_ge(S["wb_diag"], g + 1)
            if g >= 2:
                pe.wait_ge(S["wb_evac"], g - 1)
            pe.matmul(PS[:, 6 + g % 2, :], ones, diagw[:, g % 2].rearrange("p e t -> p (e t)"), start=True, stop=True)\
                .then_inc(S["wb_sum"], 1)
            wb_rounds[1] += 1
        pe.wait_ge(S["wb_evac"], wb_rounds[1])

    def route_act(n_exp):
        for r in range(2 * n_exp // 4):
            g = wb_rounds[2]
            e4, tt = r // 2, r % 2
            act.wait_ge(S["wb_sum"], g + 1)
            act.activation(wbc[:, 4 * e4:4 * e4 + 4, tt * P:(tt + 1) * P],
                           PS[:, 6 + g % 2, :].rearrange("p (e t) -> p e t", t=P), ACT.Copy).then_inc(S["wb_evac"], 1)
            wb_rounds[2] += 1

    def spread_dve(W, n_exp):
        for r in range(2 * n_exp // 4):
            g = wb_rounds[0]
            e4, tt = r // 2, r % 2
            if g >= 2:
                dve.wait_ge(S["wb_sum"], g - 1)
            dve.tensor_tensor(diagw[:, g % 2], over(ident, 4), along(W[:, tt, 4 * e4:4 * e4 + 4], P), ALU.mult)\
                .then_inc(S["wb_diag"], 1)
            wb_rounds[0] += 1
        dve.wait_ge(S["wb_evac"], wb_rounds[0])

    def top2_dve(n, le, W8, sp_, scale):
        v8, i8, i2, e1, w1, w2 = sp_
        iota = const("iota8")
        for tt in range(2):
            dv.link(dve.max(v8[:, tt, :], le[:, tt, :]))
            dv.link(dve.max_index(i8[:, tt, :], v8[:, tt, :], le[:, tt, :]))
        dv.link(dve.tensor_copy(i2, i8[:, :, 0:2]))
        dve.tensor_tensor(e1, v8[:, :, 1], v8[:, :, 0], ALU.subtract).then_inc(S["top_diff"], 1)
        dve.wait_ge(S["top_exp"], n + 1)
        dv.link(dve.tensor_scalar(w2, e1, 1.0, None, ALU.add))
        dv.link(dve.reciprocal(w1, w2))
        if scale is not None:
            dv.link(dve.tensor_tensor(w1, w1, scale, ALU.mult))
        dv.link(dve.tensor_tensor(w2, e1, w1, ALU.mult))
        for tt in range(2):
            dv.link(dve.tensor_scalar(W8[:, tt, :], iota, i2[:, tt, 0:1], w1[:, tt:tt + 1], ALU.is_equal, ALU.mult))
            dv.link(dve.tensor_scalar(v8[:, tt, :], iota, i2[:, tt, 1:2], w2[:, tt:tt + 1], ALU.is_equal, ALU.mult))
        dv.link(dve.tensor_tensor(W8, W8, v8, ALU.add))

    def top2_act(n, e1):
        act.wait_ge(S["top_diff"], n + 1)
        act.activation(e1, e1, ACT.Exp).then_inc(S["top_exp"], 1)

    rt = Space(work, rt_pos, work_len)
    lg36 = rt.take(2, 36)
    gpad, gv8, le8, W8r = rt.take(2, 8), rt.take(2, 8), rt.take(2, 8), rt.take(2, 8)
    gi8 = rt.take(2, 8).bitcast(U32)
    v8r, i8r, i2r = rt.take(2, 8), rt.take(2, 8).bitcast(U32), rt.take(2, 2)
    gidx, ge, gsum, ptop, e1r, w1r, w2r = rt.take(2), rt.take(2, 4), rt.take(2), rt.take(2), rt.take(2), rt.take(2), rt.take(2)
    goh, lsel, Wall = rt.take(2, 4), rt.take(2, 4, 8), rt.take(2, N_EXP1)
    top_tiles = (v8r, i8r, i2r, e1r, w1r, w2r)

    def route1_dve():
        dve.wait_ge(S["logits"], 1)
        dv.link(dve.tensor_tensor(lg36, PS[:, 4, 0:128].rearrange("p (t n) -> p t n", t=2)[:, :, 0:36], over(rt_bias, 2),
                                  ALU.add))
        dv.link(dve.memset(gpad, -3e38))
        dv.link(dve.tensor_copy(gpad[:, :, 0:4], lg36[:, :, 0:4]))
        for tt in range(2):
            dv.link(dve.max(gv8[:, tt, :], gpad[:, tt, :]))
            dv.link(dve.max_index(gi8[:, tt, :], gv8[:, tt, :], gpad[:, tt, :]))
        dv.link(dve.tensor_copy(gidx, gi8[:, :, 0]))
        dve.tensor_tensor(ge, lg36[:, :, 0:4], along(gv8[:, :, 0], 4), ALU.subtract).then_inc(S["rt_diff"], 1)
        dve.wait_ge(S["rt_exp"], 1)
        dv.link(dve.tensor_reduce(gsum, ge, AX.X, ALU.add))
        dv.link(dve.reciprocal(ptop, gsum))
        dv.link(dve.tensor_tensor(goh, over(const("iota8")[:, 0:4], 2), along(gidx, 4), ALU.is_equal))
        dv.link(dve.tensor_tensor(lsel, lg36[:, :, 4:36].rearrange("p t (g e) -> p t g e", g=4), along(goh, 8), ALU.mult))
        dv.link(dve.tensor_reduce(le8, lsel.rearrange("p t g e -> p t e g"), AX.X, ALU.add))
        top2_dve(0, le8, W8r, top_tiles, ptop)
        dv.link(dve.tensor_tensor(Wall.rearrange("p t (g e) -> p t g e", g=4), along(goh, 8), over(W8r, 4, 2), ALU.mult))
        spread_dve(Wall, N_EXP1)

    def route1_act():
        act.wait_ge(S["rt_diff"], 1)
        act.activation(ge, ge, ACT.Exp).then_inc(S["rt_exp"], 1)
        top2_act(0, e1r)
        route_act(N_EXP1)

    def route2_dve():
        dve.wait_ge(S["logits"], 2)
        dv.link(dve.tensor_copy(le8, PS[:, 4, 0:128].rearrange("p (t n) -> p t n", t=2)[:, :, 0:8]))
        top2_dve(1, le8, W8r, top_tiles, None)
        spread_dve(W8r, N_EXP2)

    def route2_act():
        top2_act(1, e1r)
        route_act(N_EXP2)

    mla = Space(work, ABOVE, work_len)
    qlat, kvlat = mla.take(4, N), mla.take(2, N)
    qn, kvn = mla.take(4, N), mla.take(2, N)
    kr = mla.take(N)
    cosF, sinF = mla.take(N), mla.take(N)
    pos = mla.take(N).bitcast(I32)
    qh, kf = mla.take(HM, N), mla.take(HM, N)
    vtk = mla.take(2, HM * VH)
    mx, nmx, esum, rsum = (mla.take(2, 2) for _ in range(4))
    lat_free = work[:, ABOVE:ABOVE + 4 * 384].rearrange("p (a b n) -> p a b n", a=2, b=2)
    sS, pT = lat_free[:, 0], lat_free[:, 1]
    ang, turns, cang, wrap = (kf[:, j, :] for j in range(4))
    oT = hT
    RP = slice(64, 64 + ROPE)
    QKSCALE = QK ** -0.5
    MLA_IN = Q_LORA + KV_LORA + ROPE

    def mla_sp():
        u = U["mla"]
        load(u, ktiles(A["mla_w_in_2"][0], 0, 512))
        load(u + 1, ktiles(A["mla_w_in_2"][0], 512, MLA_IN - 512))
        for j in range(2):
            load(u + 2 + j, ktiles(A["mla_w_qb_2"][0], 768 * j, 768))
        load(u + 4, ktiles(A["mla_w_kvb_2"][0], 0, 2048))

    def mla_pe():
        pe.wait_ge(S["norm_done"], 6)
        u = U["mla"]
        w0, w1 = unit(u, KT, 512), unit(u + 1, KT, MLA_IN - 512)
        arrived(u)
        for i in range(7):
            if i == 4:
                arrived(u + 1)
            w, c0 = (w0, i * P) if i < 4 else (w1, (i - 4) * P)
            rows_, m = (slice(0, P), P) if i < 6 else (RP, ROPE)
            product(tile_begin("mla", i)[rows_, 0:N], [(w[:, k, c0:c0 + m], hT[:, k, :]) for k in range(KT)])\
                .then_inc(S["tile_full"], 1)
        norm_pe(6, qlat, 4, False, None)
        norm_pe(7, kvlat, 2, False, None)
        rot = const("rot")[RP, RP]
        o = tile_begin("mla", 7)
        pe.wait_ge(S["emptied_act"], tile_owner[first_tile["mla"] + 6][1])
        product(o[RP, 0:N], [(rot, kr[RP, :])]).then_inc(S["tile_full"], 1)
        for h in range(HM):
            if h % 8 == 0:
                arrived(u + 2 + h // 8)
            w = unit(u + 2 + h // 8, 4, 768)
            pe.wait_ge(S["norm_done"], 7)
            c0 = (h % 8) * QK
            product(tile_begin("q", h)[0:QK, 0:N], [(w[:, k, c0:c0 + QK], qn[:, k, :]) for k in range(4)])\
                .then_inc(S["tile_full"], 1)
        for h in range(HM):
            o = tile_begin("rot", h)
            pe.wait_ge(S["emptied_act"], tile_owner[first_tile["q"] + h][1])
            product(o[RP, 0:N], [(rot, qh[RP, h, :])]).then_inc(S["tile_full"], 1)
        arrived(u + 4)
        pe.wait_ge(S["norm_done"], 8)
        w = unit(u + 4, 2, 2048)
        for h in range(HM):
            product(tile_begin("kv", h)[0:64, 0:N], [(w[:, k, h * P:h * P + 64], kvn[:, k, :]) for k in range(2)])\
                .then_inc(S["tile_full"], 1)
        for j in range(4):
            tt, half_ = j // 2, j % 2
            wv = w.rearrange("p k (h c) -> p k h c", c=P)[:, :, half_ * 8:half_ * 8 + 8, 64:P]
            product(tile_begin("kv", HM + j), [(kvn[:, k, tt * P:(tt + 1) * P], wv[:, k]) for k in range(2)])\
                .then_inc(S["tile_full"], 1)
        all_emptied(pe, "kv")
        pe.wait_ge(S["rope_done"], 1)
        for i in range(HM + 2):
            if i < HM:
                at_scores_pe(i)
            if 1 <= i <= HM:
                at_turn_pe(i - 1)
            if i >= 2:
                at_out_pe(i - 2)

    PARTS = ((0, P, 0), (P, 3 * P, 1))

    def at_scores_pe(h):
        if h >= 2:
            pe.wait_ge(S["at_masked"], h - 1)
        for c0, c1, qt in PARTS:
            ins = pe.matmul(PS[:, h % 2, c0:c1], qh[0:QK, h, qt * P:(qt + 1) * P], kf[0:QK, h, 0:c1 - c0], start=True,
                            stop=True)
        ins.then_inc(S["at_scores"], 1)

    def at_turn_pe(h):
        pe.wait_ge(S["at_weights"], h + 1)
        if h >= 2:
            pe.wait_ge(S["at_turn_evac"], h - 1)
        for j in range(3):
            ins = pe.transpose(PS[:, 2 + h % 2, j * P:(j + 1) * P], sS[:, h % 2, j * P:(j + 1) * P], ident)
        ins.then_inc(S["at_turned"], 1)

    def at_out_pe(h):
        pe.wait_ge(S["at_turn_evac"], h + 1)
        if h >= 2:
            pe.wait_ge(S["at_oe"], h - 1)
        o = PS[half(h), 4 + h % 2, 0:N]
        v = vtk[:, :, h * VH:(h + 1) * VH]
        pe.matmul(o, v[:, 0, :], pT[:, h % 2, 0:2 * P], start=True, stop=False, skip_group_check=True)
        pe.matmul(o[:, P:2 * P], v[:, 1, :], pT[:, h % 2, 2 * P:3 * P], start=False, stop=True, skip_group_check=True)\
            .then_inc(S["at_out"], 1)

    def mla_act():
        act.dma_start(pos[RP, :], A["positions_2"].broadcast_to([ROPE, N])).then_inc(S["positions"], 16)

        def evac(name, i, dst, src):
            act.activation(dst, src, ACT.Copy).then_inc(S["emptied_act"], 1)

        for i in range(7):
            o = tile_full(act, "mla", i)
            if i < 6:
                evac("mla", i, qlat[:, i, :] if i < 4 else kvlat[:, i - 4, :], o[:, 0:N])
            else:
                evac("mla", i, kr[RP, :], o[RP, 0:N])
        act.wait_ge(S["rope_args"], 1)
        act.activation(cosF[RP, :], cang[RP, :], ACT.Sin)
        act.activation(sinF[RP, :], ang[RP, :], ACT.Sin).then_inc(S["rope_tables"], 1)
        norm_act(6)
        norm_act(7)
        for h in range(HM):
            evac("q", h, qh[0:QK, h, :], tile_full(act, "q", h)[0:QK, 0:N])
        for h in range(HM):
            evac("kv", h, kf[0:64, h, :], tile_full(act, "kv", h)[0:64, 0:N])
        for j in range(4):
            evac("kv", HM + j, vtk[:, j // 2, (j % 2) * 512:(j % 2) * 512 + 512], tile_full(act, "kv", HM + j))
        for i in range(HM + 2):
            if i < HM:
                h = i
                act.wait_ge(S["at_max"], h + 1)
                for c0, c1, qt in PARTS:
                    s = sS[:, h % 2, c0:c1]
                    ins = act.activation(s, s, ACT.Exp, scale=QKSCALE, bias=nmx[:, h % 2, qt:qt + 1],
                                         accum_out=esum[:, h % 2, qt:qt + 1])
                ins.then_inc(S["at_exp"], 1)
            if 1 <= i <= HM:
                h = i - 1
                act.wait_ge(S["at_turned"], h + 1)
                if h >= 2:
                    act.wait_ge(S["at_out"], h - 1)
                act.activation(pT[:, h % 2, :], PS[:, 2 + h % 2, 0:384], ACT.Copy).then_inc(S["at_turn_evac"], 1)
            if i >= 2:
                h = i - 2
                act.wait_ge(S["at_out"], h + 1)
                act.activation(oT[half(h), h // 2, :], PS[half(h), 4 + h % 2, 0:N], ACT.Copy).then_inc(S["at_oe"], 1)

    def mla_dve():
        dve.wait_ge(S["positions"], 16)
        two_pi = 2 * math.pi
        c1, c2 = 6.28125, float(np.float32(0.0019340515136718750))
        c3 = two_pi - c1 - c2
        magic = 1.5 * 2 ** 23
        pi_in = 3.1415925
        a, tn, ca, wr = ang[RP, :], turns[RP, :], cang[RP, :], wrap[RP, :]
        dv.link(dve.tensor_copy(a, pos[RP, :]))
        dv.link(dve.tensor_scalar(a, a, const("invfreq")[RP, :], None, ALU.mult))
        dv.link(dve.tensor_scalar(tn, a, 1.0 / two_pi, magic, ALU.mult, ALU.add))
        dv.link(dve.tensor_scalar(tn, tn, magic, None, ALU.subtract))
        for c in (c1, c2, c3):
            dv.link(dve.scalar_tensor_tensor(out=a, in0=tn, scalar=-c, in1=a, op0=ALU.mult, op1=ALU.add))
        dv.link(dve.tensor_scalar(ca, a, math.pi / 2, None, ALU.add))
        dv.link(dve.tensor_scalar(wr, ca, math.pi, -two_pi, ALU.is_gt, ALU.mult))
        dv.link(dve.tensor_tensor(ca, ca, wr, ALU.add))
        dv.link(dve.tensor_scalar(ca, ca, pi_in, -pi_in, ALU.min, ALU.max))
        dve.tensor_scalar(a, a, pi_in, -pi_in, ALU.min, ALU.max).then_inc(S["rope_args"], 1)
        dve.wait_ge(S["emptied_act"], tile_owner[first_tile["mla"] + 3][1])
        norm_dve(6, qlat, 4, False, qn, lambda k: col("mla_q_norm_2", k), None, EPS)
        dve.wait_ge(S["emptied_act"], tile_owner[first_tile["mla"] + 5][1])
        norm_dve(7, kvlat, 2, False, kvn, lambda k: col("mla_kv_norm_2", k), None, EPS)
        dve.wait_ge(S["rope_tables"], 1)
        o = tile_full(dve, "mla", 7)
        dve.wait_ge(S["emptied_act"], tile_owner[first_tile["mla"] + 6][1])
        dv.link(dve.tensor_tensor(tmp[RP, 0, :], kr[RP, :], cosF[RP, :], ALU.mult))
        dve.tensor_tensor(tmp[RP, 1, :], o[RP, 0:N], sinF[RP, :], ALU.mult).then_inc(S["emptied_dve"], 1)
        dve.wait_ge(S["emptied_dve"], tile_owner[first_tile["mla"] + 7][1])
        dv.link(dve.tensor_tensor(kf[RP, :, :], over(tmp[RP, 0, :], HM), over(tmp[RP, 1, :], HM), ALU.add))
        turned = [xc, sq]
        for h in range(HM):
            o = tile_full(dve, "rot", h)
            dve.tensor_tensor(turned[h // 8][RP, h % 8, :], o[RP, 0:N], sinF[RP, :], ALU.mult).then_inc(S["emptied_dve"], 1)
        dve.wait_ge(S["emptied_dve"], tile_owner[first_tile["rot"] + HM - 1][1])
        dve.wait_ge(S["emptied_act"], tile_owner[first_tile["q"] + HM - 1][1])
        dv.link(dve.tensor_tensor(qh[RP, :, :], qh[RP, :, :], over(cosF[RP, :], HM), ALU.mult))
        for j in range(2):
            q8 = qh[RP, 8 * j:8 * j + 8, :]
            ins = dve.tensor_tensor(q8, q8, turned[j][RP, :, :], ALU.add)
            if j == 0:
                dv.link(ins)
        ins.then_inc(S["rope_done"], 1)
        for i in range(HM + 1):
            if i < HM:
                h = i
                dve.wait_ge(S["at_scores"], h + 1)
                if h >= 2:
                    dve.wait_ge(S["at_turned"], h - 1)
                s = sS[:, h % 2, :]
                dve.tensor_tensor(s, PS[:, h % 2, 0:384], const("causal"), ALU.add).then_inc(S["at_masked"], 1)
                dve.wait_ge(S["at_masked"], h + 1)
                for c0, c1, qt in PARTS:
                    ins = dve.tensor_reduce(mx[:, h % 2, qt:qt + 1], s[:, c0:c1], AX.X, ALU.max)
                dv.link(ins)
                dve.tensor_scalar(nmx[:, h % 2, :], mx[:, h % 2, :], -QKSCALE, None, ALU.mult).then_inc(S["at_max"], 1)
            if i >= 1:
                h = i - 1
                dve.wait_ge(S["at_exp"], h + 1)
                dv.link(dve.reciprocal(rsum[:, h % 2, :], esum[:, h % 2, :]))
                for c0, c1, qt in PARTS:
                    s = sS[:, h % 2, c0:c1]
                    ins = dve.tensor_scalar(s, s, rsum[:, h % 2, qt:qt + 1], None, ALU.mult)
                ins.then_inc(S["at_weights"], 1)

    gd = Space(work, ABOVE, work_len)
    qkv = gd.take(3 * H, N)
    gq, gk, gv = (qkv[:, j * H:(j + 1) * H, :] for j in range(3))
    zs = gd.take(H, N)
    Sg = gd.take(H, P)
    decU = gd.take(2 * H, C)
    CTg = decU
    Ug, ksg = gd.take(H, P), gd.take(H, P)
    beta, nbeta, ga, gz, gl_, gc = (gd.take(N) for _ in range(6))
    glast, eglast, expA = gd.take(4), gd.take(4), gd.take(1)
    egc, wsr = ga, gz
    gdiag, eglb = gd.take(4, H), gd.take(4, H)
    gtk = gd.take(4, 4, H)
    oms, ostd = gd.take(H), gd.take(H)

    def halves(buf):
        a = buf.rearrange("p k n -> p (k n)")
        return a[:, 0:1024], a[:, 1024:2048]

    (XTg, Xg), (Yg, attn), (NTg, og) = halves(xc), halves(sq), halves(hT)
    XTg, Xg, Yg, attn, NTg = (t.rearrange("p (z t) -> p z t", t=C) for t in (XTg, Xg, Yg, attn, NTg))
    og = og.rearrange("p (h e) -> p h e", h=H)
    osq = NTg.rearrange("p z t -> p (z t)").rearrange("p (h e) -> p h e", h=H)
    g8 = slice(0, H)

    def heads2(bank, parts=C):
        return PS[0:parts, bank:bank + 2, :].rearrange("p b (h e) -> p (b h) e", e=P)

    def problems(bank):
        return PS[0:C, bank:bank + 2, :].rearrange("p b (z t) -> p (b z) t", t=C)

    def gdn_sp():
        for j in range(8):
            load(U["gdn_in"] + j, ktiles(A["gdn_w_in_2"][0], 512 * j, 512))

    def gdn_pe():
        pe.wait_ge(S["norm_done"], 10)
        for i in range(32):
            if i % 4 == 0:
                arrived(U["gdn_in"] + i // 4)
            w = unit(U["gdn_in"] + i // 4, KT, 512)
            product(tile_begin("gdn_in", i)[:, 0:N], [(w[:, k, (i % 4) * P:(i % 4 + 1) * P], hT[:, k, :]) for k in range(KT)])\
                .then_inc(S["tile_full"], 1)
        o = tile_begin("gdn_in", 32)
        for j in range(2):
            ins = product(o[g8, j * N:(j + 1) * N], [(w_ba[:, k, j * H:(j + 1) * H], hT[:, k, :]) for k in range(KT)])
        ins.then_inc(S["tile_full"], 1)
        for j in range(8):
            if j % 4 == 0:
                pe.wait_ge(S["gd_sq"], j // 4 + 1)
            src = (sq, xc)[j // 4]
            product(tile_begin("l2", j), [(ones, src[:, 2 * (j % 4):2 * (j % 4) + 2, :])]).then_inc(S["tile_full"], 1)
        pe.wait_ge(S["gd_rows"], 1)
        for j, t in enumerate((beta, egc, wsr, gc)):
            for c in range(4):
                pe.transpose(PS[0:C, 0, (j * 4 + c) * H:(j * 4 + c + 1) * H], t[g8, c * C:(c + 1) * C], ident[g8, g8])
        pe.matmul(PS[:, 1, 0:4 * H], ones[g8, :], gdiag[g8].rearrange("p c h -> p (c h)"), start=True, stop=True)\
            .then_inc(S["gd_tok"], 1)
        all_emptied(pe, "l2")
        pe.wait_ge(S["gd_ready"], 1)
        for c in range(4):
            if c % 2 == 0:
                gd_scores_pe(c // 2)
                inverse_pe(NCH + c // 2, CTg, Xg, XTg, Yg)
            gd_chunk_pe(c)

    def gd_scores_pe(cp):
        if cp:
            pe.wait_ge(S["gd_mix"], 2 * cp)
            pe.wait_ge(S["gd_step"], 2 * cp)
        for z in range(2 * H):
            h, t0 = z // 2, (2 * cp + z % 2) * C
            at = slice((z % 8) * C, (z % 8 + 1) * C)
            kz = gk[:, h, t0:t0 + C]
            pe.matmul(PS[0:C, z // 8, at], kz, kz, start=True, stop=True)
            pe.matmul(PS[0:C, 2 + z // 8, at], kz, gq[:, h, t0:t0 + C], start=True, stop=True)
        for h in range(H):
            at = slice((h % 4) * P, (h % 4 + 1) * P)
            pick = const("pick", H)[:, h * C:(h + 1) * C]
            pe.matmul(PS[0:C, 4 + h // 4, at], pick, gc[g8, cp * P:(cp + 1) * P], start=True, stop=True)
            ins = pe.matmul(PS[0:C, 6 + h // 4, at], pick, nbeta[g8, cp * P:(cp + 1) * P], start=True, stop=True)
        ins.then_inc(S["gd_sc"], 1)

    def gd_chunk_pe(c):
        if c:
            pe.wait_ge(S["gd_step"], c)
            pe.wait_ge(S["gd_mix"], c)
        t = slice(c * C, (c + 1) * C)
        for h in range(H):
            at = slice((h % 4) * P, (h % 4 + 1) * P)
            pe.transpose(PS[0:C, h // 4, at], gv[:, h, t], ident)
            pe.transpose(PS[0:C, 2 + h // 4, at], gk[:, h, t], ident)
            pe.matmul(PS[0:C, 4 + h // 4, at], gk[:, h, t], Sg[:, h, :], start=True, stop=True)
            ins = pe.matmul(PS[0:C, 6 + h // 4, at], gq[:, h, t], Sg[:, h, :], start=True, stop=True)
        ins.then_inc(S["gd_ks"], 1)
        pe.wait_ge(S["gd_rhs"], c + 1)
        for h in range(H):
            at = slice((h % 4) * P, (h % 4 + 1) * P)
            ins = pe.matmul(PS[0:C, h // 4, at], XTg[0:C, 2 * h + c % 2, :], Ug[0:C, h, :], start=True, stop=True)
        ins.then_inc(S["gd_u"], 1)
        pe.wait_ge(S["gd_ue"], c + 1)
        for h in range(H):
            at = slice((h % 4) * P, (h % 4 + 1) * P)
            ins = pe.matmul(PS[0:C, 2 + h // 4, at], attn[0:C, 2 * h + c % 2, :], Ug[0:C, h, :], start=True, stop=True)
            if c < 3:
                ins = pe.matmul(PS[:, 4 + h // 4, at], ksg[0:C, h, :], Ug[0:C, h, :], start=True, stop=True)
        ins.then_inc(S["gd_y"], 1)
        pe.wait_ge(S["gd_o"], c + 1)
        for h in range(H):
            ins = pe.transpose(PS[:, 6, h * C:(h + 1) * C], og[0:C, h, :], i64)
        ins.then_inc(S["gd_ot"], 1)

    def gdn_act():
        def evac(name, i, dst, src, func, **kw):
            act.activation(dst, src, func, **kw).then_inc(S["emptied_act"], 1)

        for j, t in enumerate((gq, gk, gv)):
            act.wait_ge(S["emptied_dve"], tile_owner[first_tile["gdn_in"] + 8 * j + 7][1])
            act.activation(t, t, ACT.Silu).then_inc(S["gd_silu"], 1)
        for h in range(H):
            evac("gdn_in", 24 + h, zs[:, h, :], tile_full(act, "gdn_in", 24 + h)[:, 0:N], ACT.Silu)
        o = tile_full(act, "gdn_in", 32)
        act.activation(beta[g8, :], o[g8, 0:N], ACT.Sigmoid)
        act.activation(expA[g8, :], gdn_bias[:, 0:1], ACT.Exp)
        evac("gdn_in", 32, ga[g8, :], o[g8, N:2 * N], ACT.Identity, bias=gdn_bias[:, 1:2])
        act.wait_ge(S["gd_abs"], 1)
        ac.link(act.activation(gl_[g8, :], gz[g8, :], ACT.Exp, scale=-1.0))
        act.activation(gl_[g8, :], gl_[g8, :], ACT.Ln, bias=1.0).then_inc(S["gd_l"], 1)
        act.wait_ge(S["gd_args"], 1)
        act.activation(wsr[g8, :], wsr[g8, :], ACT.Exp)
        act.activation(egc[g8, :], gc[g8, :], ACT.Exp)
        act.activation(eglast[g8, :], glast[g8, :], ACT.Exp).then_inc(S["gd_gexp"], 1)
        for j in range(8):
            dst = (sq, xc)[j // 4][:, 2 * (j % 4):2 * (j % 4) + 2, :]
            evac("l2", j, dst, tile_full(act, "l2", j).rearrange("p (h t) -> p h t", h=2), ACT.Ln, bias=EPS)
        act.wait_ge(S["emptied_act"], tile_owner[first_tile["l2"] + 7][1])
        act.activation(sq, sq, ACT.Exp, scale=-0.5, bias=-0.5 * math.log(P)).then_inc(S["gd_rs"], 1)
        act.activation(xc, xc, ACT.Exp, scale=-0.5).then_inc(S["gd_rs"], 1)
        for c in range(4):
            if c % 2 == 0:
                act.wait_ge(S["gd_e"], c // 2 + 1)
                act.activation(decU[0:C], decU[0:C], ACT.Exp).then_inc(S["gd_exp"], 1)
                inverse_act(NCH + c // 2, Yg)
            act.wait_ge(S["gd_u"], c + 1)
            act.activation(Ug[0:C], heads2(0), ACT.Copy).then_inc(S["gd_ue"], 1)
            act.wait_ge(S["gd_var"], c + 1)
            act.activation(ostd[0:C, :], oms[0:C, :], ACT.Sqrt).then_inc(S["gd_std"], 1)

    def gdn_dve():
        for i in range(24):
            o = tile_full(dve, "gdn_in", i)
            y = qkv[:, i, :]
            dv.link(dve.tensor_scalar(y, o[:, 0:N], col("gdn_conv_w_2", 3 * 24 + i), None, ALU.mult))
            for back in (1, 2, 3):
                ins = dve.scalar_tensor_tensor(out=y[:, back:], in0=o[:, 0:N - back],
                                               scalar=col("gdn_conv_w_2", (3 - back) * 24 + i), in1=y[:, back:],
                                               op0=ALU.mult, op1=ALU.add)
                if back < 3:
                    dv.link(ins)
            ins.then_inc(S["emptied_dve"], 1)
        for j, (t, s) in enumerate(((gq, sq), (gk, xc))):
            dve.wait_ge(S["gd_silu"], j + 1)
            dve.tensor_tensor(s, t, t, ALU.mult).then_inc(S["gd_sq"], 1)
        dve.wait_ge(S["emptied_act"], tile_owner[first_tile["gdn_in"] + 32][1])
        dve.scalar_tensor_tensor(out=gz[g8, :], in0=ga[g8, :], scalar=-1.0, in1=ga[g8, :], op0=ALU.mult, op1=ALU.max)\
           .then_inc(S["gd_abs"], 1)
        dve.wait_ge(S["gd_l"], 1)
        dv.link(dve.scalar_tensor_tensor(out=ga[g8, :], in0=ga[g8, :], scalar=0.0, in1=gl_[g8, :], op0=ALU.max, op1=ALU.add))
        dv.link(dve.tensor_scalar(ga[g8, :], ga[g8, :], expA[g8, :], -1.0, ALU.mult, ALU.mult))
        dv.link(dve.tensor_tensor_scan(gc[g8, :], const("resetf")[g8, 0:N], ga[g8, :], 0.0, ALU.mult, ALU.add))
        dv.link(dve.tensor_copy(glast[g8, :], gc[g8, C - 1::C]))
        dv.link(dve.tensor_scalar(nbeta[g8, :], beta[g8, :], -1.0, None, ALU.mult))
        ch = lambda t: t[g8, :].rearrange("p (c t) -> p c t", t=C)
        dve.tensor_tensor(ch(wsr), along(glast[g8, :], C), ch(gc), ALU.subtract).then_inc(S["gd_args"], 1)
        dve.wait_ge(S["gd_gexp"], 1)
        dve.tensor_tensor(gdiag[g8], over(ident[g8, g8], 4), along(eglast[g8, :], H), ALU.mult).then_inc(S["gd_rows"], 1)
        dve.wait_ge(S["gd_tok"], 1)
        dv.link(dve.tensor_copy(gtk[0:C], PS[0:C, 0, 0:16 * H].rearrange("p (j c h) -> p j c h", j=4, h=H)))
        dv.link(dve.tensor_copy(eglb, PS[:, 1, 0:4 * H].rearrange("p (c h) -> p c h", h=H)))
        dv.link(dve.memset(Sg, 0.0))
        for j, (t, s) in enumerate(((gq, sq), (gk, xc))):
            dve.wait_ge(S["gd_rs"], j + 1)
            ins = dve.tensor_tensor(t, t, s, ALU.mult)
            if j == 0:
                dv.link(ins)
        ins.then_inc(S["gd_ready"], 1)
        dve.wait_ge(S["gd_ready"], 1)
        for c in range(4):
            if c % 2 == 0:
                gd_pair_dve(c // 2)
            gd_chunk_dve(c)

    def gd_pair_dve(cp):
        dve.wait_ge(S["gd_sc"], cp + 1)
        gct = gtk[0:C, 3, 2 * cp:2 * cp + 2, :].rearrange("p c h -> p h c")
        for b in range(2):
            z8 = slice(8 * b, 8 * b + 8)
            d8 = decU[0:C, z8].rearrange("p (h c) t -> p h c t", c=2)
            ps8 = PS[0:C, 4 + b, :].rearrange("p (h c t) -> p h c t", c=2, t=C)
            ins = dve.tensor_tensor(d8, ps8, along(gct[:, 4 * b:4 * b + 4], C), ALU.subtract)
            dv.link(ins)
        dve.tensor_tensor(decU[0:C], decU[0:C], over(const("madd", C)[:, 0:C], 2 * H), ALU.add).then_inc(S["gd_e"], 1)
        dve.wait_ge(S["gd_exp"], cp + 1)
        dv.link(dve.tensor_tensor(attn[0:C], problems(2), decU[0:C], ALU.mult))
        dv.link(dve.tensor_tensor(NTg[0:C], problems(0), decU[0:C], ALU.mult))
        dv.link(dve.tensor_tensor(NTg[0:C], NTg[0:C], problems(6), ALU.mult))
        inverse_dve(NCH + cp, NTg[0:C], lambda lev: over(const("level", C)[:, lev * P:lev * P + C], 2 * H), CTg, Xg, XTg)

    def gd_chunk_dve(c):
        per_token = lambda j: along(gtk[0:C, j, c, :], P)
        dve.wait_ge(S["gd_ks"], c + 1)
        u = Ug[0:C]
        dv.link(dve.tensor_tensor(u, heads2(4), per_token(1), ALU.mult))
        dv.link(dve.tensor_tensor(u, heads2(0), u, ALU.subtract))
        dve.tensor_tensor(u, u, per_token(0), ALU.mult)
        dve.tensor_tensor(ksg[0:C], heads2(2), per_token(2), ALU.mult)
        o = og[0:C]
        dve.tensor_tensor(o, heads2(6), per_token(1), ALU.mult).then_inc(S["gd_rhs"], 1)
        dve.wait_ge(S["gd_y"], c + 1)
        dve.wait_ge(S["gd_rhs"], c + 1)
        dv.link(dve.tensor_tensor(o, o, heads2(2), ALU.add))
        if c < 3:
            dv.link(dve.tensor_tensor(Sg, Sg, along(eglb[:, c, :], P), ALU.mult))
            dve.tensor_tensor(Sg, Sg, heads2(4, P), ALU.add).then_inc(S["gd_step"], 1)
        dv.link(dve.tensor_tensor(osq[0:C], o, o, ALU.mult))
        dv.link(dve.tensor_reduce(oms[0:C, :], osq[0:C], AX.X, ALU.add))
        dve.tensor_scalar(oms[0:C, :], oms[0:C, :], 1.0 / P, EPS, ALU.mult, ALU.add).then_inc(S["gd_var"], 1)
        dve.wait_ge(S["gd_std"], c + 1)
        dv.link(dve.reciprocal(oms[0:C, :], ostd[0:C, :]))
        dve.tensor_tensor(o, o, along(oms[0:C, :], P), ALU.mult).then_inc(S["gd_o"], 1)
        dve.wait_ge(S["gd_ot"], c + 1)
        z = zs[:, :, c * C:(c + 1) * C]
        dve.scalar_tensor_tensor(out=z, in0=PS[:, 6, :].rearrange("p (h t) -> p h t", t=C), scalar=col("gdn_out_norm_2"),
                                 in1=z, op0=ALU.mult, op1=ALU.mult).then_inc(S["gd_mix"], 1)
        if c < 3:
            dve.wait_ge(S["gd_step"], c + 1)

    result = work[:, ABOVE:ABOVE + 2 * D].rearrange("p (t d) -> p t d", t=2)

    def final_pe():
        pe.wait_ge(S["norm_done"], 12)
        for tt in range(2):
            for k in range(KT):
                ins = pe.transpose(PS[:, 2 * tt + k // 4, (k % 4) * P:(k % 4 + 1) * P], hT[:, k, tt * P:(tt + 1) * P], ident)
            ins.then_inc(S["final_turned"], 1)

    def final_act():
        for tt in range(2):
            act.wait_ge(S["final_turned"], tt + 1)
            act.activation(result[:, tt, :], PS[:, 2 * tt:2 * tt + 2, :].rearrange("p b n -> p (b n)"), ACT.Copy)\
               .then_inc(S["result"], 1)

    def final_sp():
        for tt in range(2):
            sp.wait_ge(S["result"], tt + 1)
            sp.dma_start(out[0, tt * P:(tt + 1) * P, :], result[:, tt, :]).then_inc(S["stored"], 16)
        sp.wait_ge(S["stored"], 32)

    block = ctx.enter_context(nc.Block())

    @block.scalar
    def _(eng):
        stage0_act()
        stage0_act2()
        norm1_act()
        w_in_act()
        ml_gates_act()
        for i in range(NCH):
            ml_step_act(i)
        headnorm_act(0, hstat)
        rw_prep_act()
        for i in range(NCH):
            rw_step_act(i)
        headnorm_act(1, ystat)
        norm_act(2)
        norm_act(3)
        route1_act()
        ex_act("moe1")
        norm_act(4)
        norm_act(5)
        mla_act()
        norm_act(8)
        ex_act("ffn")
        norm_act(9)
        gdn_act()
        norm_act(10)
        route2_act()
        ex_act("moe2")
        norm_act(11)
        final_act()

    @block.sync
    def _(eng):
        ada_sp()
        w_in_sp()
        sp.wait_ge(S["mixed"], 1)
        out_sp("w_out", A["w_out"][0])
        ex_sp("moe1")
        mla_sp()
        out_sp("mla_out", A["mla_w_out_2"][0])
        ex_sp("ffn")
        gdn_sp()
        out_sp("gdn_out", A["gdn_w_out_2"][0])
        ex_sp("moe2")
        final_sp()

    @block.gpsimd
    def _(eng):
        stage0_pool()
        ml_pool()

    @block.tensor
    def _(eng):
        stage0_pe()
        ada_pe()
        norm1_pe()
        w_in_pe()
        ml_gates_pe()
        for i in range(NCH):
            ml_step_pe(i)
        headnorm_pe(0, hs)
        rw_prep_pe()
        for i in range(NCH):
            rw_step_pe(i)
        headnorm_pe(1, yr)
        pe.wait_ge(S["mixed"], 1)
        out_pe("w_out", mixT)
        norm_pe(2, xT, KT, True, lambda e: all_emptied(e, "w_out"))
        norm_pe(3, xT, KT, True, lambda e: e.wait_ge(S["norm_done"], 3))
        route_pe(w_rt1, 36, 3, N_EXP1)
        ex_pe("moe1")
        norm_pe(4, xT, KT, True, lambda e: e.wait_ge(S["resid"], 1))
        norm_pe(5, xT, KT, False, None)
        mla_pe()
        pe.wait_ge(S["at_oe"], HM)
        out_pe("mla_out", oT)
        norm_pe(8, xT, KT, False, None)
        pe.wait_ge(S["norm_done"], 9)
        ex_pe("ffn")
        norm_pe(9, xT, KT, False, None)
        gdn_pe()
        pe.wait_ge(S["gd_mix"], 4)
        out_pe("gdn_out", zs)
        norm_pe(10, xT, KT, False, None)
        route_pe(w_rt2, N_EXP2, 10, N_EXP2)
        ex_pe("moe2")
        norm_pe(11, xT, KT, False, None)
        final_pe()

    @block.vector
    def _(eng):
        stage0_dve()
        ada_dve()
        norm1_dve()
        conv_dve()
        all_emptied(dve, "w_in")
        ml_gates_dve()
        for i in range(NCH):
            ml_step_dve(i)
        headnorm_dve(0, hs, hsq, hstat, LN_EPS)
        ml_out_dve()
        rw_prep_dve()
        for i in range(NCH):
            rw_step_dve(i)
        headnorm_dve(1, yr, ysq, ystat, GN_EPS)
        rw_out_dve()

        def m1(t0):
            return lambda k: mod1[:, t0 + k, 0:1]

        def m2(layer, t0):
            return lambda k: mod2[:, layer, t0 + k, 0:1]

        def g2(j):
            return lambda k: gain2[:, j, k:k + 1]

        def cl(name, t0=0):
            return lambda k: col(name, t0 + k)

        out_dve("w_out", m1(16), ALPHA)
        norm_dve(2, xT, KT, True, xT, cl("ln1_g"), cl("ln1_b"), LN_EPS)
        norm_dve(3, xT, KT, True, hT, m1(32), m1(24), LN_EPS)
        route1_dve()
        ex_dve("moe1", True)
        ex_resid_dve("moe1", m1(40), ALPHA)
        dve.wait_ge(S["resid"], 1)
        norm_dve(4, xT, KT, True, xT, cl("ln2_g"), cl("ln2_b"), LN_EPS)
        norm_dve(5, xT, KT, False, hT, g2(0), m2(0, 0), EPS)
        mla_dve()
        out_dve("mla_out", m2(0, 16), 1.0)
        norm_dve(8, xT, KT, False, hT, g2(1), m2(0, 24), EPS)
        ex_dve("ffn", False)
        ex_resid_dve("ffn", m2(0, 40), 1.0)
        dve.wait_ge(S["resid"], 2)
        norm_dve(9, xT, KT, False, hT, g2(2), m2(1, 0), EPS)
        gdn_dve()
        out_dve("gdn_out", m2(1, 16), 1.0)
        norm_dve(10, xT, KT, False, hT, g2(3), m2(1, 24), EPS)
        route2_dve()
        ex_dve("moe2", True)
        ex_resid_dve("moe2", m2(1, 40), 1.0)
        dve.wait_ge(S["resid"], 3)
        norm_dve(11, xT, KT, False, hT, cl("final_norm_2"), None, EPS)

    return ctx


def kernel(**inputs):
    import concourse.bacc as bacc
    from concourse.bass_utils import run_bass_kernel_spmd

    nc = bacc.Bacc("TRN2", target_bir_lowering=False, num_devices=1, dynamic_dma_scratch_size=1024)
    consts, const_at = constants()
    arrays, drams = {}, {}
    for name, a in list(inputs.items()) + [("consts", consts)]:
        a = np.ascontiguousarray(a)
        arrays[f"in_{name}_dram"] = a
        drams[name] = nc.dram_tensor(f"in_{name}_dram", a.shape, mybir.dt.from_np(a.dtype), kind="ExternalInput").ap()
    out = nc.dram_tensor("out_0_dram", (1, N, D), F32, kind="ExternalOutput").ap()
    build(nc, drams, out, const_at).close()
    r = run_bass_kernel_spmd(nc, [arrays], core_ids=[0])
    return r.results[0]["out_0_dram"]
```

```python
from contextlib import ExitStack
import math

import numpy as np

import concourse.bass as bass
from concourse import mybir

ALU = mybir.AluOpType
ACT = mybir.ActivationFunctionType
AX = mybir.AxisListType
F32 = mybir.dt.float32
I32 = mybir.dt.int32
U32 = mybir.dt.uint32

P = 128
D = 1024
KT = D // P
N = 256
C = 64
NCH = 2 * N // C
H = 8
SLOT = 4096
SLOTS = 6
SEG = {"mq": 0, "mk": 4, "rr": 8, "rk": 12, "rv": 16, "mv": 20, "mo": 24}
GATES = 3584
N_EXP1, F_EXP1 = 32, 512
N_EXP2, F_EXP2 = 8, 1408
D_FF = 2816
HM, QK, ROPE, VH = 16, 96, 32, 64
Q_LORA, KV_LORA = 512, 256
ALPHA = 2.0 ** 0.25
DECAY_SCALE = math.exp(-0.5)
LN_EPS, GN_EPS, EPS = 1e-6, 64e-5, 1e-6
NEG = -1e30

ORDER = [list(range(8)), [3, 2, 1, 0, 7, 6, 5, 4]]


def constants():
    parts, at = [], {}
    p = np.arange(P)

    def put(name, a):
        a = np.asarray(a, np.float32).reshape(a.shape[0], -1)
        full = np.zeros((P, a.shape[1]), np.float32)
        full[: a.shape[0]] = a
        at[name] = (sum(x.shape[1] for x in parts), a.shape[1])
        parts.append(full)

    put("ident", np.eye(P))
    put("ones", np.ones((P, P)))
    put("zeros", np.zeros((P, P)))
    put("blk1", (p[:, None] // C) == (p[None, :] // C))
    s, t = np.arange(C)[:, None], np.arange(C)[None, :]
    past = [s < t, s > t]
    seen = [s <= t, s >= t]
    rw = np.stack([np.concatenate([past[d], seen[d]], 1) for d in range(2)], 1)
    put("rwmask", np.concatenate([rw, rw], 0))
    put("bmask65", (p[:, None] // C) == (np.arange(130)[None, :] // 65))
    lv = np.zeros((C, 6, 2, C))
    for lev in range(6):
        b = 1 << lev
        same = (s // (2 * b) == t // (2 * b)) & (s // b != t // b)
        for d in range(2):
            lv[:, lev, d] = same & past[d]
    put("level", np.concatenate([lv, lv], 0))
    madd = np.stack([np.where(seen[d], 0.0, NEG) for d in range(2)], 1)
    put("madd", np.concatenate([madd, madd], 0))
    pick = np.zeros((40, 2 * H, C))
    for d in range(2):
        for h in range(H):
            pick[32 * d + h, d * H + h] = 1
    put("pick", pick)
    tok = np.arange(2 * N)
    put("resetf", np.broadcast_to(tok % C != 0, (P, 2 * N)))
    put("resetb", np.broadcast_to(tok % C != C - 1, (P, 2 * N)))
    q, k = p[:, None], p[None, :]
    caus = np.where(k <= q, 0.0, NEG)
    put("causal", np.concatenate([caus, np.zeros((P, P)), caus], 1))
    put("iota", np.broadcast_to(np.arange(P), (P, P)))
    put("before", q < k)
    rot = np.zeros((QK, QK))
    half = ROPE // 2
    for i in range(half):
        rot[64 + half + i, 64 + i] = -1
        rot[64 + i, 64 + half + i] = 1
    put("rot", rot)
    inv = np.zeros((P, 1))
    inv[64:96, 0] = np.tile((10000.0 ** (-np.arange(half, dtype=np.float32) / half)).astype(np.float32), 2)
    put("invfreq", inv)
    return np.ascontiguousarray(np.concatenate(parts, 1)), at


def row_params():
    return [("c", 8), ("c_ctx", 8), ("c_2", 8), ("b_ada", 48), ("ada_b_2", 96), ("conv_w", 180), ("m_norm_w", 4),
            ("r_w0", 8), ("r_a0", 4), ("r_kk", 4), ("r_ka", 4), ("r_bonus", 4), ("r_norm_w", 4), ("r_norm_b", 4),
            ("ln1_g", 8), ("ln1_b", 8), ("ln2_g", 8), ("ln2_b", 8), ("norm_mix_2", 16), ("norm_ffn_2", 16),
            ("final_norm_2", 8), ("mla_q_norm_2", 4), ("mla_kv_norm_2", 2), ("gdn_conv_w_2", 96),
            ("gdn_out_norm_2", 1)]


ROW_TILES = 5


class Sems(dict):

    def __init__(self, nc, ctx):
        super().__init__()
        self.nc, self.ctx = nc, ctx

    def __missing__(self, name):
        self[name] = self.ctx.enter_context(self.nc.semaphore(name))
        return self[name]


class Chain:

    def __init__(self, eng, sem):
        self.eng, self.sem, self.n = eng, sem, 0

    def link(self, ins):
        self.n += 1
        ins.then_inc(self.sem, 1)
        self.eng.wait_ge(self.sem, self.n)


class Space:

    def __init__(self, tensor, start, end):
        self.t, self.pos, self.end, self.high = tensor, start, end, start

    def take(self, *shape):
        n = int(np.prod(shape))
        a = self.t[:, self.pos:self.pos + n]
        self.pos += n
        self.high = max(self.high, self.pos)
        assert self.pos <= self.end, (self.pos, self.end)
        if len(shape) == 1:
            return a
        names = "abcd"[:len(shape)]
        return a.rearrange(f"p ({' '.join(names)}) -> p {' '.join(names)}",
                           **{x: s for x, s in zip(names[1:], shape[1:])})


def along(ap, n):
    return ap.unsqueeze(len(ap.shape)).broadcast_to(list(ap.shape) + [n])


def over(ap, n, axis=1):
    shape = list(ap.shape)
    return ap.unsqueeze(axis).broadcast_to(shape[:axis] + [n] + shape[axis:])


def build(nc, A, out, const_at):
    ctx = ExitStack()
    S = Sems(nc, ctx)

    def sb(name, shape, dt=F32):
        return ctx.enter_context(nc.sbuf_tensor(name, shape, dt))[tuple(slice(None) for _ in shape)]

    n_const = sum(w for _, w in const_at.values())
    consts = sb("consts", [P, n_const])
    cols = sb("param_cols", [P, ROW_TILES * P])
    w_lora = sb("w_lora", [P, H * C])
    w_a = sb("w_a", [C, H * C])
    w_g = sb("w_g", [P, H * C])
    w_gate = sb("w_gate", [P, KT, 2, 40])
    w_rt1 = sb("w_rt1", [P, KT, 36])
    w_rt2 = sb("w_rt2", [P, KT, N_EXP2])
    w_ba = sb("w_ba", [P, KT, 16])
    rt_bias = sb("rt_bias", [P, 36])
    gate_bias = sb("gate_bias", [40, 2])
    gdn_bias = sb("gdn_bias", [H, 2])
    cond = sb("cond", [P, 3, KT])
    mod1 = sb("mod1", [P, 48, 2])
    mod2 = sb("mod2", [P, 2, 48])
    gain2 = sb("gain2", [P, 4, KT])
    xT = sb("xT", [P, KT, N])
    hT = sb("hT", [P, KT, N])
    xc = sb("xc", [P, KT, N])
    sq = sb("sq", [P, KT, N])
    mean = sb("mean", [P, N])
    rstd = sb("rstd", [P, N])
    tmp = sb("tmp", [P, 2, N])
    work_len = SLOTS * SLOT + 14940
    work = sb("work", [P, work_len])
    PS = ctx.enter_context(nc.psum_tensor("PS", [P, 8, 512], F32))

    ring = [work[:, i * SLOT:(i + 1) * SLOT] for i in range(SLOTS)]
    ABOVE = SLOTS * SLOT

    def const(name, parts=P):
        at, w = const_at[name]
        return consts[0:parts, at:at + w]

    ident, ones, zeros = const("ident"), const("ones"), const("zeros")

    row_at, n_rows = {}, 0
    for name, n in row_params():
        row_at[name] = n_rows
        n_rows += n
    assert n_rows <= ROW_TILES * P

    def col(name, t=0, n=1):
        return cols[:, row_at[name] + t:row_at[name] + t + n]

    pe, dve, act, pool, sp = nc.tensor, nc.vector, nc.scalar, nc.gpsimd, nc.sync
    dv = Chain(dve, S["dve_step"])
    ac = Chain(act, S["act_step"])
    po = Chain(pool, S["pool_step"])

    landed = [S[f"landed{i}"] for i in range(SLOTS)]
    N_ADA1, N_ADA = 12, 36
    N_AHEAD = 6
    order = []
    for n in range(N_ADA1):
        order.append(("ada", n))
        if n % 2:
            order.append(("ada", N_ADA1 + n // 2))
    ada_behind, n = [], N_ADA1 + N_AHEAD
    for j in range(8):
        ada_behind.append(list(range(n, n + (2 if j < 6 else 3))))
        n += len(ada_behind[j])
        order += [("w_in", j)] + [("ada", k) for k in ada_behind[j]]
    assert n == N_ADA
    place = {x: u for u, x in enumerate(order)}
    U = {}
    n_units = len(order)
    for name, n in (("w_out", 2), ("moe1", 96), ("mla", 5), ("mla_out", 2), ("ffn", 18), ("gdn_in", 8), ("gdn_out", 2),
                    ("moe2", 72)):
        U[name] = n_units
        n_units += n

    def unit(u, k, n):
        return ring[u % SLOTS][:, 0:k * n].rearrange("p (k n) -> p k n", k=k)

    downs_before = {"moe1": 0, "ffn": 32, "moe2": 32 + 6}
    unit_tile = {}

    def released(u):
        if u < len(order):
            name, j = order[u]
        else:
            name = max((x for x in U if U[x] <= u), key=lambda x: U[x])
            j = u - U[name]
        if name == "ada":
            if j < N_ADA1:
                sp.wait_ge(S["ada_rows"], j + 1)
            else:
                sp.wait_ge(S["ada_pool"], j - N_ADA1 + 1)
        elif name in downs_before:
            sp.wait_ge(S["weights_used"], downs_before[name] + {"moe1": 32, "ffn": 6, "moe2": 24}[name])
        else:
            tile, i = unit_tile[name][j]
            sp.wait_ge(S["tile_full"], first_tile[tile] + i + 1)

    def load(u, src):
        if u >= SLOTS:
            released(u - SLOTS)
        sp.dma_start(unit(u, src.shape[1], src.shape[2]), src).then_inc(landed[u % SLOTS], 16)

    def arrived(u, i=0, eng=pe):
        eng.wait_ge(landed[u % SLOTS], i * 16 + 16 * (u // SLOTS + 1))

    def ktiles(w, n0, n):
        return w.rearrange("(k p) n -> p k n", p=P)[:, :, n0:n0 + n]

    tile_owner = []
    tile_count = {"act": 0, "dve": 0}
    first_tile = {}
    for name, spec in (("w_in", ["dve"] * 20 + ["act"] * 13), ("lora", ["act"] * 16), ("kap", ["act"] * 4),
                       ("bonus", ["dve"] * 4), ("w_out", ["dve"] * 8), ("mla", ["act"] * 7 + ["dve"]),
                       ("q", ["act"] * 16), ("rot", ["dve"] * 16), ("kv", ["act"] * 20), ("mla_out", ["dve"] * 8),
                       ("gdn_ba", ["act"]), ("gdn_qk", ["dve"] * 16), ("gdn_l2q", ["act"] * 4), ("gdn_v", ["dve"] * 8),
                       ("gdn_l2k", ["act"] * 4), ("gdn_z", ["act"] * 8), ("gdn_out", ["dve"] * 8)):
        first_tile[name] = len(tile_owner)
        for e in spec:
            tile_count[e] += 1
            tile_owner.append((e, tile_count[e]))

    unit_tile["w_in"] = [("w_in", 4 * j + 3) for j in range(7)] + [("w_in", 32)]
    unit_tile["w_out"] = [("w_out", 3), ("w_out", 7)]
    unit_tile["mla"] = [("mla", 3), ("mla", 6), ("q", 7), ("q", 15), ("kv", 19)]
    unit_tile["mla_out"] = [("mla_out", 3), ("mla_out", 7)]
    unit_tile["gdn_in"] = ([("gdn_qk", 4 * j + 3) for j in range(4)] + [("gdn_v", 3), ("gdn_v", 7)] +
                           [("gdn_z", 3), ("gdn_z", 7)])
    unit_tile["gdn_out"] = [("gdn_out", 3), ("gdn_out", 7)]

    def tile_begin(name, i):
        g = first_tile[name] + i
        if g >= 4:
            e, n = tile_owner[g - 4]
            pe.wait_ge(S[f"emptied_{e}"], n)
        return PS[:, 4 + g % 4, :]

    def tile_full(eng, name, i):
        g = first_tile[name] + i
        eng.wait_ge(S["tile_full"], g + 1)
        return PS[:, 4 + g % 4, :]

    def all_emptied(eng, name):
        names = list(first_tile)
        at = names.index(name) + 1
        end = first_tile[names[at]] if at < len(names) else len(tile_owner)
        for e in ("act", "dve"):
            n = max([k for o, k in tile_owner[:end] if o == e], default=0)
            if n:
                eng.wait_ge(S[f"emptied_{e}"], n)

    def product(outp, pairs, **kw):
        for n, (lhs, rhs) in enumerate(pairs):
            ins = pe.matmul(outp, lhs, rhs, start=n == 0, stop=n == len(pairs) - 1, **kw)
        return ins

    tok = work[:, ABOVE:ABOVE + 4096].rearrange("p (t n) -> p t n", t=4)
    rows = work[:, ABOVE + 6144:ABOVE + 6144 + ROW_TILES * P].rearrange("p (t n) -> p t n", n=P)
    N_COND = 24
    small_loads = [0]

    def stage0_act():
        def ld(dst, src):
            small_loads[0] += 1
            act.dma_start(dst, src).then_inc(S["small"], 16)

        act.wait_ge(S["zeroed"], 4)
        r = 0
        for name, n in row_params():
            a = A[name]
            flat = a
            while len(flat.shape) > 1:
                k = len(flat.shape)
                flat = flat.rearrange("a b -> (a b)" if k == 2 else "a b c -> (a b) c" if k == 3 else "a b c d -> (a b) c d")
            v = flat.rearrange("(t p) -> t p", p=P)
            t = 0
            while t < n:
                m = min(n - t, P - (r + t) % P)
                dst = rows[(r + t) % P:(r + t) % P + m, (r + t) // P, :]
                if r >= N_COND:
                    ld(dst, v[t:t + m, :])
                t += m
            r += n
            if r == N_COND:
                ld(tok[:, 0:2, :], A["ctx"][0].rearrange("(t p) d -> p t d", p=P))
                ld(tok[:, 2:4, :], A["x"][0].rearrange("(t p) d -> p t d", p=P))
        for d in range(2):
            for j in range(2):
                c0 = GATES + 16 * d + 8 * j
                ld(w_gate[:, :, j, 32 * d:32 * d + 8], ktiles(A["w_in"][0], c0, 8))
            ld(gate_bias[32 * d:32 * d + 8, 0:1], A["m_bias_i"][0, d:d + 1, :].rearrange("a h -> h a"))
            ld(gate_bias[32 * d:32 * d + 8, 1:2], A["m_bias_f"][0, d:d + 1, :].rearrange("a h -> h a"))
        ld(w_lora[:, :], A["r_wB"][0].rearrange("d k n -> (d k) n"))
        ld(w_a[:, :], A["r_aB"][0])
        ld(w_g[:, :], A["r_gB"][0])
        ld(w_rt1[:, :, 0:4], ktiles(A["rt_g"][0], 0, 4))
        ld(w_rt1[:, :, 4:36], ktiles(A["rt_e"][0], 0, 32))
        ld(w_rt2[:, :, :], ktiles(A["moe_w_router_2"][0], 0, N_EXP2))
        ld(w_ba[:, :, :], ktiles(A["gdn_w_in_2"][0], 4096, 16))
        ld(rt_bias[:, 0:4], A["rt_g_b"][0:1, :].broadcast_to([P, 4]))
        ld(rt_bias[:, 4:36], A["rt_e_b"][0:1, :].broadcast_to([P, 32]))
        ld(gdn_bias[:, 0:1], A["gdn_a_log_2"].rearrange("a h -> h a"))
        ld(gdn_bias[:, 1:2], A["gdn_dt_bias_2"].rearrange("a h -> h a"))

    def first_sp():
        sp.wait_ge(S["zeroed"], 1)
        for name, n in row_params()[0:3]:
            v = A[name] if len(A[name].shape) == 1 else A[name].rearrange("a b -> (a b)")
            sp.dma_start(rows[row_at[name]:row_at[name] + n, 0, :], v.rearrange("(t p) -> t p", p=P)).then_inc(S["first"], 16)
        sp.dma_start(consts[:, :], A["consts"]).then_inc(S["first"], 16)

    def stage0_pool():
        pool.memset(rows[:, :, :], 0.0).then_inc(S["zeroed"], 1)
        pool.memset(w_gate[:, :, :, :], 0.0).then_inc(S["zeroed"], 1)
        pool.memset(gate_bias[:, :], 0.0).then_inc(S["zeroed"], 1)
        pool.memset(mean[:, :], 0.0).then_inc(S["zeroed"], 1)

    COND_BANK = 6

    def cond_pe():
        pe.wait_ge(S["first"], 16 * 4)
        pe.transpose(PS[:, COND_BANK, 0:N_COND], rows[0:N_COND, 0, :], ident[0:N_COND, 0:N_COND]).then_inc(S["turned"], 1)

    def cond_act():
        act.wait_ge(S["turned"], 1)
        act.activation(cond.rearrange("p v k -> p (v k)"), PS[:, COND_BANK, 0:N_COND], ACT.Silu).then_inc(S["cond"], 1)

    def stage0_pe():
        pe.wait_ge(S["small"], 16 * small_loads[0])
        for t in range(ROW_TILES):
            ins = pe.transpose(PS[:, t // 4, (t % 4) * P:(t % 4 + 1) * P], rows[:, t, :], ident)
        ins.then_inc(S["turned"], 1)
        pe.wait_ge(S["params"], 1)
        for tt in range(4):
            if tt >= 2:
                pe.wait_ge(S["x_evac"], tt - 1)
            for k in range(KT):
                ins = pe.transpose(PS[:, 2 * (tt % 2) + k // 4, (k % 4) * P:(k % 4 + 1) * P],
                                   tok[:, tt, k * P:(k + 1) * P], ident)
            ins.then_inc(S["turned"], 1)

    ctxT = work[:, ABOVE + 4096:ABOVE + 4096 + 2048].rearrange("p (k n) -> p k n", k=KT)

    def stage0_dve():
        dve.wait_ge(S["turned"], 2)
        dv.link(dve.tensor_copy(cols[:, 0:512], PS[:, 0, :]))
        dve.tensor_copy(cols[:, 512:640], PS[:, 1, 0:128]).then_inc(S["params"], 1)
        dve.wait_ge(S["params"], 1)

    def stage0_act2():
        for tt in range(4):
            act.wait_ge(S["turned"], tt + 3)
            dst = (ctxT if tt < 2 else xT)[:, :, (tt % 2) * P:(tt % 2 + 1) * P]
            b = 2 * (tt % 2)
            act.activation(dst, PS[:, b:b + 2, :].rearrange("p b (k n) -> p (b k) n", n=P), ACT.Copy)\
               .then_inc(S["x_evac"], 1)

    ADA_BANKS = (7, 2)
    ada_src = [(A["w_ada"][0]), (A["ada_w_2"][0]), (A["ada_w_2"][1])]
    ada_row = work[:, ABOVE + 6784:ABOVE + 6784 + 2 * 512].rearrange("p (b n) -> p b n", b=2)
    ADA_SUMS = 6
    ada_sum = work[:, work_len - ADA_SUMS * 512:work_len].rearrange("p (b n) -> p b n", b=ADA_SUMS)

    def ada_load(n):
        load(place["ada", n], ktiles(ada_src[n // 12], (n % 12) * 512, 512))

    def ada1_pe(n):
        u = place["ada", n]
        arrived(u)
        if n == 0:
            pe.wait_ge(S["cond"], 1)
        if n >= 2:
            pe.wait_ge(S["ada_evac"], n - 1)
        w = unit(u, KT, 512)
        product(PS[0:2, 4 + n % 2, :], [(cond[:, 0:2, k], w[:, k, :]) for k in range(KT)]).then_inc(S["ada_rows"], 1)
        if n:
            ada1_turn_pe(n - 1)

    def ada1_turn_pe(n):
        pe.wait_ge(S["ada_evac"], n + 1)
        for m in range(4):
            c0 = (n * 4 + m) * 2
            ins = pe.matmul(PS[:, ADA_BANKS[0], c0:c0 + 2], ada_row[0:2, n % 2, m * P:(m + 1) * P], ident[0:2, 0:2],
                            start=True, stop=True)
        ins.then_inc(S["ada_cols"], 1)

    def ada1_act(n):
        act.wait_ge(S["ada_rows"], n + 1)
        if n >= 2:
            act.wait_ge(S["ada_cols"], n - 1)
        act.activation(ada_row[0:2, n % 2, :], PS[0:2, 4 + n % 2, :], ACT.Copy).then_inc(S["ada_evac"], 1)

    def ada1_dve():
        dve.wait_ge(S["ada_cols"], N_ADA1)
        dv.link(dve.tensor_tensor(mod1[:, :, :], PS[:, ADA_BANKS[0], 0:96].rearrange("p (m s) -> p m s", s=2),
                                  along(col("b_ada", 0, 48), 2), ALU.add))
        for m in (8, 32):
            dv.link(dve.tensor_scalar(mod1[:, m:m + 8, :], mod1[:, m:m + 8, :], 1.0, None, ALU.add))

    def ada2_act(n):
        u = place["ada", n]
        arrived(u, 0, act)
        w = unit(u, KT, 512)
        for k in range(KT):
            ins = act.activation(w[:, k, :], w[:, k, :], ACT.Copy, scale=cond[:, 2, k:k + 1])
        ins.then_inc(S["ada_mul"], 1)

    def ada2_pool(n):
        pool.wait_ge(S["ada_mul"], n - N_ADA1 + 1)
        if n >= N_ADA1 + ADA_SUMS:
            pool.wait_ge(S["ada_cols"], n - ADA_SUMS + 1)
        t = unit(place["ada", n], KT, 512)
        po.link(pool.tensor_tensor(t[:, 0:4, :], t[:, 0:4, :], t[:, 4:8, :], ALU.add))
        po.link(pool.tensor_tensor(t[:, 0:2, :], t[:, 0:2, :], t[:, 2:4, :], ALU.add))
        pool.tensor_tensor(ada_sum[:, n % ADA_SUMS, :], t[:, 0, :], t[:, 1, :], ALU.add).then_inc(S["ada_pool"], 1)

    def ada2_pe(n):
        if n == N_ADA1:
            pe.wait_ge(S["x_evac"], 4)
        j = n - N_ADA1
        pe.wait_ge(S["ada_pool"], j + 1)
        for m in range(4):
            c0 = j * 4 + m
            ins = pe.matmul(PS[:, ADA_BANKS[1], c0:c0 + 1], ada_sum[:, n % ADA_SUMS, m * P:(m + 1) * P], ones[:, 0:1], start=True,
                            stop=True)
        ins.then_inc(S["ada_cols"], 1)

    def ada2_dve():
        dve.wait_ge(S["ada_cols"], N_ADA)
        dv.link(dve.tensor_tensor(mod2.rearrange("p l m -> p (l m)"), PS[:, ADA_BANKS[1], 0:96], col("ada_b_2", 0, 96),
                                  ALU.add))
        for m in (8, 32):
            dv.link(dve.tensor_scalar(mod2[:, :, m:m + 8], mod2[:, :, m:m + 8], 1.0, None, ALU.add))
        for l in range(2):
            dv.link(dve.tensor_tensor(gain2[:, 2 * l, :], mod2[:, l, 8:16], col("norm_mix_2", 8 * l, 8), ALU.mult))
            dv.link(dve.tensor_tensor(gain2[:, 2 * l + 1, :], mod2[:, l, 32:40], col("norm_ffn_2", 8 * l, 8), ALU.mult))

    def norm_sums(n, mean_too=True):
        return sum(1 + c for _, _, c, *_ in NORMS[:n]) + (1 if not mean_too else 1 + NORMS[n][2])

    def norm_pe(n, ready=None):
        src, kt, centred = NORMS[n][0:3]
        if centred:
            ready(pe)
            product(PS[:, 0, 0:N], [(ones, src[:, k, :]) for k in range(kt)]).then_inc(S["norm_sums"], 1)
        for k in range(kt):
            if k in (0, kt // 2):
                pe.wait_ge(S["norm_sq"], 2 * n + 1 + (k > 0))
            ins = pe.matmul(PS[:, 1, 0:N], ones, sq[:, k, :], start=k == 0, stop=k == kt - 1)
        ins.then_inc(S["norm_sums"], 1)

    def norm_affine(n, k, engine):
        _, _, _, dst, gains, biases, _ = NORMS[n]
        if engine is act:
            return act.activation(dst[:, k, :], xc[:, k, :], ACT.Identity, scale=gains(k),
                                  bias=0.0 if biases is None else biases(k))
        if biases is None:
            return dve.tensor_scalar(dst[:, k, :], xc[:, k, :], gains(k), None, ALU.mult)
        return dve.tensor_scalar(dst[:, k, :], xc[:, k, :], gains(k), biases(k), ALU.mult, ALU.add)

    def norm_dve(n):
        src, kt, centred, dst, gains, biases, eps = NORMS[n]
        width = kt * P
        first, second = slice(0, kt // 2), slice(kt // 2, kt)
        if centred:
            dve.wait_ge(S["norm_sums"], norm_sums(n, False))
            dv.link(dve.tensor_scalar(mean[:, :], PS[:, 0, 0:N], 1.0 / width, None, ALU.mult))
            dv.link(dve.tensor_tensor(xc[:, 0:kt, :], src, over(mean[:, :], kt), ALU.subtract))
            src = xc[:, 0:kt, :]
        for part in (first, second):
            dve.tensor_tensor(sq[:, part, :], src[:, part, :], src[:, part, :], ALU.mult).then_inc(S["norm_sq"], 1)
        dve.wait_ge(S["norm_sums"], norm_sums(n))
        dve.tensor_scalar(tmp[:, 0, :], PS[:, 1, 0:N], 1.0 / width, eps, ALU.mult, ALU.add).then_inc(S["norm_ms"], 1)
        dve.wait_ge(S["norm_std"], n + 1)
        dv.link(dve.reciprocal(rstd[:, :], tmp[:, 1, :]))
        dve.tensor_tensor(xc[:, second, :], src[:, second, :], over(rstd[:, :], kt - kt // 2), ALU.mult)\
           .then_inc(S["norm_scaled"], 1)
        dv.link(dve.tensor_tensor(xc[:, first, :], src[:, first, :], over(rstd[:, :], kt // 2), ALU.mult))
        for k in range(kt // 2):
            ins = norm_affine(n, k, dve)
        ins.then_inc(S["norm_done"], 1)
        dve.wait_ge(S["norm_done"], 2 * n + 2)

    def norm_act(n):
        kt = NORMS[n][1]
        act.wait_ge(S["norm_ms"], n + 1)
        act.activation(tmp[:, 1, :], tmp[:, 0, :], ACT.Sqrt).then_inc(S["norm_std"], 1)
        act.wait_ge(S["norm_scaled"], n + 1)
        for k in range(kt // 2, kt):
            ins = norm_affine(n, k, act)
        ins.then_inc(S["norm_done"], 1)

    def normed(eng, n):
        eng.wait_ge(S["norm_done"], 2 * n + 2)

    above = Space(work, ABOVE, work_len)
    hall = above.take(KT, 2 * N)
    q1 = above.take(4, N)
    rr = above.take(4, N)
    rv = above.take(4, C + 2 * N)
    mo = above.take(4, N)
    li, lf = above.take(2 * N), above.take(2 * N)
    lw, la, lg = above.take(2 * N), above.take(2 * N), above.take(N)
    mixT = above.take(KT, N)
    gT = above.take(4, N)
    k1 = hT[:, :, :].rearrange("p (k a) n -> p k (a n)", a=2)
    rk = xc[:, :, :].rearrange("p (k a) n -> p k (a n)", a=2)
    mv = sq[:, :, :].rearrange("p (k a) n -> p k (a n)", a=2)
    section = [("mq", q1, True), ("mk", k1, False), ("rr", rr, True), ("rk", rk, False), ("rv", rv[:, :, C:], False),
               ("mv", mv, False), ("mo", mo, True)]

    def early_sp():
        for name, j in order:
            if name == "ada":
                ada_load(j)
            elif j < 7:
                load(place["w_in", j], ktiles(A["w_in"][0], 512 * j, 512))
            else:
                load(place["w_in", j], ktiles(A["w_in"][0], GATES, 352))

    def w_in_pe():
        normed(pe, 1)
        for i in range(28):
            u = place["w_in", i // 4]
            if i % 4 == 0:
                arrived(u)
                for n in [[], range(N_ADA1, N_ADA1 + N_AHEAD), *ada_behind][i // 4]:
                    ada2_pe(n)
            w = unit(u, KT, 512)
            o = tile_begin("w_in", i)
            lat = section[i // 4][2]
            t0, n = (N, N) if lat else (0, 2 * N)
            product(o[:, 0:n], [(w[:, k, (i % 4) * P:(i % 4 + 1) * P], hall[:, k, t0:t0 + n]) for k in range(KT)])\
                .then_inc(S["tile_full"], 1)
        for j in range(2):
            o = tile_begin("w_in", 28 + j)
            product(o[0:40, :], [(w_gate[:, k, j, :], hall[:, k, :]) for k in range(KT)]).then_inc(S["tile_full"], 1)
        arrived(place["w_in", 7])
        w = unit(place["w_in", 7], KT, 352)
        for j, (c0, m, t0, n) in enumerate(((32, P, 0, 2 * N), (160, C, 0, 2 * N), (224, P, N, N))):
            o = tile_begin("w_in", 30 + j)
            product(o[0:m, 0:n], [(w[:, k, c0:c0 + m], hall[:, k, t0:t0 + n]) for k in range(KT)])\
                .then_inc(S["tile_full"], 1)
        for n in ada_behind[5] + ada_behind[6] + ada_behind[7]:
            ada2_pe(n)

    def conv_dve():
        for i in range(20):
            o = tile_full(dve, "w_in", i)
            _, dst, lat = section[i // 4]
            y = dst[:, i % 4, :]

            def w(a, b):
                return col("conv_w", (3 * a + b) * 20 + i)

            n = N if lat else 2 * N
            dv.link(dve.tensor_scalar(y, o[:, 0:n], w(1, 1), None, ALU.mult))
            if not lat:
                for b, (y0, y1, x0, x1) in ((0, (1, N, 0, N - 1)), (2, (0, N - 1, 1, N))):
                    dv.link(dve.scalar_tensor_tensor(out=y[:, y0:y1], in0=o[:, x0:x1], scalar=w(1, b), in1=y[:, y0:y1],
                                                     op0=ALU.mult, op1=ALU.add))
            yg = y[:, n - N:n].rearrange("p (r c) -> p r c", c=64)
            xg = o[:, n - N:n].rearrange("p (r c) -> p r c", c=64)
            taps = [(a, b) for a in range(3) for b in range(3) if (a, b) != (1, 1)]
            for a, b in taps:
                r0, r1 = max(0, 1 - a), min(4, 5 - a)
                c0, c1 = max(0, 1 - b), min(64, 65 - b)
                ins = dve.scalar_tensor_tensor(
                    out=yg[:, r0:r1, c0:c1], in0=xg[:, r0 + a - 1:r1 + a - 1, c0 + b - 1:c1 + b - 1], scalar=w(a, b),
                    in1=yg[:, r0:r1, c0:c1], op0=ALU.mult, op1=ALU.add)
                if (a, b) == taps[-1]:
                    ins.then_inc(S["emptied_dve"], 1)
                else:
                    dv.link(ins)

    def w_in_act():
        def evac(i, dst, src, func, **kw):
            act.activation(dst, src, func, **kw).then_inc(S["emptied_act"], 1)

        for n in range(ada_behind[0][0], ada_behind[6][0]):
            ada2_act(n)
        for i in range(20, 24):
            evac(i, mv[:, i - 20, :], tile_full(act, "w_in", i), ACT.Copy)
        for n in ada_behind[6]:
            ada2_act(n)
        for i in range(24, 28):
            evac(i, mo[:, i - 24, :], tile_full(act, "w_in", i)[:, 0:N], ACT.Sigmoid)
        for n in ada_behind[7]:
            ada2_act(n)
        for j, dst in enumerate((li, lf)):
            evac(28 + j, dst[0:40, :], tile_full(act, "w_in", 28 + j)[0:40, :], ACT.Identity, bias=gate_bias[:, j:j + 1])
        evac(30, lw, tile_full(act, "w_in", 30), ACT.Tanh)
        evac(31, la[0:C, :], tile_full(act, "w_in", 31)[0:C, :], ACT.Copy)
        evac(32, lg, tile_full(act, "w_in", 32)[:, 0:N], ACT.Sigmoid)
        act.wait_ge(S["emptied_dve"], 8)
        ac.link(act.activation(q1, q1, ACT.Silu))
        ac.link(act.activation(k1, k1, ACT.Silu))
        act.activation(k1, k1, ACT.Copy, scale=C ** -0.5).then_inc(S["qk_ready"], 1)

    R40 = 40
    ml = Space(work, 0, SLOTS * SLOT)
    z_ = ml.take(2 * N)
    e_ = ml.take(2 * N)
    b_, m_, a_, Dm, nD = (ml.take(2 * N) for _ in range(5))
    inter, einvm, wts = (ml.take(2 * N) for _ in range(3))
    mprev, DC, decay = (ml.take(NCH) for _ in range(3))
    diag = ml.take(NCH, R40)
    wtok = ml.take(NCH, R40)
    gtok = ml.take(3, 4, R40)
    decb = ml.take(NCH, R40)
    vt = ml.take(NCH, H, C + 1)
    Cst = ml.take(4, 2, 2 * (C + 1))
    kw = ml.take(2, H, C)
    Em = ml.take(2, H, C)
    Pm = ml.take(2, H, C)
    hn = ml.take(2, 2, 4, C + 1)
    den, rden = ml.take(2, H), ml.take(2, H)
    hs = ml.take(4, H * C)
    hsq = ml.take(4, H * C)
    ct = ml.take(4, 2, 2 * (C + 1))
    kw2 = ml.take(2, H, C)
    hstat = [ml.take(4 * H) for _ in range(2)]
    nDh = ml.take(4, H, C)
    g40 = lambda t: t[0:R40, :]
    T64 = lambda t: t[0:C]

    def ml_pool():
        pool.wait_ge(S["tile_full"], first_tile["w_in"] + 33)
        pool.wait_ge(S["ada_pool"], N_ADA - N_ADA1)
        for t in (b_, m_, mprev, DC):
            pool.memset(g40(t), 0.0)
        pool.memset(vt[0:C], 1.0)
        pool.memset(Cst, 0.0)
        pool.memset(hs[0:C], 0.0)
        pool.memset(rv[:, :, 0:C], 0.0).then_inc(S["zeroed"], 1)

    def ml_gates_dve():
        dve.wait_ge(S["emptied_act"], 10)
        dve.wait_ge(S["tile_full"], first_tile["w_in"] + 33)
        dve.wait_ge(S["zeroed"], 5)
        dve.scalar_tensor_tensor(out=g40(z_), in0=g40(lf), scalar=-1.0, in1=g40(lf), op0=ALU.mult, op1=ALU.max).then_inc(S["ml_z"], 1)
        dve.wait_ge(S["ml_gexp"], 1)
        dv.link(dve.scalar_tensor_tensor(out=g40(lf), in0=g40(lf), scalar=0.0, in1=g40(e_), op0=ALU.min,
                                         op1=ALU.subtract))
        f, w = slice(0, 8), slice(32, 40)
        rf, rb = const("resetf"), const("resetb")
        dv.link(dve.tensor_tensor_scan(b_[f, :], rf[f, :], lf[f, :], 0.0, ALU.mult, ALU.add))
        dv.link(dve.tensor_tensor_scan(b_[w, ::-1], rb[w, ::-1], lf[w, ::-1], 0.0, ALU.mult, ALU.add))
        dv.link(dve.tensor_tensor_scan(m_[f, :], lf[f, :], li[f, :], 0.0, ALU.add, ALU.max))
        for s0 in (0, N):
            part = lambda t: t[w, s0:s0 + N][:, ::-1]
            dv.link(dve.tensor_tensor_scan(part(m_), part(lf), part(li), m_[w, 0:1] if s0 else 0.0, ALU.add, ALU.max))
        dv.link(dve.tensor_copy(mprev[f, 1:8], m_[f, 63:511:C]))
        dv.link(dve.tensor_copy(mprev[w, 0:3], m_[w, 64:256:C]))
        dv.link(dve.tensor_copy(mprev[w, 4:7], m_[w, 320:512:C]))
        dv.link(dve.tensor_copy(mprev[w, 7:8], m_[w, 0:1]))
        dv.link(dve.tensor_tensor(g40(a_), g40(li), g40(b_), ALU.subtract))
        dv.link(dve.tensor_tensor(g40(Dm), g40(m_), g40(b_), ALU.subtract))
        dv.link(dve.tensor_tensor(g40(nD), g40(b_), g40(m_), ALU.subtract))
        dv.link(dve.tensor_copy(DC[f, :], Dm[f, 63::C]))
        dv.link(dve.tensor_copy(DC[w, :], Dm[w, 0::C]))
        chunked = lambda t: g40(t).rearrange("p (c t) -> p c t", t=C)
        dv.link(dve.tensor_tensor(chunked(inter), along(g40(mprev), C), chunked(Dm), ALU.subtract))
        dv.link(dve.tensor_tensor(chunked(wts), chunked(a_), along(g40(DC), C), ALU.subtract))
        dve.tensor_tensor(g40(decay), g40(mprev), g40(DC), ALU.subtract).then_inc(S["ml_args"], 1)
        dve.wait_ge(S["ml_gexp"], 2)
        for r in (f, w):
            ins = dve.tensor_tensor(nDh[r], over(nD[r, N:2 * N].rearrange("p (c t) -> p c t", t=C), H, 2),
                                    over(along(ident[r, r], C), 4), ALU.mult)
        dv.link(ins)
        dve.tensor_tensor(diag[0:R40], over(ident[0:R40, 0:R40], NCH), along(g40(decay), R40), ALU.mult)\
           .then_inc(S["ml_args"], 1)
        dve.wait_ge(S["ml_tok"], 1)
        dv.link(dve.tensor_copy(T64(wtok), PS[0:C, 0, 0:NCH * R40].rearrange("p (c r) -> p c r", r=R40)))
        dv.link(dve.tensor_copy(T64(gtok), PS[0:C, 1, 0:12 * R40].rearrange("p (g c r) -> p g c r", g=3, r=R40)))
        dve.tensor_copy(decb, PS[:, 2, 0:NCH * R40].rearrange("p (c r) -> p c r", r=R40)).then_inc(S["ml_gtok"], 1)
        dve.wait_ge(S["ml_gtok"], 1)

    def ml_gates_act():
        act.wait_ge(S["ml_z"], 1)
        ac.link(act.activation(g40(e_), g40(z_), ACT.Exp, scale=-1.0))
        act.activation(g40(e_), g40(e_), ACT.Ln, bias=1.0).then_inc(S["ml_gexp"], 1)
        act.wait_ge(S["ml_args"], 1)
        act.activation(g40(inter), g40(inter), ACT.Exp)
        act.activation(g40(wts), g40(wts), ACT.Exp)
        act.activation(g40(decay), g40(decay), ACT.Exp)
        act.activation(g40(einvm), g40(m_), ACT.Exp, scale=-1.0).then_inc(S["ml_gexp"], 1)
        act.wait_ge(S["zeroed"], 5)
        for c in range(NCH):
            act.wait_ge(S["ml_vt"], c + 1)
            act.activation(vt[0:C, c, :, 0:C], PS[0:C, 4 + c % 4, :].rearrange("p (h e) -> p h e", h=H), ACT.Copy)\
               .then_inc(S["ml_ve"], 1)

    def ml_gates_pe():
        all_emptied(pe, "w_in")
        for c in range(NCH):
            if c >= 4:
                pe.wait_ge(S["ml_ve"], c - 3)
            for p in range(4):
                ins = pe.transpose(PS[0:C, 4 + c % 4, p * P:(p + 1) * P], mv[:, p, c * C:(c + 1) * C], ident)
            ins.then_inc(S["ml_vt"], 1)
        pe.wait_ge(S["ml_args"], 2)
        i40 = ident[0:R40, 0:R40]
        for c in range(NCH):
            pe.transpose(PS[0:C, 0, c * R40:(c + 1) * R40], wts[0:R40, c * C:(c + 1) * C], i40)
        for g, t in enumerate((a_, inter, einvm)):
            for c in range(4):
                o = (g * 4 + c) * R40
                pe.transpose(PS[0:C, 1, o:o + R40], t[0:R40, (4 + c) * C:(5 + c) * C], i40)
        pe.matmul(PS[:, 2, 0:NCH * R40], ones[0:R40, :], diag[0:R40].rearrange("p c r -> p (c r)"), start=True,
                  stop=True).then_inc(S["ml_tok"], 1)
        pe.wait_ge(S["ml_ve"], NCH)
        pe.wait_ge(S["ml_gtok"], 1)
        pe.wait_ge(S["qk_ready"], 1)

    def half(h):
        return slice(C * (h % 2), C * (h % 2) + C)

    def ml_ahead_pe(i):
        cs = [ORDER[d][i] for d in range(2)]
        for d in range(2):
            for p in range(4):
                ins = pe.transpose(PS[0:C, d, p * P:(p + 1) * P], k1[:, p, cs[d] * C:(cs[d] + 1) * C], ident)
        ins.then_inc(S["ml_ktok"], 1)
        if i >= 4:
            for d in range(2):
                ck, cq = cs[d] * C, (cs[d] - 4) * C
                for h in range(H):
                    at = (d * 4 + h // 2) * C
                    pe.matmul(PS[0:C, 2 + h % 2, at:at + C], k1[half(h), h // 2, ck:ck + C],
                              q1[half(h), h // 2, cq:cq + C], start=True, stop=True)

    def ml_step_pe(i):
        if i:
            pe.wait_ge(S["ml_step"], i)
        else:
            ml_ahead_pe(0)
        cs = [ORDER[d][i] for d in range(2)]
        lat = i >= 4
        if lat:
            for d in range(2):
                o = PS[0:C, 4 + d, :]
                pe.matmul(o, ident[0:C, 0:C], over(const("madd", C)[:, d * C:(d + 1) * C], H), start=True, stop=False)
                ins = pe.matmul(o, ones[32 * d:32 * d + 8, 0:C],
                                nDh[32 * d:32 * d + 8, cs[d] - 4].rearrange("p h t -> p (h t)"), start=False, stop=True)
            ins.then_inc(S["ml_sc"], 1)
            pe.wait_ge(S["ml_p"], i - 3)
        pe.wait_ge(S["ml_kw"], i + 1)
        if lat:
            for d in range(2):
                cq = (cs[d] - 4) * C
                for p in range(4):
                    pe.matmul(PS[0:C, 4 + 2 * d + p // 2, (p % 2) * 130:(p % 2) * 130 + 130], q1[:, p, cq:cq + C],
                              Cst[:, 2 * d + p // 2, p % 2, :], start=True, stop=True)
                for h in range(H):
                    ins = pe.matmul(PS[0:C, 2 * d + h // 4, (h % 4) * 65:(h % 4) * 65 + 65], Pm[0:C, d, h, :],
                                    vt[0:C, cs[d], h, :], start=True, stop=True)
            ins.then_inc(S["ml_num"], 1)
            pe.wait_ge(S["ml_hn"], i - 3)
        if i < NCH - 1:
            for d in range(2):
                for p in range(4):
                    ins = pe.matmul(PS[:, 4 + 2 * d + p // 2, (p % 2) * 130:(p % 2) * 130 + 130],
                                    kw[0:C, d, 2 * p:2 * p + 2, :].rearrange("s h e -> s (h e)"),
                                    vt[0:C, cs[d], 2 * p:2 * p + 2, :].rearrange("s h e -> s (h e)"), start=True, stop=True)
            ins.then_inc(S["ml_st"], 1)
            ml_ahead_pe(i + 1)

    def ml_step_dve(i):
        cs = [ORDER[d][i] for d in range(2)]
        lat = i >= 4
        rows_of = lambda d: slice(32 * d, 32 * d + 8)
        dve.wait_ge(S["ml_ktok"], i + 1)
        for d in range(2):
            ins = dve.tensor_tensor(kw[0:C, d], PS[0:C, d, :].rearrange("p (h e) -> p h e", h=H),
                                    along(wtok[0:C, cs[d], rows_of(d)], C), ALU.mult)
        ins.then_inc(S["ml_kw"], 1)
        if lat:
            j = i - 4
            dve.wait_ge(S["ml_sc"], j + 1)
            for d in range(2):
                ins = dve.tensor_tensor(Em[0:C, d], PS[0:C, 4 + d, :].rearrange("p (h t) -> p h t", h=H),
                                        along(gtok[0:C, 0, cs[d] - 4, rows_of(d)], C), ALU.add)
            ins.then_inc(S["ml_e"], 1)
            dve.wait_ge(S["ml_exp"], j + 1)
            for b in range(2):
                ins = dve.tensor_tensor(Pm[0:C, :, b::2, :], PS[0:C, 2 + b, :].rearrange("p (d h t) -> p d h t", d=2, t=C),
                                        Em[0:C, :, b::2, :], ALU.mult)
            ins.then_inc(S["ml_p"], 1)
            dve.wait_ge(S["ml_num"], j + 1)
            for d in range(2):
                g = gtok[0:C, 1, cs[d] - 4, rows_of(d)].rearrange("p (b h) -> p b h", b=2)
                ins = dve.tensor_tensor(hn[0:C, d], PS[0:C, 4 + 2 * d:6 + 2 * d, 0:260].rearrange("p b (h e) -> p b h e", h=4),
                                        along(g, C + 1), ALU.mult)
            dv.link(ins)
            h4 = hn[0:C].rearrange("p d b h e -> p (d b) (h e)")
            dve.tensor_tensor(h4, h4, PS[0:C, 0:4, 0:260], ALU.add).then_inc(S["ml_hn"], 1)
            dve.wait_ge(S["ml_hn"], j + 1)
            hz = hn[0:C].rearrange("p d b h e -> p d (b h) e")
            dv.link(dve.scalar_tensor_tensor(out=den[0:C], in0=hz[:, :, :, C], scalar=-1.0, in1=hz[:, :, :, C], op0=ALU.mult,
                                             op1=ALU.max))
            for d in range(2):
                ins = dve.tensor_tensor(den[0:C, d], den[0:C, d], gtok[0:C, 2, cs[d] - 4, rows_of(d)], ALU.max)
            dv.link(ins)
            dv.link(dve.reciprocal(rden[0:C], den[0:C]))
            dv.link(dve.tensor_tensor(kw2[0:C], hz[:, :, :, 0:C], along(rden[0:C], C), ALU.mult))
            for d in range(2):
                dst = hs[0:C, cs[d] - 4, :].rearrange("p (h e) -> p h e", h=H)
                dv.link(dve.tensor_tensor(dst, dst, kw2[0:C, d], ALU.add))
        if i < NCH - 1:
            dve.wait_ge(S["ml_st"], i + 1)
            dv.link(dve.tensor_tensor(ct, PS[:, 4:8, 0:260].rearrange("p b (q e) -> p b q e", q=2),
                                      over(over(const("bmask65"), 2), 4), ALU.mult))
            for d in range(2):
                cv = Cst[:, 2 * d:2 * d + 2].rearrange("p b q (h e) -> p (b q h) e", h=2)
                ins = dve.tensor_tensor(cv, cv, along(decb[:, cs[d], rows_of(d)], C + 1), ALU.mult)
            dv.link(ins)
            dve.tensor_tensor(Cst, Cst, ct, ALU.add).then_inc(S["ml_step"], 1)
            dve.wait_ge(S["ml_step"], i + 1)

    def ml_step_act(i):
        if i >= 4:
            act.wait_ge(S["ml_e"], i - 3)
            act.activation(Em[0:C], Em[0:C], ACT.Exp).then_inc(S["ml_exp"], 1)

    def headnorm_dve(n, buf, scratch, stat, eps):
        v = buf[0:C].rearrange("p c (h e) -> p (c h) e", e=C)
        w = scratch[0:C].rearrange("p c (h e) -> p (c h) e", e=C)
        s0, s1 = stat[0][0:C, :], stat[1][0:C, :]
        dv.link(dve.tensor_reduce(s0, v, AX.X, ALU.add))
        dv.link(dve.tensor_scalar(s0, s0, 1.0 / C, None, ALU.mult))
        dv.link(dve.tensor_tensor(v, v, along(s0, C), ALU.subtract))
        dv.link(dve.tensor_tensor(w, v, v, ALU.mult))
        dv.link(dve.tensor_reduce(s0, w, AX.X, ALU.add))
        dve.tensor_scalar(s1, s0, 1.0 / C, eps, ALU.mult, ALU.add).then_inc(S["hn_var"], 1)
        dve.wait_ge(S["hn_std"], n + 1)
        dv.link(dve.reciprocal(s0, s1))
        dve.tensor_tensor(v, v, along(s0, C), ALU.mult).then_inc(S["hn_done"], 1)
        dve.wait_ge(S["hn_done"], n + 1)

    def headnorm_act(n, stat):
        act.wait_ge(S["hn_var"], n + 1)
        act.activation(stat[1][0:C, :], stat[1][0:C, :], ACT.Sqrt).then_inc(S["hn_std"], 1)

    def headnorm_pe(n, buf):
        pe.wait_ge(S["hn_done"], n + 1)
        for p in range(4):
            for c in range(4):
                ins = pe.transpose(PS[:, p, c * C:(c + 1) * C], buf[0:C, c, p * P:(p + 1) * P], ident[0:C, 0:C])
        ins.then_inc(S["hn_turned"], 1)

    def ml_out_dve():
        dve.wait_ge(S["hn_turned"], 1)
        dve.wait_ge(S["emptied_act"], 8)
        for p in range(4):
            ins = dve.scalar_tensor_tensor(out=mixT[:, p, :], in0=PS[:, p, 0:N], scalar=col("m_norm_w", p),
                                           in1=mo[:, p, :], op0=ALU.mult, op1=ALU.mult)
        ins.then_inc(S["ml_out"], 1)
        dve.wait_ge(S["ml_out"], 1)

    rw = Space(work, 0, SLOTS * SLOT)
    BK = rw.take(2, 4, NCH * 2 * C)
    KR = rw.take(2, 4, NCH * 2 * C)
    BKc = [BK[:, d].rearrange("p q (c j t) -> p q c j t", c=NCH, j=2) for d in range(2)]
    KRc = [KR[:, d].rearrange("p q (c j t) -> p q c j t", c=NCH, j=2) for d in range(2)]
    lw2 = [rw.take(4, 2 * N), hall[:, 0:4, :]]
    kh, nb = rw.take(4, 2 * N), rw.take(4, 2 * N)
    kmod = hall[:, 4:8, :]
    csum = k1
    eb = [rk, mv]
    kss = mv
    at = rw.pos - 3 * 4 * 2 * N
    later = Space(work, at, rw.pos)
    Msc = later.take(2 * H, 2 * C)
    BKt, UV = later.take(2, H * C), later.take(2, H * C)
    CTm, Xm = later.take(H, P), later.take(H, P)
    NTm = rw.take(H, P)
    later = Space(work, ABOVE, ABOVE + KT * 2 * N)
    XTm, Ym = later.take(H, P), later.take(H, P)
    Gs = later.take(2, 4 * C)
    S0 = later.take(2, 4, P)
    yr = hT[:, :, :].rearrange("p (c a) n -> p c (a n)", a=2)
    st = xc[:, 0:4, :].rearrange("p (d q) n -> p d (q n)", d=2).rearrange("p d (q n) -> p d q n", n=P)
    ysq = sq[:, :, :].rearrange("p (c a) n -> p c (a n)", a=2)
    ystat = [tmp[:, 0, 128 + 32 * j:160 + 32 * j] for j in range(2)]
    eC = tmp[:, 0, 0:64].rearrange("p (d q c) -> p d q c", d=2, q=4)
    omka = tmp[:, 0, 64:68]
    prod = q1
    rv_all = rv[:, :, C:]

    def rw_prep_pe():
        pe.wait_ge(S["hn_turned"], 1)
        for j in range(12):
            o = tile_begin("lora", j)
            p = j % 4
            if j < 8:
                s = slice(C * (j // 4), C * (j // 4) + C)
                pairs = [(w_lora[s, p * P:(p + 1) * P], lw[s, :])]
            else:
                pairs = [(w_a[:, p * P:(p + 1) * P], la[0:C, :])]
            product(o, pairs).then_inc(S["tile_full"], 1)
        for p in range(4):
            product(tile_begin("lora", 12 + p)[:, 0:N], [(w_g[:, p * P:(p + 1) * P], lg)]).then_inc(S["tile_full"], 1)
        pe.wait_ge(S["rw_kap"], 1)
        for p in range(4):
            product(tile_begin("kap", p), [(const("blk1"), eb[1][:, p, :])]).then_inc(S["tile_full"], 1)
        pe.wait_ge(S["rw_bonus"], 1)
        for p in range(4):
            product(tile_begin("bonus", p)[:, 0:N], [(const("blk1"), prod[:, p, :])]).then_inc(S["tile_full"], 1)

    def rw_prep_act():
        def evac(name, i, dst, src, func, **kw):
            act.activation(dst, src, func, **kw).then_inc(S["emptied_act"], 1)

        act.wait_ge(S["ml_out"], 1)
        for j in range(12):
            p = j % 4
            dst, bias = (lw2[j // 4][:, p, :], col("r_w0", j)) if j < 8 else (nb[:, p, :], col("r_a0", p))
            evac("lora", j, dst, tile_full(act, "lora", j), ACT.Sigmoid, bias=bias)
        for p in range(4):
            evac("lora", 12 + p, gT[:, p, :], tile_full(act, "lora", 12 + p)[:, 0:N], ACT.Copy)
        for p in range(4):
            evac("kap", p, csum[:, p, :], tile_full(act, "kap", p), ACT.Copy)
        act.wait_ge(S["rw_kss"], 1)
        ac.link(act.activation(csum, csum, ACT.Ln, scale=2.0 ** 20))
        act.activation(csum, csum, ACT.Exp, scale=-0.5, bias=10 * math.log(2.0)).then_inc(S["rw_rs"], 1)
        for n in range(6):
            act.wait_ge(S["rw_arg"], n + 1)
            src, scale = ((eb[n % 2], -DECAY_SCALE), (csum, -DECAY_SCALE), (csum, DECAY_SCALE))[n % 3]
            act.activation(eb[n % 2], src, ACT.Exp, scale=scale).then_inc(S["rw_exp"], 1)

    def rw_prep_dve():
        for p in range(4):
            ins = dve.tensor_scalar(kh[:, p, :], rk[:, p, :], col("r_kk", p), None, ALU.mult)
        dv.link(ins)
        dve.tensor_tensor(eb[1], kh, kh, ALU.mult).then_inc(S["rw_kap"], 1)
        dv.link(dve.tensor_scalar(omka, col("r_ka", 0, 4), -1.0, 1.0, ALU.mult, ALU.add))
        dve.wait_ge(S["emptied_act"], tile_owner[first_tile["lora"] + 11][1])
        for p in range(4):
            ins = dve.tensor_scalar(kmod[:, p, :], nb[:, p, :], col("r_ka", p), omka[:, p:p + 1], ALU.mult, ALU.add)
        dv.link(ins)
        dv.link(dve.tensor_tensor(kmod, kmod, rk, ALU.mult))
        for p in range(4):
            ins = dve.scalar_tensor_tensor(out=prod[:, p, :], in0=rr[:, p, :], scalar=col("r_bonus", p),
                                           in1=kmod[:, p, N:2 * N], op0=ALU.mult, op1=ALU.mult)
        ins.then_inc(S["rw_bonus"], 1)
        dve.wait_ge(S["emptied_act"], tile_owner[first_tile["kap"] + 3][1])
        dve.tensor_scalar(csum, csum, 1e-24, None, ALU.max).then_inc(S["rw_kss"], 1)
        for p in range(4):
            o = tile_full(dve, "bonus", p)[:, 0:N]
            ins = dve.tensor_tensor(prod[:, p, :], o, rv_all[:, p, N:2 * N], ALU.mult)
            ins.then_inc(S["emptied_dve"], 1)
        dve.wait_ge(S["rw_rs"], 1)
        dv.link(dve.tensor_tensor(kh, kh, csum, ALU.mult))
        dv.link(dve.scalar_tensor_tensor(out=nb, in0=kh, scalar=-1.0, in1=nb, op0=ALU.mult, op1=ALU.mult))
        n = 0
        for d in range(2):
            mask = const("resetb" if d else "resetf")
            step = -1 if d else 1
            for p in range(4):
                ins = dve.tensor_tensor_scan(csum[:, p, ::step], mask[:, ::step], lw2[d][:, p, ::step], 0.0, ALU.mult,
                                             ALU.add)
            dv.link(ins)
            chunks = lambda t: t.rearrange("p q (c t) -> p q c t", t=C)
            dve.tensor_tensor(eb[n % 2], csum, lw2[d], ALU.subtract).then_inc(S["rw_arg"], 1)
            dve.wait_ge(S["rw_exp"], n + 1)
            dve.tensor_tensor(KRc[d][:, :, :, 0, :], chunks(kh), chunks(eb[n % 2]), ALU.mult).then_inc(S["rw_arg"], 1)
            n += 1
            dve.wait_ge(S["rw_exp"], n + 1)
            e = chunks(eb[n % 2])
            dv.link(dve.tensor_copy(eC[:, d], e[:, :, :, 0 if d else C - 1]))
            dve.tensor_tensor(KRc[d][:, :, 4:8, 1, :], chunks(rr), e[:, :, 4:8, :], ALU.mult).then_inc(S["rw_arg"], 1)
            n += 1
            dve.wait_ge(S["rw_exp"], n + 1)
            e = chunks(eb[n % 2])
            dv.link(dve.tensor_tensor(BKc[d][:, :, :, 0, :], chunks(nb), e, ALU.mult))
            dv.link(dve.tensor_tensor(BKc[d][:, :, :, 1, :], chunks(kmod), e, ALU.mult))
            n += 1
        dve.wait_ge(S["zeroed"], 5)
        dv.link(dve.memset(S0, 0.0))
        dv.link(dve.memset(NTm, 0.0))
        dve.memset(yr[0:C], 0.0).then_inc(S["rw_ready"], 1)
        dve.wait_ge(S["rw_ready"], 1)

    def four(t, g):
        return t[:, 4 * g:4 * g + 4, :]

    def bank4(b):
        return PS[:, b, :].rearrange("p (z t) -> p z t", t=P)

    def inverse_pe(n, CT, X, XT, Y, levels=range(6)):
        def each(bank, g, lhs, rhs):
            for z in range(4):
                ins = pe.matmul(PS[:, bank + g, z * P:(z + 1) * P], lhs[:, 4 * g + z, :],
                                rhs[:, 4 * g + z, :] if rhs is not None else ident, start=True, stop=True)
            return ins

        for lev in levels:
            for g in range(2):
                pe.wait_ge(S["inv_ct"], 12 * n + 2 * lev + g + 1)
                if lev:
                    pe.wait_ge(S["inv_x"], 10 * n + 2 * (lev - 1) + g + 1)
                each(0, g, CT, X if lev else None).then_inc(S["inv_y"], 1)
            if lev:
                for g in range(2):
                    pe.wait_ge(S["inv_ye"], 10 * n + 2 * (lev - 1) + g + 1)
                    pe.wait_ge(S["inv_xt"], 12 * n + 2 * (lev - 1) + g + 1)
                    if lev < 5:
                        each(2, g, XT, Y)
                    each(4, g, Y, XT).then_inc(S["inv_z"], 1)
        if 5 in levels:
            pe.wait_ge(S["inv_xt"], 12 * (n + 1))

    def inverse_part_dve(NT, mask, CT, lev, g):
        halves_ = lambda t: four(t, g).rearrange("p z (a t) -> p z a t", t=C)
        dve.tensor_tensor(halves_(CT), halves_(NT), mask(lev, g), ALU.mult).then_inc(S["inv_ct"], 1)

    def inverse_dve(n, NT, mask, CT, X, XT, begun=False):
        i4 = over(ident, 4)

        def part(lev, g):
            inverse_part_dve(NT, mask, CT, lev, g)

        if not begun:
            for g in range(2):
                part(0, g)
        for g in range(2):
            dve.wait_ge(S["inv_ct"], 12 * n + g + 1)
            dve.tensor_tensor(four(XT, g), four(CT, g), i4, ALU.add).then_inc(S["inv_xt"], 1)
        for g in range(2):
            dve.wait_ge(S["inv_y"], 12 * n + g + 1)
            dve.tensor_tensor(four(X, g), bank4(g), i4, ALU.add).then_inc(S["inv_x"], 1)
            dve.wait_ge(S["inv_xt"], 12 * n + g + 1)
            part(1, g)
        for lev in range(1, 6):
            for g in range(2):
                if lev < 5:
                    dve.wait_ge(S["inv_y"], 12 * n + 2 * lev + g + 1)
                    part(lev + 1, g)
            for g in range(2):
                dve.wait_ge(S["inv_z"], 10 * n + 2 * (lev - 1) + g + 1)
                if lev < 5:
                    dve.tensor_tensor(four(X, g), four(X, g), bank4(2 + g), ALU.add).then_inc(S["inv_x"], 1)
                dve.tensor_tensor(four(XT, g), four(XT, g), bank4(4 + g), ALU.add).then_inc(S["inv_xt"], 1)

    def inverse_act(n, Y):
        for lev in range(1, 6):
            for g in range(2):
                act.wait_ge(S["inv_y"], 12 * n + 2 * lev + g + 1)
                act.activation(four(Y, g), bank4(g), ACT.Copy).then_inc(S["inv_ye"], 1)

    def rw_nt_pe(i):
        cs = [ORDER[d][i] for d in range(2)]
        for d in range(2):
            for h in range(H):
                t0 = cs[d] * P
                ins = pe.matmul(PS[half(h), 6 + h % 2, (4 * d + h // 2) * C:(4 * d + h // 2 + 1) * C],
                                BK[half(h), d, h // 2, t0:t0 + C], KR[half(h), d, h // 2, t0:t0 + C], start=True, stop=True)
        ins.then_inc(S["rw_nt"], 1)

    def rw_step_pe(i):
        cs = [ORDER[d][i] for d in range(2)]
        lat = i >= 4
        if i == 0:
            pe.wait_ge(S["rw_ready"], 1)
            rw_nt_pe(0)
        for d in range(2):
            if d == 1 and i > 0:
                pe.wait_ge(S["rw_step"], i)
            for h in range(H):
                c = cs[d]
                lhs = BK[half(h), d, h // 2, c * P:(c + 1) * P]
                n = P if lat else C
                ins = pe.matmul(PS[:, 2 * d + h % 2, (h // 2) * P:(h // 2) * P + n], lhs,
                                KR[half(h), d, h // 2, c * P:c * P + n], start=True, stop=True)
        ins.then_inc(S["rw_sc"], 1)
        pe.wait_ge(S["rw_nte"], i + 1)
        for d in range(2):
            for p in range(4):
                pe.transpose(PS[:, 4 + d, p * P:(p + 1) * P], BK[:, d, p, cs[d] * P:(cs[d] + 1) * P], ident)
                ins = pe.transpose(PS[:, 6 + d, p * P:(p + 1) * P], rv[:, p, cs[d] * C:cs[d] * C + P], ident)
        ins.then_inc(S["rw_tr"], 1)
        pe.wait_ge(S["rw_m"], i + 1)
        inverse_pe(i, CTm, Xm, XTm, Ym, range(1))
        pe.wait_ge(S["rw_bk"], i + 1)
        for d in range(2):
            for p in range(4):
                for h in (2 * p, 2 * p + 1):
                    o = PS[half(h), 6 + d, p * C:(p + 1) * C]
                    pe.matmul(o, KR[:, d, p, cs[d] * P:cs[d] * P + C], S0[:, d, p, half(h)], start=True, stop=False,
                              skip_group_check=True)
                    ins = pe.matmul(o, Msc[C:P, d * H + h, 0:C], UV[C:P, d, h * C:(h + 1) * C], start=False, stop=True,
                                    skip_group_check=True)
        ins.then_inc(S["rw_g"], 1)
        inverse_pe(i, CTm, Xm, XTm, Ym, range(1, 6))
        pe.wait_ge(S["rw_ge"], i + 1)
        for d in range(2):
            for h in range(H):
                ins = pe.matmul(PS[0:C, d, h * C:(h + 1) * C], XTm[:, 4 * d + h // 2, half(h)],
                                Gs[:, d, (h // 2) * C:(h // 2 + 1) * C], start=True, stop=True)
        ins.then_inc(S["rw_u"], 1)
        if i < NCH - 1:
            rw_nt_pe(i + 1)
        pe.wait_ge(S["rw_ue"], i + 1)
        for d in range(2):
            if lat:
                for p in range(4):
                    pe.matmul(PS[0:C, 2 + d, p * P:(p + 1) * P], KR[:, d, p, cs[d] * P + C:(cs[d] + 1) * P],
                              S0[:, d, p, :], start=True, stop=False, skip_group_check=True)
                    for h in (2 * p, 2 * p + 1):
                        ins = pe.matmul(PS[0:C, 2 + d, h * C:(h + 1) * C], Msc[:, d * H + h, C:P],
                                        UV[:, d, h * C:(h + 1) * C], start=False, stop=h % 2 == 1,
                                        skip_group_check=True)
            if i < NCH - 1:
                for p in range(4):
                    ins = pe.matmul(PS[:, 4 + d, p * P:(p + 1) * P], BKt[:, d, p * P:(p + 1) * P],
                                    UV[:, d, p * P:(p + 1) * P], start=True, stop=True)
        ins.then_inc(S["rw_y"], 1)

    def rw_mask(lev, g):
        return over(over(const("level")[:, lev * P + g * C:lev * P + g * C + C], 2), 4)

    def rw_nt_dve(i):
        dve.wait_ge(S["rw_nt"], i + 1)
        for b in range(2):
            hb = slice(C * b, C * b + C)
            ins = dve.tensor_copy(NTm[hb, :, hb], PS[hb, 6 + b, :].rearrange("p (z t) -> p z t", t=C))
        ins.then_inc(S["rw_nte"], 1)
        dve.wait_ge(S["rw_nte"], i + 1)
        for g in range(2):
            inverse_part_dve(NTm, rw_mask, CTm, 0, g)

    def rw_step_dve(i):
        cs = [ORDER[d][i] for d in range(2)]
        lat = i >= 4
        n = P if lat else C
        if i == 0:
            rw_nt_dve(0)
        dve.wait_ge(S["rw_sc"], i + 1)
        for d in range(2):
            mask = const("rwmask")[:, d * P:d * P + n]
            for b in range(2):
                ins = dve.tensor_tensor(Msc[:, d * H + b:(d + 1) * H:2, 0:n],
                                        PS[:, 2 * d + b, :].rearrange("p (h j) -> p h j", j=P)[:, :, 0:n],
                                        over(mask, 4), ALU.mult)
        ins.then_inc(S["rw_m"], 1)
        dve.wait_ge(S["rw_m"], i + 1)
        inverse_dve(i, NTm, rw_mask, CTm, Xm, XTm, begun=True)
        if i < NCH - 1:
            rw_nt_dve(i + 1)
        dve.wait_ge(S["rw_y"], i + 1)
        if lat:
            for d in range(2):
                dst = yr[0:C, cs[d] - 4, :]
                dv.link(dve.tensor_tensor(dst, dst, PS[0:C, 2 + d, :], ALU.add))
        if i < NCH - 1:
            b8 = over(const("blk1"), 8)
            dv.link(dve.tensor_tensor(st.rearrange("p d q n -> p (d q) n"),
                                      PS[:, 4:6, :].rearrange("p b (q n) -> p (b q) n", n=P), b8, ALU.mult))
            dv.link(dve.tensor_tensor(S0, S0, st, ALU.add))
            for d in range(2):
                ins = dve.tensor_tensor(S0[:, d], S0[:, d], along(eC[:, d, :, cs[d]], P), ALU.mult)
            ins.then_inc(S["rw_step"], 1)
            dve.wait_ge(S["rw_step"], i + 1)

    def rw_step_act(i):
        act.wait_ge(S["rw_tr"], i + 1)
        act.activation(BKt, PS[:, 4:6, :], ACT.Copy)
        act.activation(UV[C:P], PS[C:P, 6:8, :], ACT.Copy).then_inc(S["rw_bk"], 1)
        act.wait_ge(S["rw_g"], i + 1)
        act.activation(Gs, PS[:, 6:8, 0:4 * C], ACT.Copy).then_inc(S["rw_ge"], 1)
        inverse_act(i, Ym)
        act.wait_ge(S["rw_u"], i + 1)
        act.activation(UV[0:C], PS[0:C, 0:2, :], ACT.Copy).then_inc(S["rw_ue"], 1)

    def rw_out_dve():
        dve.wait_ge(S["hn_turned"], 2)
        for p in range(4):
            dv.link(dve.tensor_scalar(mixT[:, 4 + p, :], PS[:, p, 0:N], col("r_norm_w", p), col("r_norm_b", p), ALU.mult,
                                      ALU.add))
            dv.link(dve.tensor_tensor(mixT[:, 4 + p, :], mixT[:, 4 + p, :], prod[:, p, :], ALU.add))
            ins = dve.tensor_tensor(mixT[:, 4 + p, :], mixT[:, 4 + p, :], gT[:, p, :], ALU.mult)
        ins.then_inc(S["mixed"], 1)
        dve.wait_ge(S["mixed"], 1)

    def out_sp(name, w):
        for j in range(2):
            load(U[name] + j, ktiles(w, 512 * j, 512))

    def out_pe(name, src):
        for m in range(KT):
            if m % 4 == 0:
                arrived(U[name] + m // 4)
            w = unit(U[name] + m // 4, KT, 512)
            product(tile_begin(name, m)[:, 0:N], [(w[:, k, (m % 4) * P:(m % 4 + 1) * P], src[:, k, :]) for k in range(KT)])\
                .then_inc(S["tile_full"], 1)

    residuals = [0]

    def residual(m, o, gate, alpha):
        t = tmp[:, m % 2, :]
        dv.link(dve.tensor_scalar(t, o, gate, None, ALU.mult))
        return dve.scalar_tensor_tensor(out=xT[:, m, :], in0=xT[:, m, :], scalar=alpha, in1=t, op0=ALU.mult, op1=ALU.add)

    def out_dve(name, gate, alpha):
        for m in range(KT):
            residual(m, tile_full(dve, name, m)[:, 0:N], gate(m), alpha).then_inc(S["emptied_dve"], 1)
        all_emptied(dve, name)

    SPLIT = {"moe1": [4], "ffn": [4, 4, 3], "moe2": [4, 4, 3]}
    COUNT = {"moe1": N_EXP1, "ffn": 2, "moe2": N_EXP2}
    FFN_F = D_FF // 2
    ex_tiles, n = {}, 0
    for name in SPLIT:
        ex_tiles[name] = n
        n += COUNT[name] * sum(SPLIT[name])

    moe = Space(work, ABOVE, work_len)
    wbc = moe.take(N_EXP1, N)
    hid = moe.take(11, N)
    sil = moe.take(4, N)
    diagw = moe.take(2, 4, P)
    rt_pos = moe.pos

    CAP = {"moe1": 64, "moe2": 128}
    PER = {name: P // n for name, n in CAP.items()}
    slots = Space(work, ABOVE, ABOVE + N_EXP1 * N)
    ys = slots.take(D)
    pickG = slots.take(2, P)
    pickW = slots.take(2, P)
    spread = slots.take(N)
    htk, sil_pair = slots.take(512), slots.take(512)
    htok = xc.rearrange("p k n -> p (k n)").rearrange("p (t d) -> p t d", t=2)
    xs = sq.rearrange("p k n -> p (k n)")[:, 0:KT * P].rearrange("p (k s) -> p k s", s=P)

    def ex_units(name):
        out, t0 = [], 0
        for n in SPLIT[name]:
            out += [("gate", t0, n), ("up", t0, n)]
            t0 += n
        t0 = 0
        for n in SPLIT[name]:
            out.append(("down", t0, n))
            t0 += n
        return out

    def ex_src(name, what, t0, n, e):
        if name == "moe1":
            w = {"gate": A["ex_gate"], "up": A["ex_up"], "down": A["ex_down"]}[what][0]
            w = w[bass.ds(e, 1)].rearrange("a k n -> (a k) n")
            c0 = 0
        elif name == "ffn":
            w = (A["ffn_w_down_2"] if what == "down" else A["ffn_w_gate_up_2"])[0]
            if what == "down":
                w = w[e * FFN_F:(e + 1) * FFN_F, :]
            c0 = e * FFN_F + (D_FF if what == "up" else 0)
        else:
            w = (A["moe_w_down_2"] if what == "down" else A["moe_w_gate_up_2"])[0]
            w = w[bass.ds(e, 1)].rearrange("a k n -> (a k) n")
            c0 = F_EXP2 if what == "up" else 0
        if what == "down":
            return w[t0 * P:(t0 + n) * P, :].rearrange("(k p) n -> p k n", p=P)
        return ktiles(w, c0 + t0 * P, n * P)

    def ex_sp(name):
        per = ex_units(name)
        body = [(e, j) for e in range(2) for j in range(len(per))]
        FT = sum(SPLIT[name])
        n_down = len(SPLIT[name])

        def released_in(b, i):
            e, j = body[b]
            what, t0, n = per[j]
            if what == "down":
                at = downs_before[name] + e * n_down + (j - 2 * n_down) + 1
                sp.wait_ge(S["weights_used"], i * (2 * n_down) + at)
            else:
                sp.wait_ge(S["gate_up"], i * (2 * FT) + (ex_tiles[name] + e * FT + t0 + n))

        def put(b, i, e0):
            e, j = body[b]
            what, t0, n = per[j]
            src = ex_src(name, what, t0, n, e0 + e)
            sp.dma_start(unit(U[name] + b, src.shape[1], src.shape[2]), src)\
                .then_inc(landed[(U[name] + b) % SLOTS], 16)

        use = ["gate", "up", "down"]
        order = sorted(range(len(body)), key=lambda b: use.index(per[body[b][1]][0])) if PER.get(name) == 2 else range(len(body))
        for b in order:
            if b < SLOTS:
                released(U[name] + b - SLOTS)
            else:
                released_in(b - SLOTS, 0)
            put(b, 0, 0)
        if COUNT[name] > 2:
            with sp.Fori(0, COUNT[name] // 2 - 1) as i:
                for b in order:
                    back = b - SLOTS
                    if back < 0:
                        released_in(back + len(body), i)
                    else:
                        released_in(back, i + 1)
                    put(b, i, i * 2 + 2)

    def open_sums():
        for b in range(4):
            pe.matmul(PS[:, b, :], zeros, consts[:, 0:512], start=True, stop=False, skip_group_check=True)

    def close_sums():
        for b in range(4):
            ins = pe.matmul(PS[:, b, :], zeros, consts[:, 0:512], start=False, stop=True, skip_group_check=True)
        ins.then_inc(S["experts"], 1)

    def ex_pe(name):
        FT = sum(SPLIT[name])
        per = ex_units(name)
        rounds = 2 * len(per) // SLOTS
        if name in CAP:
            pe.wait_ge(S["htok"], tokens_turned[name])
        open_sums()
        with pe.Fori(0, COUNT[name] // 2) as i:
            for e in range(2):
                base = ex_tiles[name] + e * FT
                u = U[name] + e * len(per)
                for n in SPLIT[name]:
                    t0 = per[u - U[name] - e * len(per)][1]
                    arrived(u, i * rounds)
                    arrived(u + 1, i * rounds)
                    wg, wu = unit(u, KT, n * P), unit(u + 1, KT, n * P)
                    for t in range(n):
                        f = t0 + t
                        if f >= 4:
                            pe.wait_ge(S["hidden"], i * (2 * FT) + (base + f - 3))
                        for j, w in enumerate((wg, wu)):
                            ins = product(PS[:, 4 + f % 4, j * N:(j + 1) * N],
                                          [(w[:, k, t * P:(t + 1) * P], hT[:, k, :]) for k in range(KT)])
                        ins.then_inc(S["gate_up"], 1)
                    u += 2
                f = 0
                for n in SPLIT[name]:
                    arrived(u, i * rounds)
                    wd = unit(u, n, D)
                    for t in range(n):
                        pe.wait_ge(S["hidden"], i * (2 * FT) + (base + f + 1))
                        for m in range(KT):
                            ins = pe.matmul(PS[:, m // 2, (m % 2) * N:(m % 2 + 1) * N], wd[:, t, m * P:(m + 1) * P],
                                            hid[:, f, :], start=False, stop=False, skip_group_check=True)
                        f += 1
                    ins.then_inc(S["weights_used"], 1)
                    u += 1
        close_sums()

    def ex_act(name):
        FT = sum(SPLIT[name])
        with act.Fori(0, COUNT[name] // 2) as i:
            for e in range(2):
                for f in range(FT):
                    act.wait_ge(S["gate_up"], i * (2 * FT) + (ex_tiles[name] + e * FT + f + 1))
                    act.activation(sil[:, f % 4, :], PS[:, 4 + f % 4, 0:N], ACT.Silu).then_inc(S["silu"], 1)

    def ex_dve(name, weighted):
        FT = sum(SPLIT[name])
        with dve.Fori(0, COUNT[name] // 2) as i:
            for e in range(2):
                for f in range(FT):
                    at = ex_tiles[name] + e * FT + f + 1
                    dve.wait_ge(S["silu"], i * (2 * FT) + at)
                    up = PS[:, 4 + f % 4, N:2 * N]
                    if weighted:
                        dve.tensor_tensor(sil[:, f % 4, :], sil[:, f % 4, :], up, ALU.mult).then_inc(S["diag_" + name], 1)
                        dve.wait_ge(S["diag_" + name], i * (2 * FT) + (COUNT[name] // 2 + e * FT + f + 1))
                        w = wbc[:, bass.ds(i * 2 + e, 1), :].rearrange("p a n -> p (a n)")
                        ins = dve.tensor_tensor(hid[:, f, :], sil[:, f % 4, :], w, ALU.mult)
                    else:
                        ins = dve.tensor_tensor(hid[:, f, :], sil[:, f % 4, :], up, ALU.mult)
                    ins.then_inc(S["hidden"], 1)

    ex_names = list(SPLIT)

    def ex_resid_dve(name, gate, alpha):
        dve.wait_ge(S["experts"], ex_names.index(name) + 1)
        for m in range(KT):
            ins = residual(m, PS[:, m // 2, (m % 2) * N:(m % 2 + 1) * N], gate(m), alpha)
            if m < KT - 1:
                dv.link(ins)
        ins.then_inc(S["resid"], 1)

    def resid_wait(eng, n):
        eng.wait_ge(S["resid"], n)

    def group_tiles(name):
        per = ex_units(name)
        return [(m, t0 + t, m * len(per) + j, t, n) for m in range(PER[name]) for j, (what, t0, n) in enumerate(per)
                if what == "gate" for t in range(n)]

    def gather_pe(name, at, also=None):
        pe.wait_ge(S["pick_" + name], at)
        for k in range(KT):
            for tt in range(2):
                ins = pe.matmul(PS[:, 4 + k // 4, (k % 4) * P:(k % 4 + 1) * P], htok[:, tt, k * P:(k + 1) * P],
                                pickG[:, tt, :], start=tt == 0, stop=tt == 1)
                if tt == 0 and also is not None:
                    ins.then_inc(also, 1)
        ins.then_inc(S["gathered_" + name], 1)

    def combine_pe(name, at):
        pe.wait_ge(S["spread_" + name], at)
        pe.wait_ge(S["ys_" + name], at)
        for m in range(KT):
            ins = pe.matmul(PS[:, m // 2, (m % 2) * N:(m % 2 + 1) * N], ys[:, m * P:(m + 1) * P], spread, start=False,
                            stop=False, skip_group_check=True)
        return ins

    def as_they_lie_pe():
        for tt in range(2):
            for k in range(KT):
                ins = pe.transpose(PS[:, 2 * tt + k // 4, (k % 4) * P:(k % 4 + 1) * P], hT[:, k, tt * P:(tt + 1) * P], ident)
        ins.then_inc(S["htok_turned"], 1)

    def with_tokens_pe(name):
        pe.wait_ge(S["htok"], tokens_turned[name])
        open_sums()
        gather_pe(name, 1)

    def tokens_act(name, at):
        act.wait_ge(S["gathered_" + name], at)
        act.activation(xs, PS[:, 4:6, :].rearrange("p b (k s) -> p (b k) s", s=P), ACT.Copy).then_inc(S["xs_" + name], 1)

    def as_they_lie_act(name):
        act.wait_ge(S["htok_turned"], tokens_turned[name])
        act.activation(htok, PS[:, 0:4, :].rearrange("p (t b) n -> p t (b n)", t=2), ACT.Copy).then_inc(S["htok"], 1)

    def is_mine_dve(name, buf, e0):
        cap, PG = CAP[name], PER[name]
        slot = over(over(const("iota")[:, 0:cap], PG), 2)
        return dve.tensor_tensor(buf.rearrange("p t (m s) -> p t m s", s=cap), slot,
                                 along(rank[:, :, bass.ds(e0, PG)], cap), ALU.is_equal)

    def first_pick_dve(name):
        dve.memset(ys, 0.0).then_inc(S["ys_" + name], 1)
        dve.memset(spread, 0.0).then_inc(S["spread_" + name], 1)
        is_mine_dve(name, pickG, 0).then_inc(S["pick_" + name], 1)

    def pick_dve(name, at, e0):
        cap, PG = CAP[name], PER[name]
        w = pickW.rearrange("p t (m s) -> p t m s", s=cap)
        dve.wait_ge(S["gathered_" + name], at)
        is_mine_dve(name, pickG, e0 + PG).then_inc(S["pick_" + name], 1)
        is_mine_dve(name, pickW, e0).then_inc(S["pickw_" + name], 1)
        dve.wait_ge(S["pickw_" + name], at * 2 - 1)
        dve.tensor_tensor(w, w, along(Wt[:, :, bass.ds(e0, PG)], cap), ALU.mult).then_inc(S["pickw_" + name], 1)

    def outputs_dve(name, at, downs):
        dve.wait_ge(S["turned_" + name], at)
        dve.tensor_copy(spread, PS[:, 7, 0:N]).then_inc(S["spread_" + name], 1)
        dve.wait_ge(S["weights_used"], downs)
        dve.tensor_copy(ys, PS[:, 4:6, :].rearrange("p b n -> p (b n)")).then_inc(S["ys_" + name], 1)

    def ex_pairs_pe(name):
        FT, cap = sum(SPLIT[name]), CAP[name]
        F = FT * P
        pair = [slice(m * cap, (m + 1) * cap) for m in range(2)]
        with_tokens_pe(name)
        with pe.Fori(0, COUNT[name] // 2) as i:
            at = i + 1
            pe.wait_ge(S["xs_" + name], at)
            pe.wait_ge(S["spread_" + name], at)
            for j in range(2):
                for m in range(2):
                    arrived(U[name] + 3 * m + j, i)
                for k in range(KT):
                    for m in range(2):
                        ins = pe.matmul(PS[pair[m], 6 + j, :], xs[:, k, pair[m]], unit(U[name] + 3 * m + j, KT, F)[:, k, :],
                                        start=k == 0, stop=k == KT - 1)
                ins.then_inc(S["pair_" + name], 1)
            pe.wait_ge(S["ys_" + name], at)
            gather_pe(name, at + 1, S["gate_up"])
            combine_pe(name, at)
            pe.wait_ge(S["hidden"], i * (2 * FT) + (ex_tiles[name] + 2 * FT))
            for f in range(FT):
                ins = pe.transpose(PS[:, 6, f * P:(f + 1) * P], htk[:, f * P:(f + 1) * P], ident)
            ins.then_inc(S["pair_turned_" + name], 1)
            pe.wait_ge(S["pickw_" + name], at * 2)
            for tt in range(2):
                ins = pe.transpose(PS[:, 7, tt * P:(tt + 1) * P], pickW[:, tt, :], ident)
            ins.then_inc(S["turned_" + name], 1)
            pe.wait_ge(S["xs_" + name], at + 1)
            pe.wait_ge(S["hid_" + name], at)
            for m in range(2):
                arrived(U[name] + 3 * m + 2, i)
            for f in range(FT):
                for j in range(2):
                    for m in range(2):
                        ins = pe.matmul(PS[pair[m], 4 + j, :], hid[:, f, pair[m]],
                                        unit(U[name] + 3 * m + 2, FT, D)[:, f, j * 512:(j + 1) * 512], start=f == 0,
                                        stop=f == FT - 1)
                        if f == FT - 1 and j == 1:
                            ins.then_inc(S["weights_used"], 1)
        combine_pe(name, COUNT[name] // 2 + 1)
        close_sums()

    def ex_pairs_act(name):
        FT = sum(SPLIT[name])
        tokens_act(name, 1)
        with act.Fori(0, COUNT[name] // 2) as i:
            act.wait_ge(S["pair_" + name], i * 2 + 1)
            for t in range(2 * FT):
                at = slice(t * C, (t + 1) * C)
                act.activation(sil_pair[:, at], PS[:, 6, at], ACT.Silu).then_inc(S["silu"], 1)
            tokens_act(name, i + 2)
            act.wait_ge(S["pair_turned_" + name], i + 1)
            act.activation(hid[:, 0:FT, 0:P], PS[:, 6, :].rearrange("p (f s) -> p f s", s=P), ACT.Copy)\
               .then_inc(S["hid_" + name], 1)

    def ex_pairs_dve(name):
        FT = sum(SPLIT[name])
        first_pick_dve(name)
        with dve.Fori(0, COUNT[name] // 2) as i:
            pick_dve(name, i + 1, i * 2)
            dve.wait_ge(S["pair_" + name], i * 2 + 2)
            for t in range(2 * FT):
                at = slice(t * C, (t + 1) * C)
                dve.wait_ge(S["silu"], i * (2 * FT) + (ex_tiles[name] + t + 1))
                dve.tensor_tensor(htk[:, at], sil_pair[:, at], PS[:, 7, at], ALU.mult).then_inc(S["hidden"], 1)
            outputs_dve(name, i + 1, i * 2 + (downs_before[name] + 2))

    def ex_slots_pe(name):
        FT, per, cap, PG = sum(SPLIT[name]), ex_units(name), CAP[name], PER[name]
        rounds = 2 * len(per) // SLOTS
        n_down, turn_groups = len(SPLIT[name]), 2 // PG

        with_tokens_pe(name)
        with pe.Fori(0, COUNT[name] // 2) as i:
            for gi in range(turn_groups):
                at = i * turn_groups + (gi + 1)
                base = ex_tiles[name] + gi * FT
                turn_u = U[name] + gi * len(per)
                pe.wait_ge(S["xs_" + name], at)
                pe.wait_ge(S["spread_" + name], at)
                for t, (m, f, u, tu, n) in enumerate(group_tiles(name)):
                    arrived(turn_u + u, i * rounds)
                    arrived(turn_u + u + 1, i * rounds)
                    if t >= 2:
                        pe.wait_ge(S["hidden"], i * (2 * FT) + (base + t - 1))
                    for j in range(2):
                        w = unit(turn_u + u + j, KT, n * P)
                        ins = product(PS[:, 6 + t % 2, j * P:(j + 1) * P],
                                      [(w[:, k, tu * P:(tu + 1) * P], xs[:, k, :]) for k in range(KT)])
                    ins.then_inc(S["gate_up"], 1)
                pe.wait_ge(S["ys_" + name], at)
                gather_pe(name, at + 1)
                combine_pe(name, at)
                pe.wait_ge(S["hidden"], i * (2 * FT) + (base + PG * FT))
                pe.wait_ge(S["pickw_" + name], at * 2)
                for tt in range(2):
                    ins = pe.transpose(PS[:, 7, tt * P:(tt + 1) * P], pickW[:, tt, :], ident)
                ins.then_inc(S["turned_" + name], 1)
                pe.wait_ge(S["xs_" + name], at + 1)
                for m in range(PG):
                    u, f = turn_u + m * len(per) + 2 * n_down, 0
                    for n in SPLIT[name]:
                        arrived(u, i * rounds)
                        wd = unit(u, n, D)
                        for t in range(n):
                            for j in range(2):
                                ins = pe.matmul(PS[m * cap:(m + 1) * cap, 4 + j, :], hid[:, m * FT + f, 0:cap],
                                                wd[:, t, j * 512:(j + 1) * 512], start=f == 0, stop=f == FT - 1)
                            f += 1
                        ins.then_inc(S["weights_used"], 1)
                        u += 1
        combine_pe(name, COUNT[name] // PG + 1)
        close_sums()

    def ex_slots_act(name):
        FT, cap, PG = sum(SPLIT[name]), CAP[name], PER[name]
        turn_groups = 2 // PG

        tokens_act(name, 1)
        with act.Fori(0, COUNT[name] // 2) as i:
            for gi in range(turn_groups):
                for t, (m, f, u, tu, n) in enumerate(group_tiles(name)):
                    act.wait_ge(S["gate_up"], i * (2 * FT) + (ex_tiles[name] + gi * FT + t + 1))
                    act.activation(sil[:, t % 4, 0:cap], PS[:, 6 + t % 2, m * cap:(m + 1) * cap], ACT.Silu)\
                       .then_inc(S["silu"], 1)
                tokens_act(name, i * turn_groups + (gi + 2))

    def ex_slots_dve(name):
        FT, cap, PG = sum(SPLIT[name]), CAP[name], PER[name]
        turn_groups, n_down = 2 // PG, len(SPLIT[name])
        first_pick_dve(name)
        with dve.Fori(0, COUNT[name] // 2) as i:
            for gi in range(turn_groups):
                at = i * turn_groups + (gi + 1)
                e0 = i * 2 + gi
                pick_dve(name, at, e0)
                for t, (m, f, u, tu, n) in enumerate(group_tiles(name)):
                    dve.wait_ge(S["silu"], i * (2 * FT) + (ex_tiles[name] + gi * FT + t + 1))
                    dve.tensor_tensor(hid[:, t, 0:cap], sil[:, t % 4, 0:cap],
                                      PS[:, 6 + t % 2, P + m * cap:P + (m + 1) * cap], ALU.mult).then_inc(S["hidden"], 1)
                outputs_dve(name, at, i * (2 * n_down) + (downs_before[name] + (gi + 1) * PG * n_down))

    tokens_turned = {"moe1": 1, "moe2": 2}

    def fits(eng, name):
        eng.wait_ge(S["fits"], tokens_turned[name])
        return eng.value_load(fit[0:1, 0:1], min_val=0, max_val=1)

    def moe_pe(name):
        ok = fits(pe, name)
        with pe.If(ok == 1):
            (ex_pairs_pe if PER[name] == 2 else ex_slots_pe)(name)
        with pe.If(ok == 0):
            weight_rows_pe(name)
            ex_pe(name)

    def moe_act(name):
        ok = fits(act, name)
        with act.If(ok == 1):
            (ex_pairs_act if PER[name] == 2 else ex_slots_act)(name)
        with act.If(ok == 0):
            weight_rows_act(name)
            ex_act(name)

    def moe_dve(name):
        ok = fits(dve, name)
        with dve.If(ok == 1):
            (ex_pairs_dve if PER[name] == 2 else ex_slots_dve)(name)
        with dve.If(ok == 0):
            weight_rows_dve(name)
            ex_dve(name, True)

    def weight_rows_pe(name):
        for r in range(2 * COUNT[name] // 4):
            pe.wait_ge(S["diag_" + name], r + 1)
            if r >= 2:
                pe.wait_ge(S["rows_" + name], r - 1)
            pe.matmul(PS[:, 6 + r % 2, :], ones, diagw[:, r % 2].rearrange("p e t -> p (e t)"), start=True, stop=True)\
                .then_inc(S["rowsum_" + name], 1)
        pe.wait_ge(S["rows_" + name], 2 * COUNT[name] // 4)

    def weight_rows_act(name):
        for r in range(2 * COUNT[name] // 4):
            e4, tt = r // 2, r % 2
            act.wait_ge(S["rowsum_" + name], r + 1)
            act.activation(wbc[:, 4 * e4:4 * e4 + 4, tt * P:(tt + 1) * P],
                           PS[:, 6 + r % 2, :].rearrange("p (e t) -> p e t", t=P), ACT.Copy).then_inc(S["rows_" + name], 1)

    def weight_rows_dve(name):
        for r in range(2 * COUNT[name] // 4):
            e4, tt = r // 2, r % 2
            if r >= 2:
                dve.wait_ge(S["rowsum_" + name], r - 1)
            dve.tensor_tensor(diagw[:, r % 2], over(ident, 4), along(Wt[:, tt, 4 * e4:4 * e4 + 4], P), ALU.mult)\
                .then_inc(S["diag_" + name], 1)
        dve.wait_ge(S["rows_" + name], 2 * COUNT[name] // 4)

    def route_pe(w, cols_n, n_norm, name):
        n_exp = COUNT[name]
        normed(pe, n_norm)
        for tt in range(2):
            ins = product(PS[:, 4, tt * 64:tt * 64 + cols_n], [(hT[:, k, tt * P:(tt + 1) * P], w[:, k, :]) for k in range(KT)])
        ins.then_inc(S["logits"], 1)
        as_they_lie_pe()
        pe.wait_ge(S["chosen"], tokens_turned[name])
        before = const("before")
        m0, m1_ = Mt[:, 0, 0:n_exp], Mt[:, 1, 0:n_exp]
        product(PS[:, 5, 0:n_exp], [(before, m0)])
        product(PS[:, 5, 64:64 + n_exp], [(ones, m0), (before, m1_)])
        product(PS[:, 5, 128:128 + n_exp], [(ones, m0), (ones, m1_)]).then_inc(S["ranked"], 1)

    def rank_dve(name):
        n_exp = COUNT[name]
        dve.wait_ge(S["ranked"], tokens_turned[name])
        dv.link(dve.memset(rank, -1.0))
        ps = PS[:, 5, 0:128].rearrange("p (t n) -> p t n", t=2)[:, :, 0:n_exp]
        r, m = rank[:, :, 0:n_exp], Mt[:, :, 0:n_exp]
        dv.link(dve.scalar_tensor_tensor(out=r, in0=ps, scalar=1.0, in1=m, op0=ALU.add, op1=ALU.mult))
        dv.link(dve.tensor_scalar(r, r, -1.0, None, ALU.add))
        dv.link(dve.tensor_reduce(most, PS[:, 5, 128:128 + n_exp], AX.X, ALU.max))
        dve.tensor_scalar(fit, most, float(CAP[name]), None, ALU.is_le).then_inc(S["fits"], 1)

    def top2_dve(n, le, W8, M8, sp_, scale):
        v8, i8, i2, e1, w1, w2 = sp_
        iota = const("iota")[:, 0:8]
        for tt in range(2):
            dv.link(dve.max(v8[:, tt, :], le[:, tt, :]))
            dv.link(dve.max_index(i8[:, tt, :], v8[:, tt, :], le[:, tt, :]))
        dv.link(dve.tensor_copy(i2, i8[:, :, 0:2]))
        for tt in range(2):
            dv.link(dve.tensor_scalar(M8[:, tt, :], iota, i2[:, tt, 0:1], None, ALU.is_equal))
            dv.link(dve.scalar_tensor_tensor(out=M8[:, tt, :], in0=iota, scalar=i2[:, tt, 1:2], in1=M8[:, tt, :],
                                             op0=ALU.is_equal, op1=ALU.add))
        dve.tensor_tensor(e1, v8[:, :, 1], v8[:, :, 0], ALU.subtract).then_inc(S["router_diff"], 1)
        dve.wait_ge(S["router_exp"], n + 2)
        dv.link(dve.tensor_scalar(w2, e1, 1.0, None, ALU.add))
        dv.link(dve.reciprocal(w1, w2))
        if scale is not None:
            dv.link(dve.tensor_tensor(w1, w1, scale, ALU.mult))
        dv.link(dve.tensor_tensor(w2, e1, w1, ALU.mult))
        for tt in range(2):
            dv.link(dve.tensor_scalar(W8[:, tt, :], iota, i2[:, tt, 0:1], w1[:, tt:tt + 1], ALU.is_equal, ALU.mult))
            dv.link(dve.tensor_scalar(v8[:, tt, :], iota, i2[:, tt, 1:2], w2[:, tt:tt + 1], ALU.is_equal, ALU.mult))
        dv.link(dve.tensor_tensor(W8, W8, v8, ALU.add))

    def top2_act(n, e1):
        act.wait_ge(S["router_diff"], n + 2)
        act.activation(e1, e1, ACT.Exp).then_inc(S["router_exp"], 1)

    rt = Space(work, rt_pos, work_len)
    lg36 = rt.take(2, 36)
    gpad, gv8, le8, W8r, M8r = (rt.take(2, 8) for _ in range(5))
    gi8 = rt.take(2, 8).bitcast(U32)
    v8r, i8r, i2r = rt.take(2, 8), rt.take(2, 8).bitcast(U32), rt.take(2, 2)
    gidx, ge, gsum, ptop, e1r, w1r, w2r = rt.take(2), rt.take(2, 4), rt.take(2), rt.take(2), rt.take(2), rt.take(2), rt.take(2)
    goh, lsel = rt.take(2, 4), rt.take(2, 4, 8)
    Wt, Mt = rt.take(2, N_EXP1 + 2), rt.take(2, N_EXP1 + 2)
    rank = rt.take(2, N_EXP1 + 2)
    most, fit = rt.take(1), rt.take(1).bitcast(I32)
    top_tiles = (v8r, i8r, i2r, e1r, w1r, w2r)

    def route1_dve():
        dve.wait_ge(S["logits"], 1)
        dv.link(dve.tensor_tensor(lg36, PS[:, 4, 0:128].rearrange("p (t n) -> p t n", t=2)[:, :, 0:36], over(rt_bias, 2),
                                  ALU.add))
        dv.link(dve.memset(gpad, -3e38))
        dv.link(dve.tensor_copy(gpad[:, :, 0:4], lg36[:, :, 0:4]))
        for tt in range(2):
            dv.link(dve.max(gv8[:, tt, :], gpad[:, tt, :]))
            dv.link(dve.max_index(gi8[:, tt, :], gv8[:, tt, :], gpad[:, tt, :]))
        dv.link(dve.tensor_copy(gidx, gi8[:, :, 0]))
        dve.tensor_tensor(ge, lg36[:, :, 0:4], along(gv8[:, :, 0], 4), ALU.subtract).then_inc(S["router_diff"], 1)
        dve.wait_ge(S["router_exp"], 1)
        dv.link(dve.tensor_reduce(gsum, ge, AX.X, ALU.add))
        dv.link(dve.reciprocal(ptop, gsum))
        dv.link(dve.tensor_tensor(goh, over(const("iota")[:, 0:4], 2), along(gidx, 4), ALU.is_equal))
        dv.link(dve.tensor_tensor(lsel, lg36[:, :, 4:36].rearrange("p t (g e) -> p t g e", g=4), along(goh, 8), ALU.mult))
        dv.link(dve.tensor_reduce(le8, lsel.rearrange("p t g e -> p t e g"), AX.X, ALU.add))
        top2_dve(0, le8, W8r, M8r, top_tiles, ptop)
        dv.link(dve.memset(Wt, 0.0))
        for t, t8 in ((Wt, W8r), (Mt, M8r)):
            ins = dve.tensor_tensor(t[:, :, 0:N_EXP1].rearrange("p t (g e) -> p t g e", g=4), along(goh, 8), over(t8, 4, 2),
                                    ALU.mult)
        ins.then_inc(S["chosen"], 1)
        rank_dve("moe1")

    def route1_act():
        act.wait_ge(S["router_diff"], 1)
        act.activation(ge, ge, ACT.Exp).then_inc(S["router_exp"], 1)
        top2_act(0, e1r)
        as_they_lie_act("moe1")

    def route2_dve():
        dve.wait_ge(S["logits"], 2)
        dv.link(dve.memset(Wt, 0.0))
        dv.link(dve.tensor_copy(le8, PS[:, 4, 0:128].rearrange("p (t n) -> p t n", t=2)[:, :, 0:8]))
        top2_dve(1, le8, Wt[:, :, 0:N_EXP2], M8r, top_tiles, None)
        dve.tensor_copy(Mt[:, :, 0:N_EXP2], M8r).then_inc(S["chosen"], 1)
        rank_dve("moe2")

    def route2_act():
        top2_act(1, e1r)
        as_they_lie_act("moe2")

    mla = Space(work, ABOVE, work_len)
    qlat, kvlat = mla.take(4, N), mla.take(2, N)
    qn, kvn = mla.take(4, N), mla.take(2, N)
    kr = mla.take(N)
    cosF, sinF = mla.take(N), mla.take(N)
    pos = mla.take(N).bitcast(I32)
    qh, kf = mla.take(HM, N), mla.take(HM, N)
    vtk = mla.take(2, HM * VH)
    mx, nmx, esum, rsum = (mla.take(2, 2, 2) for _ in range(4))
    lat_free = work[:, ABOVE:ABOVE + 8 * 384].rearrange("p (a b m n) -> p a b m n", a=2, b=2, m=2)
    sS, pT = lat_free[:, 0], lat_free[:, 1]
    ang, turns, cang, wrap = (kf[:, j, :] for j in range(4))
    oT = hT
    RP = slice(64, 64 + ROPE)
    QKSCALE = QK ** -0.5
    MLA_IN = Q_LORA + KV_LORA + ROPE

    def mla_sp():
        u = U["mla"]
        load(u, ktiles(A["mla_w_in_2"][0], 0, 512))
        load(u + 1, ktiles(A["mla_w_in_2"][0], 512, MLA_IN - 512))
        for j in range(2):
            load(u + 2 + j, ktiles(A["mla_w_qb_2"][0], 768 * j, 768))
        load(u + 4, ktiles(A["mla_w_kvb_2"][0], 0, 2048))

    def mla_pe():
        normed(pe, 5)
        u = U["mla"]
        w0, w1 = unit(u, KT, 512), unit(u + 1, KT, MLA_IN - 512)
        arrived(u)
        for i in range(7):
            if i == 4:
                arrived(u + 1)
            w, c0 = (w0, i * P) if i < 4 else (w1, (i - 4) * P)
            rows_, m = (slice(0, P), P) if i < 6 else (RP, ROPE)
            product(tile_begin("mla", i)[rows_, 0:N], [(w[:, k, c0:c0 + m], hT[:, k, :]) for k in range(KT)])\
                .then_inc(S["tile_full"], 1)
        norm_pe(6)
        norm_pe(7)
        rot = const("rot")[RP, RP]
        o = tile_begin("mla", 7)
        pe.wait_ge(S["emptied_act"], tile_owner[first_tile["mla"] + 6][1])
        product(o[RP, 0:N], [(rot, kr[RP, :])]).then_inc(S["tile_full"], 1)
        for h in range(HM):
            if h % 8 == 0:
                arrived(u + 2 + h // 8)
            w = unit(u + 2 + h // 8, 4, 768)
            normed(pe, 6)
            c0 = (h % 8) * QK
            product(tile_begin("q", h)[0:QK, 0:N], [(w[:, k, c0:c0 + QK], qn[:, k, :]) for k in range(4)])\
                .then_inc(S["tile_full"], 1)
        for h in range(HM):
            o = tile_begin("rot", h)
            pe.wait_ge(S["emptied_act"], tile_owner[first_tile["q"] + h][1])
            product(o[RP, 0:N], [(rot, qh[RP, h, :])]).then_inc(S["tile_full"], 1)
        arrived(u + 4)
        normed(pe, 7)
        w = unit(u + 4, 2, 2048)
        for h in range(HM):
            product(tile_begin("kv", h)[0:64, 0:N], [(w[:, k, h * P:h * P + 64], kvn[:, k, :]) for k in range(2)])\
                .then_inc(S["tile_full"], 1)
        for j in range(4):
            tt, half_ = j // 2, j % 2
            wv = w.rearrange("p k (h c) -> p k h c", c=P)[:, :, half_ * 8:half_ * 8 + 8, 64:P]
            product(tile_begin("kv", HM + j), [(kvn[:, k, tt * P:(tt + 1) * P], wv[:, k]) for k in range(2)])\
                .then_inc(S["tile_full"], 1)
        all_emptied(pe, "kv")
        pe.wait_ge(S["rope_done"], 1)
        at_scores_pe(0)
        at_scores_pe(1)
        for i in range(HP + 1):
            if i < HP:
                at_turn_pe(i)
            if i + 2 < HP:
                at_scores_pe(i + 2)
            if i >= 1:
                at_out_pe(i - 1)

    HP = HM // 2
    PARTS = ((0, P, 0), (P, 3 * P, 1))

    def at_scores_pe(g):
        if g >= 2:
            pe.wait_ge(S["at_masked"], g - 1)
        for m in range(2):
            for c0, c1, qt in PARTS:
                h = 2 * g + m
                ins = pe.matmul(PS[:, 2 * (g % 2) + m, c0:c1], qh[0:QK, h, qt * P:(qt + 1) * P], kf[0:QK, h, 0:c1 - c0],
                                start=True, stop=True)
        ins.then_inc(S["at_scores"], 1)

    def at_turn_pe(g):
        pe.wait_ge(S["at_weights"], g + 1)
        if g >= 1:
            pe.wait_ge(S["at_turn_evac"], g)
        for m in range(2):
            for j in range(3):
                ins = pe.transpose(PS[:, 4 + m, j * P:(j + 1) * P], sS[:, g % 2, m, j * P:(j + 1) * P], ident)
        ins.then_inc(S["at_turned"], 1)

    def at_out_pe(g):
        pe.wait_ge(S["at_turn_evac"], g + 1)
        if g >= 2:
            pe.wait_ge(S["at_oe"], g - 1)
        for j, (c0, p0, p1) in enumerate(((0, 0, 2 * P), (P, 2 * P, 3 * P))):
            for m in range(2):
                h = 2 * g + m
                ins = pe.matmul(PS[half(h), 6 + g % 2, c0:N], vtk[:, j, h * VH:(h + 1) * VH], pT[:, g % 2, m, p0:p1],
                                start=j == 0, stop=j == 1, skip_group_check=True)
        ins.then_inc(S["at_out"], 1)

    def mla_act():
        act.dma_start(pos[RP, :], A["positions_2"].broadcast_to([ROPE, N])).then_inc(S["positions"], 16)

        def evac(name, i, dst, src):
            act.activation(dst, src, ACT.Copy).then_inc(S["emptied_act"], 1)

        for i in range(7):
            o = tile_full(act, "mla", i)
            if i < 6:
                evac("mla", i, qlat[:, i, :] if i < 4 else kvlat[:, i - 4, :], o[:, 0:N])
            else:
                evac("mla", i, kr[RP, :], o[RP, 0:N])
        act.wait_ge(S["rope_args"], 1)
        act.activation(cosF[RP, :], cang[RP, :], ACT.Sin)
        act.activation(sinF[RP, :], ang[RP, :], ACT.Sin).then_inc(S["rope_tables"], 1)
        norm_act(6)
        norm_act(7)
        for h in range(HM):
            evac("q", h, qh[0:QK, h, :], tile_full(act, "q", h)[0:QK, 0:N])
        for h in range(HM):
            evac("kv", h, kf[0:64, h, :], tile_full(act, "kv", h)[0:64, 0:N])
        for j in range(4):
            evac("kv", HM + j, vtk[:, j // 2, (j % 2) * 512:(j % 2) * 512 + 512], tile_full(act, "kv", HM + j))
        for i in range(HP + 2):
            if i < HP:
                g = i
                act.wait_ge(S["at_max"], g + 1)
                for m in range(2):
                    for c0, c1, qt in PARTS:
                        s = sS[:, g % 2, m, c0:c1]
                        ins = act.activation(s, s, ACT.Exp, scale=QKSCALE, bias=nmx[:, g % 2, qt, m:m + 1],
                                             accum_out=esum[:, g % 2, qt, m:m + 1])
                ins.then_inc(S["at_exp"], 1)
            if 1 <= i <= HP:
                g = i - 1
                act.wait_ge(S["at_turned"], g + 1)
                if g >= 2:
                    act.wait_ge(S["at_out"], g - 1)
                act.activation(pT[:, g % 2], PS[:, 4:6, 0:384], ACT.Copy).then_inc(S["at_turn_evac"], 1)
            if i >= 2:
                g = i - 2
                act.wait_ge(S["at_out"], g + 1)
                act.activation(oT[:, g, :], PS[:, 6 + g % 2, 0:N], ACT.Copy).then_inc(S["at_oe"], 1)

    def mla_dve():
        dve.wait_ge(S["positions"], 16)
        two_pi = 2 * math.pi
        c1, c2 = 6.28125, float(np.float32(0.0019340515136718750))
        c3 = two_pi - c1 - c2
        magic = 1.5 * 2 ** 23
        pi_in = 3.1415925
        a, tn, ca, wr = ang[RP, :], turns[RP, :], cang[RP, :], wrap[RP, :]
        dv.link(dve.tensor_copy(a, pos[RP, :]))
        dv.link(dve.tensor_scalar(a, a, const("invfreq")[RP, :], None, ALU.mult))
        dv.link(dve.tensor_scalar(tn, a, 1.0 / two_pi, magic, ALU.mult, ALU.add))
        dv.link(dve.tensor_scalar(tn, tn, magic, None, ALU.subtract))
        for c in (c1, c2, c3):
            dv.link(dve.scalar_tensor_tensor(out=a, in0=tn, scalar=-c, in1=a, op0=ALU.mult, op1=ALU.add))
        dv.link(dve.tensor_scalar(ca, a, math.pi / 2, None, ALU.add))
        dv.link(dve.tensor_scalar(wr, ca, math.pi, -two_pi, ALU.is_gt, ALU.mult))
        dv.link(dve.tensor_tensor(ca, ca, wr, ALU.add))
        dv.link(dve.tensor_scalar(ca, ca, pi_in, -pi_in, ALU.min, ALU.max))
        dve.tensor_scalar(a, a, pi_in, -pi_in, ALU.min, ALU.max).then_inc(S["rope_args"], 1)
        dve.wait_ge(S["emptied_act"], tile_owner[first_tile["mla"] + 3][1])
        norm_dve(6)
        dve.wait_ge(S["emptied_act"], tile_owner[first_tile["mla"] + 5][1])
        norm_dve(7)
        dve.wait_ge(S["rope_tables"], 1)
        o = tile_full(dve, "mla", 7)
        dve.wait_ge(S["emptied_act"], tile_owner[first_tile["mla"] + 6][1])
        dv.link(dve.tensor_tensor(tmp[RP, 0, :], kr[RP, :], cosF[RP, :], ALU.mult))
        dve.tensor_tensor(tmp[RP, 1, :], o[RP, 0:N], sinF[RP, :], ALU.mult).then_inc(S["emptied_dve"], 1)
        dve.wait_ge(S["emptied_dve"], tile_owner[first_tile["mla"] + 7][1])
        dv.link(dve.tensor_tensor(kf[RP, :, :], over(tmp[RP, 0, :], HM), over(tmp[RP, 1, :], HM), ALU.add))
        turned = [xc, sq]
        for h in range(HM):
            o = tile_full(dve, "rot", h)
            dve.tensor_tensor(turned[h // 8][RP, h % 8, :], o[RP, 0:N], sinF[RP, :], ALU.mult).then_inc(S["emptied_dve"], 1)
        dve.wait_ge(S["emptied_dve"], tile_owner[first_tile["rot"] + HM - 1][1])
        dve.wait_ge(S["emptied_act"], tile_owner[first_tile["q"] + HM - 1][1])
        dv.link(dve.tensor_tensor(qh[RP, :, :], qh[RP, :, :], over(cosF[RP, :], HM), ALU.mult))
        for j in range(2):
            q8 = qh[RP, 8 * j:8 * j + 8, :]
            ins = dve.tensor_tensor(q8, q8, turned[j][RP, :, :], ALU.add)
            if j == 0:
                dv.link(ins)
        ins.then_inc(S["rope_done"], 1)
        for i in range(HP + 1):
            if i < HP:
                g = i
                dve.wait_ge(S["at_scores"], g + 1)
                if g >= 2:
                    dve.wait_ge(S["at_turned"], g - 1)
                s, b = sS[:, g % 2], 2 * (g % 2)
                dve.tensor_tensor(s, PS[:, b:b + 2, 0:384], over(const("causal"), 2), ALU.add).then_inc(S["at_masked"], 1)
                dve.wait_ge(S["at_masked"], g + 1)
                for c0, c1, qt in PARTS:
                    ins = dve.tensor_reduce(mx[:, g % 2, qt, :], s[:, :, c0:c1], AX.X, ALU.max)
                dv.link(ins)
                dve.tensor_scalar(nmx[:, g % 2], mx[:, g % 2], -QKSCALE, None, ALU.mult).then_inc(S["at_max"], 1)
            if i >= 1:
                g = i - 1
                dve.wait_ge(S["at_exp"], g + 1)
                dv.link(dve.reciprocal(rsum[:, g % 2], esum[:, g % 2]))
                for c0, c1, qt in PARTS:
                    s = sS[:, g % 2, :, c0:c1]
                    ins = dve.tensor_tensor(s, s, along(rsum[:, g % 2, qt, :], c1 - c0), ALU.mult)
                ins.then_inc(S["at_weights"], 1)

    gd = Space(work, ABOVE, work_len)
    qkv = gd.take(3 * H, N)
    gq, gk, gv = (qkv[:, j * H:(j + 1) * H, :] for j in range(3))
    zs = gd.take(H, N)
    Sg = gd.take(H, P)
    CTg = gd.take(H, P)
    decU = CTg.rearrange("p h t -> p (h t)")[:, 0:H * C].rearrange("p (h t) -> p h t", t=C)
    Ug, ksg = gd.take(H, P), gd.take(H, P)
    beta, nbeta, ga, gz, gl_, gc = (gd.take(N) for _ in range(6))
    glast, eglast, expA = gd.take(4), gd.take(4), gd.take(1)
    egc, wsr = ga, gz
    gdiag, eglb = gd.take(4, H), gd.take(4, H)
    gtk = gd.take(4, 2, H)
    oms, ostd = gd.take(H), gd.take(H)

    def halves(buf):
        a = buf.rearrange("p k n -> p (k n)")
        return a[:, 0:1024], a[:, 1024:2048]

    (XTg, Xg), (Yg, attn), (NTg, og) = halves(xc), halves(sq), halves(hT)
    XTg, Xg, Yg, NTg, og = (t.rearrange("p (h e) -> p h e", h=H) for t in (XTg, Xg, Yg, NTg, og))
    attn = attn[:, 0:H * C].rearrange("p (h t) -> p h t", t=C)
    osq = Yg
    weighted = Yg[:, 0:4, :].rearrange("p a (b t) -> p (a b) t", t=C)
    g8 = slice(0, H)

    def rows2(c):
        return slice(C * (c % 2), C * (c % 2) + C)

    def heads2(bank, parts):
        return PS[parts, bank:bank + 2, :].rearrange("p b (h e) -> p (b h) e", e=P)

    def heads1(bank):
        return PS[:, bank, :].rearrange("p (h t) -> p h t", t=C)

    def gdn_sp():
        for j in range(8):
            load(U["gdn_in"] + j, ktiles(A["gdn_w_in_2"][0], 512 * j, 512))

    def gdn_pe():
        normed(pe, 9)
        o = tile_begin("gdn_ba", 0)
        for j in range(2):
            ins = product(o[g8, j * N:(j + 1) * N], [(w_ba[:, k, j * H:(j + 1) * H], hT[:, k, :]) for k in range(KT)])
        ins.then_inc(S["tile_full"], 1)

        def project(name, i, j):
            if j % 4 == 0:
                arrived(U["gdn_in"] + j // 4)
            w = unit(U["gdn_in"] + j // 4, KT, 512)
            product(tile_begin(name, i)[:, 0:N], [(w[:, k, (j % 4) * P:(j % 4 + 1) * P], hT[:, k, :]) for k in range(KT)])\
                .then_inc(S["tile_full"], 1)

        def norms(name, src, n):
            pe.wait_ge(S["gd_sq"], n)
            for j in range(4):
                product(tile_begin(name, j), [(ones, src[:, 2 * j:2 * j + 2, :])]).then_inc(S["tile_full"], 1)

        for i in range(16):
            project("gdn_qk", i, i)
        norms("gdn_l2q", sq, 1)
        for i in range(8):
            project("gdn_v", i, 16 + i)
        norms("gdn_l2k", xc, 2)
        for i in range(8):
            project("gdn_z", i, 24 + i)
        pe.wait_ge(S["gd_rows"], 1)
        for j, t in enumerate((beta, egc, wsr, gc)):
            for cp in range(2):
                pe.transpose(PS[:, 0, (j * 2 + cp) * H:(j * 2 + cp + 1) * H], t[g8, cp * P:(cp + 1) * P], ident[g8, g8])
        pe.matmul(PS[:, 1, 0:4 * H], ones[g8, :], gdiag[g8].rearrange("p c h -> p (c h)"), start=True, stop=True)\
            .then_inc(S["gd_tok"], 1)
        all_emptied(pe, "gdn_z")
        pe.wait_ge(S["gd_ready"], 1)
        for c in range(4):
            if c == 0:
                gd_scores_pe(0, range(H))
            if c % 2 == 0:
                inverse_pe(NCH + c // 2, CTg, Xg, XTg, Yg)
            gd_chunk_pe(c)

    def gd_scores_pe(cp, heads):
        for h in heads:
            at = slice(h * C, (h + 1) * C)
            pick = const("pick", H)[:, at]
            for c in (2 * cp, 2 * cp + 1):
                r, t = rows2(c), slice(c * C, (c + 1) * C)
                pe.matmul(PS[r, 0, at], gk[:, h, t], gk[:, h, t], start=True, stop=True)
                pe.matmul(PS[r, 1, at], gk[:, h, t], gq[:, h, t], start=True, stop=True)
                pe.matmul(PS[r, 2, at], pick, gc[g8, t], start=True, stop=True)
                ins = pe.matmul(PS[r, 3, at], pick, nbeta[g8, t], start=True, stop=True)
        if H - 1 in heads:
            ins.then_inc(S["gd_sc"], 1)

    gd_banks = [(h // 4, slice((h % 4) * P, (h % 4 + 1) * P)) for h in range(H)]

    def gd_tokens_pe(c):
        r, t = rows2(c), slice(c * C, (c + 1) * C)
        for h, (b, at) in enumerate(gd_banks):
            pe.matmul(PS[r, b, at], gv[:, h, t], ident, start=True, stop=True)
            pe.matmul(PS[r, 2 + b, at], gk[:, h, t], ident, start=True, stop=True)
            pe.matmul(PS[r, 4 + b, at], gk[:, h, t], Sg[:, h, :], start=True, stop=True)

    def gd_chunk_pe(c):
        r, t = rows2(c), slice(c * C, (c + 1) * C)
        banks = gd_banks
        if c % 2 == 0:
            gd_tokens_pe(c)
        if c:
            pe.wait_ge(S["gd_mix"], c)
        for h, (b, at) in enumerate(banks):
            ins = pe.matmul(PS[r, 6 + b, at], gq[:, h, t], Sg[:, h, :], start=True, stop=True)
        ins.then_inc(S["gd_ks"], 1)
        pe.wait_ge(S["gd_rhs"], c + 1)
        for h, (b, at) in enumerate(banks):
            ins = pe.matmul(PS[r, b, at], XTg[:, h, r], Ug[:, h, :], start=True, stop=True)
        ins.then_inc(S["gd_u"], 1)
        pe.wait_ge(S["gd_ue"], c + 1)
        pe.wait_ge(S["gd_inter"], c + 1)
        for h, (b, at) in enumerate(banks):
            ins = pe.matmul(PS[r, 2 + b, at], attn[r, h, :], Ug[r, h, :], start=True, stop=True)
            if c < 3:
                ins = pe.matmul(PS[:, 4 + b, at], ksg[r, h, :], Ug[r, h, :], start=True, stop=True)
        ins.then_inc(S["gd_y"], 1)
        if c < 3:
            pe.wait_ge(S["gd_step"], c + 1)
            if c % 2 == 0:
                gd_tokens_pe(c + 1)
            else:
                gd_scores_pe(c // 2 + 1, range(H // 2))
        pe.wait_ge(S["gd_o"], c + 1)
        for h in range(H):
            ins = pe.transpose(PS[:, 6, h * C:(h + 1) * C], og[r, h, :], ident[r, r])
        ins.then_inc(S["gd_ot"], 1)
        if c == 1:
            gd_scores_pe(1, range(H // 2, H))

    def gdn_act():
        def evac(name, i, dst, src, func, **kw):
            act.activation(dst, src, func, **kw).then_inc(S["emptied_act"], 1)

        o = tile_full(act, "gdn_ba", 0)
        act.activation(beta[g8, :], o[g8, 0:N], ACT.Sigmoid)
        act.activation(expA[g8, :], gdn_bias[:, 0:1], ACT.Exp)
        evac("gdn_ba", 0, ga[g8, :], o[g8, N:2 * N], ACT.Identity, bias=gdn_bias[:, 1:2])
        act.wait_ge(S["gd_abs"], 1)
        ac.link(act.activation(gl_[g8, :], gz[g8, :], ACT.Exp, scale=-1.0))
        act.activation(gl_[g8, :], gl_[g8, :], ACT.Ln, bias=1.0).then_inc(S["gd_l"], 1)
        act.wait_ge(S["gd_args"], 1)
        act.activation(wsr[g8, :], wsr[g8, :], ACT.Exp)
        act.activation(egc[g8, :], gc[g8, :], ACT.Exp)
        act.activation(eglast[g8, :], glast[g8, :], ACT.Exp).then_inc(S["gd_gexp"], 1)

        def silu(t, name, last):
            act.wait_ge(S["emptied_dve"], tile_owner[first_tile[name] + last][1])
            act.activation(t, t, ACT.Silu).then_inc(S["gd_silu"], 1)

        def rsqrt(name, buf, bias):
            for j in range(4):
                evac(name, j, buf[:, 2 * j:2 * j + 2, :], tile_full(act, name, j).rearrange("p (h t) -> p h t", h=2), ACT.Ln,
                     bias=EPS)
            act.wait_ge(S["emptied_act"], tile_owner[first_tile[name] + 3][1])
            act.activation(buf, buf, ACT.Exp, scale=-0.5, bias=bias).then_inc(S["gd_rs"], 1)

        silu(gq, "gdn_qk", 7)
        silu(gk, "gdn_qk", 15)
        rsqrt("gdn_l2q", sq, -0.5 * math.log(P))
        silu(gv, "gdn_v", 7)
        rsqrt("gdn_l2k", xc, 0.0)
        for h in range(H):
            evac("gdn_z", h, zs[:, h, :], tile_full(act, "gdn_z", h)[:, 0:N], ACT.Silu)
        for c in range(4):
            if c % 2 == 0:
                act.wait_ge(S["gd_e"], c // 2 + 1)
                act.activation(decU, decU, ACT.Exp).then_inc(S["gd_exp"], 1)
                inverse_act(NCH + c // 2, Yg)
            act.wait_ge(S["gd_u"], c + 1)
            r = rows2(c)
            act.activation(Ug[r], heads2(0, r), ACT.Copy).then_inc(S["gd_ue"], 1)
            act.wait_ge(S["gd_var"], c + 1)
            act.activation(ostd[r, :], oms[r, :], ACT.Sqrt).then_inc(S["gd_std"], 1)

    def conv4_dve(name, i, j):
        o = tile_full(dve, name, i)
        y = qkv[:, j, :]
        dv.link(dve.tensor_scalar(y, o[:, 0:N], col("gdn_conv_w_2", 3 * 24 + j), None, ALU.mult))
        for back in (1, 2, 3):
            ins = dve.scalar_tensor_tensor(out=y[:, back:], in0=o[:, 0:N - back],
                                           scalar=col("gdn_conv_w_2", (3 - back) * 24 + j), in1=y[:, back:],
                                           op0=ALU.mult, op1=ALU.add)
            if back < 3:
                dv.link(ins)
        ins.then_inc(S["emptied_dve"], 1)

    def gd_square_dve(j):
        t, s = ((gq, sq), (gk, xc))[j]
        dve.wait_ge(S["gd_silu"], j + 1)
        dve.tensor_tensor(s, t, t, ALU.mult).then_inc(S["gd_sq"], 1)

    def gd_gates_dve():
        dve.wait_ge(S["emptied_act"], tile_owner[first_tile["gdn_ba"]][1])
        dve.scalar_tensor_tensor(out=gz[g8, :], in0=ga[g8, :], scalar=-1.0, in1=ga[g8, :], op0=ALU.mult, op1=ALU.max)\
           .then_inc(S["gd_abs"], 1)
        dve.wait_ge(S["gd_l"], 1)
        dv.link(dve.scalar_tensor_tensor(out=ga[g8, :], in0=ga[g8, :], scalar=0.0, in1=gl_[g8, :], op0=ALU.max, op1=ALU.add))
        dv.link(dve.tensor_scalar(ga[g8, :], ga[g8, :], expA[g8, :], -1.0, ALU.mult, ALU.mult))
        dv.link(dve.tensor_tensor_scan(gc[g8, :], const("resetf")[g8, 0:N], ga[g8, :], 0.0, ALU.mult, ALU.add))
        dv.link(dve.tensor_copy(glast[g8, :], gc[g8, C - 1::C]))
        dv.link(dve.tensor_scalar(nbeta[g8, :], beta[g8, :], -1.0, None, ALU.mult))
        ch = lambda t: t[g8, :].rearrange("p (c t) -> p c t", t=C)
        dve.tensor_tensor(ch(wsr), along(glast[g8, :], C), ch(gc), ALU.subtract).then_inc(S["gd_args"], 1)
        dve.wait_ge(S["gd_gexp"], 1)
        dve.tensor_tensor(gdiag[g8], over(ident[g8, g8], 4), along(eglast[g8, :], H), ALU.mult).then_inc(S["gd_rows"], 1)

    def gdn_dve():
        gd_gates_dve()
        for i in range(16):
            conv4_dve("gdn_qk", i, i)
            if i == 10:
                gd_square_dve(0)
        gd_square_dve(1)
        for i in range(8):
            conv4_dve("gdn_v", i, 16 + i)
        dv.link(dve.memset(Sg, 0.0))
        dv.link(dve.memset(Ug, 0.0))
        for j, (t, s) in enumerate(((gq, sq), (gk, xc))):
            dve.wait_ge(S["gd_rs"], j + 1)
            dv.link(dve.tensor_tensor(t, t, s, ALU.mult))
        dve.wait_ge(S["gd_tok"], 1)
        dv.link(dve.tensor_copy(gtk, PS[:, 0, 0:8 * H].rearrange("p (j c h) -> p j c h", j=4, h=H)))
        dv.link(dve.tensor_copy(eglb, PS[:, 1, 0:4 * H].rearrange("p (c h) -> p c h", h=H)))
        dve.wait_ge(S["tile_full"], first_tile["gdn_z"] + 8)
        dve.memset(NTg, 0.0).then_inc(S["gd_ready"], 1)
        dve.wait_ge(S["gd_ready"], 1)
        for c in range(4):
            if c % 2 == 0:
                gd_pair_dve(c // 2)
            gd_chunk_dve(c)

    def gd_pair_dve(cp):
        dve.wait_ge(S["gd_sc"], cp + 1)
        dv.link(dve.tensor_tensor(decU, heads1(2), along(gtk[:, 3, cp, :], C), ALU.subtract))
        dve.tensor_tensor(decU, decU, over(const("madd")[:, 0:C], H), ALU.add).then_inc(S["gd_e"], 1)
        dve.wait_ge(S["gd_exp"], cp + 1)
        dve.tensor_tensor(attn, heads1(1), decU, ALU.mult)
        dv.link(dve.tensor_tensor(weighted, heads1(0), decU, ALU.mult))
        for c in range(2):
            r = rows2(c)
            ins = dve.tensor_tensor(NTg[r, :, r], weighted[r], heads1(3)[r], ALU.mult)
        dv.link(ins)
        inverse_dve(NCH + cp, NTg, lambda lev, g: over(over(const("level")[:, lev * P:lev * P + C], 2), 4), CTg, Xg, XTg)

    def gd_chunk_dve(c):
        r = rows2(c)
        per_token = lambda j: along(gtk[r, j, c // 2, :], P)
        dve.wait_ge(S["gd_ks"], c + 1)
        u, o = Ug[r], og[r]
        dv.link(dve.tensor_tensor(u, heads2(4, r), per_token(1), ALU.mult))
        dv.link(dve.tensor_tensor(u, heads2(0, r), u, ALU.subtract))
        dve.tensor_tensor(u, u, per_token(0), ALU.mult).then_inc(S["gd_rhs"], 1)
        dve.tensor_tensor(ksg[r], heads2(2, r), per_token(2), ALU.mult)
        dve.tensor_tensor(o, heads2(6, r), per_token(1), ALU.mult).then_inc(S["gd_inter"], 1)
        dve.wait_ge(S["gd_y"], c + 1)
        if c < 3:
            dv.link(dve.tensor_tensor(Sg, Sg, along(eglb[:, c, :], P), ALU.mult))
            dve.tensor_tensor(Sg, Sg, heads2(4, slice(0, P)), ALU.add)
        dve.wait_ge(S["gd_inter"], c + 1)
        dve.tensor_tensor(o, o, heads2(2, r), ALU.add).then_inc(S["gd_step"], 1)
        dve.wait_ge(S["gd_step"], c + 1)
        dv.link(dve.tensor_tensor(osq[r], o, o, ALU.mult))
        dv.link(dve.tensor_reduce(oms[r, :], osq[r], AX.X, ALU.add))
        dve.tensor_scalar(oms[r, :], oms[r, :], 1.0 / P, EPS, ALU.mult, ALU.add).then_inc(S["gd_var"], 1)
        dve.wait_ge(S["gd_std"], c + 1)
        dv.link(dve.reciprocal(oms[r, :], ostd[r, :]))
        dve.tensor_tensor(o, o, along(oms[r, :], P), ALU.mult).then_inc(S["gd_o"], 1)
        dve.wait_ge(S["gd_ot"], c + 1)
        z = zs[:, :, c * C:(c + 1) * C]
        dve.scalar_tensor_tensor(out=z, in0=PS[:, 6, :].rearrange("p (h t) -> p h t", t=C), scalar=col("gdn_out_norm_2"),
                                 in1=z, op0=ALU.mult, op1=ALU.mult).then_inc(S["gd_mix"], 1)

    result = work[:, ABOVE:ABOVE + 2 * D].rearrange("p (t d) -> p t d", t=2)

    def final_pe():
        normed(pe, 11)
        for tt in range(2):
            for k in range(KT):
                ins = pe.transpose(PS[:, 2 * tt + k // 4, (k % 4) * P:(k % 4 + 1) * P], hT[:, k, tt * P:(tt + 1) * P], ident)
            ins.then_inc(S["final_turned"], 1)

    def final_act():
        for tt in range(2):
            act.wait_ge(S["final_turned"], tt + 1)
            act.activation(result[:, tt, :], PS[:, 2 * tt:2 * tt + 2, :].rearrange("p b n -> p (b n)"), ACT.Copy)\
               .then_inc(S["result"], 1)

    def final_sp():
        for tt in range(2):
            sp.wait_ge(S["result"], tt + 1)
            sp.dma_start(out[0, tt * P:(tt + 1) * P, :], result[:, tt, :]).then_inc(S["stored"], 16)
        sp.wait_ge(S["stored"], 32)

    def of_mod1(t0, which=0):
        return lambda k: mod1[:, t0 + k, which:which + 1]

    def of_mod2(layer, t0):
        return lambda k: mod2[:, layer, t0 + k:t0 + k + 1]

    def of_gain2(j):
        return lambda k: gain2[:, j, k:k + 1]

    def of_col(name):
        return lambda k: col(name, k)

    NORMS = [
        (ctxT, KT, True, hall[:, :, 0:N], of_mod1(8, 1), of_mod1(0, 1), LN_EPS),
        (xT, KT, True, hall[:, :, N:2 * N], of_mod1(8), of_mod1(0), LN_EPS),
        (xT, KT, True, xT, of_col("ln1_g"), of_col("ln1_b"), LN_EPS),
        (xT, KT, True, hT, of_mod1(32), of_mod1(24), LN_EPS),
        (xT, KT, True, xT, of_col("ln2_g"), of_col("ln2_b"), LN_EPS),
        (xT, KT, False, hT, of_gain2(0), of_mod2(0, 0), EPS),
        (qlat, 4, False, qn, of_col("mla_q_norm_2"), None, EPS),
        (kvlat, 2, False, kvn, of_col("mla_kv_norm_2"), None, EPS),
        (xT, KT, False, hT, of_gain2(1), of_mod2(0, 24), EPS),
        (xT, KT, False, hT, of_gain2(2), of_mod2(1, 0), EPS),
        (xT, KT, False, hT, of_gain2(3), of_mod2(1, 24), EPS),
        (xT, KT, False, hT, of_col("final_norm_2"), None, EPS),
    ]

    EARLY = 6

    block = ctx.enter_context(nc.Block())

    @block.scalar
    def _(eng):
        stage0_act()
        cond_act()
        for n in range(N_ADA1):
            if n == EARLY:
                stage0_act2()
            ada1_act(n)
            if n % 2:
                ada2_act(N_ADA1 + n // 2)
        norm_act(0)
        norm_act(1)
        w_in_act()
        ml_gates_act()
        for i in range(NCH):
            ml_step_act(i)
        headnorm_act(0, hstat)
        rw_prep_act()
        for i in range(NCH):
            rw_step_act(i)
        headnorm_act(1, ystat)
        norm_act(2)
        norm_act(3)
        route1_act()
        moe_act("moe1")
        norm_act(4)
        norm_act(5)
        mla_act()
        norm_act(8)
        ex_act("ffn")
        norm_act(9)
        gdn_act()
        norm_act(10)
        route2_act()
        moe_act("moe2")
        norm_act(11)
        final_act()

    @block.sync
    def _(eng):
        first_sp()
        early_sp()
        sp.wait_ge(S["mixed"], 1)
        out_sp("w_out", A["w_out"][0])
        ex_sp("moe1")
        mla_sp()
        out_sp("mla_out", A["mla_w_out_2"][0])
        ex_sp("ffn")
        gdn_sp()
        out_sp("gdn_out", A["gdn_w_out_2"][0])
        ex_sp("moe2")
        final_sp()

    @block.gpsimd
    def _(eng):
        stage0_pool()
        for n in range(N_ADA1, N_ADA):
            ada2_pool(n)
        ml_pool()

    @block.tensor
    def _(eng):
        cond_pe()
        for n in range(EARLY):
            ada1_pe(n)
        stage0_pe()
        for n in range(EARLY, N_ADA1):
            ada1_pe(n)
        ada1_turn_pe(N_ADA1 - 1)
        norm_pe(0, lambda e: e.wait_ge(S["x_evac"], 4))
        norm_pe(1, lambda e: e.wait_ge(S["x_evac"], 4))
        w_in_pe()
        ml_gates_pe()
        for i in range(NCH):
            ml_step_pe(i)
        headnorm_pe(0, hs)
        rw_prep_pe()
        for i in range(NCH):
            rw_step_pe(i)
        headnorm_pe(1, yr)
        pe.wait_ge(S["mixed"], 1)
        out_pe("w_out", mixT)
        norm_pe(2, lambda e: all_emptied(e, "w_out"))
        norm_pe(3, lambda e: normed(e, 2))
        route_pe(w_rt1, 36, 3, "moe1")
        moe_pe("moe1")
        norm_pe(4, lambda e: e.wait_ge(S["resid"], 1))
        norm_pe(5)
        mla_pe()
        pe.wait_ge(S["at_oe"], HP)
        out_pe("mla_out", oT)
        norm_pe(8)
        normed(pe, 8)
        ex_pe("ffn")
        norm_pe(9)
        gdn_pe()
        pe.wait_ge(S["gd_mix"], 4)
        out_pe("gdn_out", zs)
        norm_pe(10)
        route_pe(w_rt2, N_EXP2, 10, "moe2")
        moe_pe("moe2")
        norm_pe(11)
        final_pe()

    @block.vector
    def _(eng):
        stage0_dve()
        ada1_dve()
        norm_dve(0)
        norm_dve(1)
        conv_dve()
        ada2_dve()
        all_emptied(dve, "w_in")
        ml_gates_dve()
        for i in range(NCH):
            ml_step_dve(i)
        headnorm_dve(0, hs, hsq, hstat, LN_EPS)
        ml_out_dve()
        rw_prep_dve()
        for i in range(NCH):
            rw_step_dve(i)
        headnorm_dve(1, yr, ysq, ystat, GN_EPS)
        rw_out_dve()

        out_dve("w_out", of_mod1(16), ALPHA)
        norm_dve(2)
        norm_dve(3)
        route1_dve()
        moe_dve("moe1")
        ex_resid_dve("moe1", of_mod1(40), ALPHA)
        dve.wait_ge(S["resid"], 1)
        norm_dve(4)
        norm_dve(5)
        mla_dve()
        out_dve("mla_out", of_mod2(0, 16), 1.0)
        norm_dve(8)
        ex_dve("ffn", False)
        ex_resid_dve("ffn", of_mod2(0, 40), 1.0)
        dve.wait_ge(S["resid"], 2)
        norm_dve(9)
        gdn_dve()
        out_dve("gdn_out", of_mod2(1, 16), 1.0)
        norm_dve(10)
        route2_dve()
        moe_dve("moe2")
        ex_resid_dve("moe2", of_mod2(1, 40), 1.0)
        dve.wait_ge(S["resid"], 3)
        norm_dve(11)

    return ctx


def kernel(**inputs):
    import concourse.bacc as bacc
    from concourse.bass_utils import run_bass_kernel_spmd

    nc = bacc.Bacc("TRN2", target_bir_lowering=False, num_devices=1, dynamic_dma_scratch_size=1024)
    consts, const_at = constants()
    arrays, drams = {}, {}
    for name, a in list(inputs.items()) + [("consts", consts)]:
        a = np.ascontiguousarray(a)
        arrays[f"in_{name}_dram"] = a
        drams[name] = nc.dram_tensor(f"in_{name}_dram", a.shape, mybir.dt.from_np(a.dtype), kind="ExternalInput").ap()
    out = nc.dram_tensor("out_0_dram", (1, N, D), F32, kind="ExternalOutput").ap()
    build(nc, drams, out, const_at).close()
    r = run_bass_kernel_spmd(nc, [arrays], core_ids=[0])
    return r.results[0]["out_0_dram"]
```
